# Optimizing a Trainium2 kernel written in Bass

```python
import math
import jax, jax.numpy as jnp
from jax import lax
import numpy as np

D_MODEL = 1024
BATCH = 1
SEQ = 512
DEPTH = 1

HEAD_DIM = 64
MIX_WIDTH = D_MODEL
A_HEADS = (MIX_WIDTH // 2) // HEAD_DIM
A_KV_HEADS = 2
A_GROUP = A_HEADS // A_KV_HEADS
B_HEADS = (MIX_WIDTH // 2) // HEAD_DIM
WINDOW = 128
BLOCK = 128
D_FF = 4 * D_MODEL
EPS = 1e-6

A_Q_W = A_HEADS * HEAD_DIM
A_KV_W = A_KV_HEADS * HEAD_DIM
B_W = B_HEADS * HEAD_DIM
IN_SPLITS = tuple(np.cumsum([A_Q_W, A_KV_W, A_KV_W, B_W, B_W, B_W]).tolist())
IN_WIDTH = A_Q_W + 2 * A_KV_W + 3 * B_W + B_HEADS


def rmsnorm(x, g):
    x32 = x.astype(jnp.float32)
    y = x32 * lax.rsqrt(jnp.mean(x32 * x32, axis=-1, keepdims=True) + EPS)
    return (y * g.astype(jnp.float32)).astype(x.dtype)

def alibi_slopes(n):
    return jnp.exp2(-(8.0 / n) * (jnp.arange(n, dtype=jnp.float32) + 1.0))

def swa_sinks_attention(q, k, v, sinks):
    b, s, _, d = q.shape
    nb = s // BLOCK
    scale = 1.0 / math.sqrt(d)
    qb = q.reshape(b, nb, BLOCK, A_KV_HEADS, A_GROUP, d)
    pad = ((0, 0), (BLOCK, 0), (0, 0), (0, 0))
    kp = jnp.pad(k, pad).reshape(b, nb + 1, BLOCK, A_KV_HEADS, d)
    vp = jnp.pad(v, pad).reshape(b, nb + 1, BLOCK, A_KV_HEADS, d)
    kb = jnp.concatenate([kp[:, :-1], kp[:, 1:]], axis=2)
    vb = jnp.concatenate([vp[:, :-1], vp[:, 1:]], axis=2)
    scores = jnp.einsum('bnqkgd,bnskd->bnkgqs', qb, kb).astype(jnp.float32) * scale
    qpos = BLOCK + jnp.arange(BLOCK)
    kpos = jnp.arange(2 * BLOCK)
    dist = qpos[:, None] - kpos[None, :]
    band = (dist >= 0) & (dist < WINDOW)
    first_pad = (jnp.arange(nb) == 0)[:, None, None] & (kpos < BLOCK)[None, None, :]
    valid = band[None] & ~first_pad
    slopes = alibi_slopes(A_HEADS).reshape(A_KV_HEADS, A_GROUP)
    alibi = -slopes[:, :, None, None] * dist.astype(jnp.float32)[None, None]
    scores = scores + alibi[None, None]
    scores = jnp.where(valid[None, :, None, None], scores, -jnp.inf)
    sink = sinks.astype(jnp.float32).reshape(1, 1, A_KV_HEADS, A_GROUP, 1, 1)
    m = jnp.maximum(jnp.max(scores, axis=-1, keepdims=True), sink)
    p = jnp.exp(scores - m)
    denom = jnp.sum(p, axis=-1, keepdims=True) + jnp.exp(sink - m)
    p = (p / denom).astype(v.dtype)
    out = jnp.einsum('bnkgqs,bnskd->bnqkgd', p, vb)
    return out.reshape(b, s, A_HEADS, d)

def forgetting_attention(q, k, v, log_f):
    b, s, h, d = q.shape
    nb = s // BLOCK
    scale = 1.0 / math.sqrt(d)
    c = jnp.cumsum(log_f, axis=1)
    c_keys = jnp.transpose(c, (0, 2, 1))
    qb = jnp.moveaxis(q.reshape(b, nb, BLOCK, h, d), 1, 0)
    cb = jnp.moveaxis(c.reshape(b, nb, BLOCK, h), 1, 0)
    kpos = jnp.arange(s)

    def block_step(args):
        qi, ci, i = args
        sc = jnp.einsum('bqhd,bshd->bhqs', qi, k).astype(jnp.float32) * scale
        bias = jnp.transpose(ci, (0, 2, 1))[..., None] - c_keys[:, :, None, :]
        qpos = i * BLOCK + jnp.arange(BLOCK)
        causal = kpos[None, :] <= qpos[:, None]
        sc = jnp.where(causal[None, None], sc + bias, -jnp.inf)
        p = jax.nn.softmax(sc, axis=-1).astype(v.dtype)
        return jnp.einsum('bhqs,bshd->bqhd', p, v)

    out = lax.map(block_step, (qb, cb, jnp.arange(nb)))
    return jnp.moveaxis(out, 0, 1).reshape(b, s, h, d)

def first_inputs(seed: int = 0) -> dict:
    key = jax.random.key(seed)
    ks = jax.random.split(key, 14)
    f32 = jnp.float32
    x = jax.random.normal(ks[0], (BATCH, SEQ, D_MODEL), f32)
    attn_norm_g = 1.0 + 0.02 * jax.random.normal(ks[1], (D_MODEL,), f32)
    w_in = jax.random.normal(ks[2], (D_MODEL, IN_WIDTH), f32) * D_MODEL ** -0.5
    b_forget = 2.0 + 0.5 * jax.random.normal(ks[3], (B_HEADS,), f32)
    q_norm_a = 1.0 + 0.02 * jax.random.normal(ks[4], (HEAD_DIM,), f32)
    k_norm_a = 1.0 + 0.02 * jax.random.normal(ks[5], (HEAD_DIM,), f32)
    sink_logits = 0.5 * jax.random.normal(ks[6], (A_HEADS,), f32)
    q_norm_b = 1.0 + 0.02 * jax.random.normal(ks[7], (HEAD_DIM,), f32)
    k_norm_b = 1.0 + 0.02 * jax.random.normal(ks[8], (HEAD_DIM,), f32)
    w_out = jax.random.normal(ks[9], (MIX_WIDTH, D_MODEL), f32) * MIX_WIDTH ** -0.5
    mlp_norm_g = 1.0 + 0.02 * jax.random.normal(ks[10], (D_MODEL,), f32)
    w_up = jax.random.normal(ks[11], (D_MODEL, D_FF), f32) * D_MODEL ** -0.5
    w_down = jax.random.normal(ks[12], (D_FF, D_MODEL), f32) * D_FF ** -0.5
    return {"x": x, "attn_norm_g": attn_norm_g, "w_in": w_in, "b_forget": b_forget,
            "q_norm_a": q_norm_a, "k_norm_a": k_norm_a, "sink_logits": sink_logits,
            "q_norm_b": q_norm_b, "k_norm_b": k_norm_b, "w_out": w_out,
            "mlp_norm_g": mlp_norm_g, "w_up": w_up, "w_down": w_down}

def first_block(x, attn_norm_g, w_in, b_forget, q_norm_a, k_norm_a, sink_logits,
              q_norm_b, k_norm_b, w_out, mlp_norm_g, w_up, w_down):
    b, s, _ = x.shape
    for _layer in range(DEPTH):
        xn = rmsnorm(x, attn_norm_g)
        proj = jnp.einsum('bsd,de->bse', xn, w_in)
        qa, ka, va, qb, kb, vb, f_logit = jnp.split(proj, IN_SPLITS, axis=-1)
        qa = rmsnorm(qa.reshape(b, s, A_HEADS, HEAD_DIM), q_norm_a)
        ka = rmsnorm(ka.reshape(b, s, A_KV_HEADS, HEAD_DIM), k_norm_a)
        va = va.reshape(b, s, A_KV_HEADS, HEAD_DIM)
        out_a = swa_sinks_attention(qa, ka, va, sink_logits)
        qb = rmsnorm(qb.reshape(b, s, B_HEADS, HEAD_DIM), q_norm_b)
        kb = rmsnorm(kb.reshape(b, s, B_HEADS, HEAD_DIM), k_norm_b)
        vb = vb.reshape(b, s, B_HEADS, HEAD_DIM)
        log_f = jax.nn.log_sigmoid(f_logit.astype(jnp.float32) + b_forget.astype(jnp.float32))
        out_b = forgetting_attention(qb, kb, vb, log_f)
        mixed = jnp.concatenate([out_a.reshape(b, s, A_Q_W), out_b.reshape(b, s, B_W)], axis=-1)
        x = x + jnp.einsum('bse,ed->bsd', mixed, w_out)
        hn = rmsnorm(x, mlp_norm_g)
        hid = jnp.square(jax.nn.relu(jnp.einsum('bsd,df->bsf', hn, w_up)))
        x = x + jnp.einsum('bsf,fd->bsd', hid, w_down)
    return x


GRID_W = 64
CTX_LEN = 256
MIX_WIDTH_2 = D_MODEL
POOL_WIDTH = MIX_WIDTH_2 // 2
N_POOL_GROUPS = 4
POOL_GROUP_DIM = POOL_WIDTH // N_POOL_GROUPS
POOL_WINDOWS = (2, 4, 8, 16)
ATTN_WIDTH = MIX_WIDTH_2 - POOL_WIDTH
N_HEADS = 8
HEAD_DIM_2 = ATTN_WIDTH // N_HEADS
NA_KH = 8
NA_KW = 16
NA_QB = 16
NA_KB = 32
NA_NCB = GRID_W // NA_QB
D_FF_2 = 4 * D_MODEL
N_MOD = 6


def _rmsnorm(x, g):
    x32 = x.astype(jnp.float32)
    y = x32 * lax.rsqrt(jnp.mean(x32 * x32, axis=-1, keepdims=True) + EPS)
    return (y * g.astype(jnp.float32)).astype(x.dtype)

def _modulate(x, gain, shift, scale):
    return _rmsnorm(x, gain) * (1 + scale) + shift

def _project(h, w_in_l):
    p = h @ w_in_l
    B, L, _ = p.shape
    u = p[..., :POOL_WIDTH]
    q, k, v = jnp.split(p[..., POOL_WIDTH:], 3, axis=-1)
    shp = (B, L, N_HEADS, HEAD_DIM_2)
    return u, q.reshape(shp), k.reshape(shp), v.reshape(shp)

def _pool_mixer(u, pool_w, pool_scale):
    B, L, _ = u.shape
    u32 = u.reshape(B, L, N_POOL_GROUPS, POOL_GROUP_DIM).astype(jnp.float32)
    cs = jnp.concatenate([jnp.zeros_like(u32[:, :1]), jnp.cumsum(u32, axis=1)], axis=1)
    t = jnp.arange(L)
    diffs = []
    for g, w in enumerate(POOL_WINDOWS):
        lo = w // 2
        hi = w - 1 - lo
        start = jnp.clip(t - lo, 0, L)
        end = jnp.clip(t + hi + 1, 0, L)
        count = (end - start).astype(jnp.float32)[None, :, None]
        diffs.append((cs[:, end, g] - cs[:, start, g]) / count - u32[:, :, g])
    d = jnp.stack(diffs, axis=2).astype(u.dtype)
    y = jnp.einsum('blgc,gcd->blgd', d, pool_w)
    return y.reshape(B, L, POOL_WIDTH) * pool_scale

def _na_column_tables():
    qcol = np.arange(GRID_W).reshape(NA_NCB, NA_QB)
    q_start = np.clip(qcol - NA_KW // 2, 0, GRID_W - NA_KW)
    kc0 = np.clip(np.arange(NA_NCB) * NA_QB - NA_KW // 2, 0, GRID_W - NA_KB)
    col_idx = kc0[:, None] + np.arange(NA_KB)
    kc = col_idx[:, None, :]
    mask = (kc >= q_start[:, :, None]) & (kc < q_start[:, :, None] + NA_KW)
    dc = np.clip(kc - qcol[:, :, None] + NA_KW - 1, 0, 2 * NA_KW - 2)
    return col_idx.astype(np.int32), mask, dc.astype(np.int32)

def _neighbourhood_attention(q, k, v, k_ctx, v_ctx, rpb):
    B, L, H, Dh = q.shape
    rows = L // GRID_W
    kh = min(NA_KH, rows)
    col_np, mask_np, dc_np = _na_column_tables()
    col_idx = jnp.asarray(col_np)
    col_mask = jnp.asarray(mask_np)[:, :, None, :]
    dc_idx = jnp.asarray(dc_np)[:, :, None, :]
    qg = q.reshape(B, rows, GRID_W, H, Dh)
    kg = k.reshape(B, rows, GRID_W, H, Dh)
    vg = v.reshape(B, rows, GRID_W, H, Dh)
    scale = Dh ** -0.5
    n_loc = kh * NA_KB

    def row_block(r):
        rs = jnp.clip(r - kh // 2, 0, rows - kh)
        q_r = lax.dynamic_index_in_dim(qg, r, axis=1, keepdims=False).reshape(B, NA_NCB, NA_QB, H, Dh)
        k_b = lax.dynamic_slice_in_dim(kg, rs, kh, axis=1)[:, :, col_idx]
        v_b = lax.dynamic_slice_in_dim(vg, rs, kh, axis=1)[:, :, col_idx]
        s_loc = jnp.einsum('bnqhd,brnkhd->bhnqrk', q_r, k_b).astype(jnp.float32) * scale
        dr_idx = rs + jnp.arange(kh) - r + (NA_KH - 1)
        bias = rpb[:, dr_idx[None, None, :, None], dc_idx]
        s_loc = jnp.where(col_mask, s_loc + bias.astype(jnp.float32), -jnp.inf)
        s_ctx = jnp.einsum('bnqhd,bkhd->bhnqk', q_r, k_ctx).astype(jnp.float32) * scale
        s = jnp.concatenate([s_loc.reshape(B, H, NA_NCB, NA_QB, n_loc), s_ctx], axis=-1)
        p = jax.nn.softmax(s, axis=-1).astype(v.dtype)
        p_loc = p[..., :n_loc].reshape(B, H, NA_NCB, NA_QB, kh, NA_KB)
        p_ctx = p[..., n_loc:]
        o = (jnp.einsum('bhnqrk,brnkhd->bnqhd', p_loc, v_b)
             + jnp.einsum('bhnqk,bkhd->bnqhd', p_ctx, v_ctx))
        return o.reshape(B, GRID_W, H, Dh)

    out = lax.map(row_block, jnp.arange(rows))
    return jnp.moveaxis(out, 0, 1).reshape(B, L, H * Dh)

def _context_attention(q, k, v):
    B, C, H, Dh = q.shape
    s = jnp.einsum('bqhd,bkhd->bhqk', q, k).astype(jnp.float32) * (Dh ** -0.5)
    p = jax.nn.softmax(s, axis=-1).astype(v.dtype)
    return jnp.einsum('bhqk,bkhd->bqhd', p, v).reshape(B, C, H * Dh)

def _sq_relu_mlp(h, w1, w2):
    return jnp.square(jax.nn.relu(h @ w1)) @ w2

def second_inputs(seed: int = 0) -> dict:
    key = jax.random.key(seed)
    ks = jax.random.split(key, 17)
    D = D_MODEL
    nrm = jax.random.normal
    return {
        'x': nrm(ks[0], (BATCH, SEQ, D), jnp.float32),
        'c': nrm(ks[1], (BATCH, D), jnp.float32),
        'ctx': nrm(ks[2], (BATCH, CTX_LEN, D), jnp.float32),
        'c_ctx': nrm(ks[3], (D,), jnp.float32),
        'w_mod': nrm(ks[4], (DEPTH, D, N_MOD * D), jnp.float32) * (0.5 * D ** -0.5),
        'b_mod': nrm(ks[5], (DEPTH, N_MOD * D), jnp.float32) * 0.02,
        'g_pre_mix': 1.0 + 0.1 * nrm(ks[6], (DEPTH, D), jnp.float32),
        'g_post_mix': 1.0 + 0.1 * nrm(ks[7], (DEPTH, D), jnp.float32),
        'g_pre_mlp': 1.0 + 0.1 * nrm(ks[8], (DEPTH, D), jnp.float32),
        'g_post_mlp': 1.0 + 0.1 * nrm(ks[9], (DEPTH, D), jnp.float32),
        'w_in': nrm(ks[10], (DEPTH, D, POOL_WIDTH + 3 * ATTN_WIDTH), jnp.float32) * D ** -0.5,
        'pool_w': nrm(ks[11], (DEPTH, N_POOL_GROUPS, POOL_GROUP_DIM, POOL_GROUP_DIM), jnp.float32) * POOL_GROUP_DIM ** -0.5,
        'pool_scale': 1.0 + 0.1 * nrm(ks[12], (DEPTH, POOL_WIDTH), jnp.float32),
        'rpb': 0.1 * nrm(ks[13], (DEPTH, N_HEADS, 2 * NA_KH - 1, 2 * NA_KW - 1), jnp.float32),
        'w_out': nrm(ks[14], (DEPTH, MIX_WIDTH_2, D), jnp.float32) * MIX_WIDTH_2 ** -0.5,
        'w_mlp_in': nrm(ks[15], (DEPTH, D, D_FF_2), jnp.float32) * D ** -0.5,
        'w_mlp_out': nrm(ks[16], (DEPTH, D_FF_2, D), jnp.float32) * D_FF_2 ** -0.5,
    }

def second_block(x, c, ctx, c_ctx, w_mod, b_mod, g_pre_mix, g_post_mix, g_pre_mlp, g_post_mlp,
              w_in, pool_w, pool_scale, rpb, w_out, w_mlp_in, w_mlp_out):
    for l in range(DEPTH):
        last = l == DEPTH - 1
        mod_x = (jax.nn.silu(c) @ w_mod[l] + b_mod[l])[:, None, :]
        mod_c = jax.nn.silu(c_ctx) @ w_mod[l] + b_mod[l]
        sh1, sc1, gt1, sh2, sc2, gt2 = jnp.split(mod_x, N_MOD, axis=-1)
        csh1, csc1, cgt1, csh2, csc2, cgt2 = jnp.split(mod_c, N_MOD, axis=-1)

        h_x = _modulate(x, g_pre_mix[l], sh1, sc1)
        h_c = _modulate(ctx, g_pre_mix[l], csh1, csc1)
        u_x, q_x, k_x, v_x = _project(h_x, w_in[l])
        u_c, q_c, k_c, v_c = _project(h_c, w_in[l])
        attn_x = _neighbourhood_attention(q_x, k_x, v_x, k_c, v_c, rpb[l])
        mix_x = jnp.concatenate([_pool_mixer(u_x, pool_w[l], pool_scale[l]), attn_x], axis=-1) @ w_out[l]
        x = x + gt1 * _rmsnorm(mix_x, g_post_mix[l])
        y_x = _sq_relu_mlp(_modulate(x, g_pre_mlp[l], sh2, sc2), w_mlp_in[l], w_mlp_out[l])
        x = x + gt2 * _rmsnorm(y_x, g_post_mlp[l])

        if not last:
            attn_c = _context_attention(q_c, k_c, v_c)
            mix_c = jnp.concatenate([_pool_mixer(u_c, pool_w[l], pool_scale[l]), attn_c], axis=-1) @ w_out[l]
            ctx = ctx + cgt1 * _rmsnorm(mix_c, g_post_mix[l])
            y_c = _sq_relu_mlp(_modulate(ctx, g_pre_mlp[l], csh2, csc2), w_mlp_in[l], w_mlp_out[l])
            ctx = ctx + cgt2 * _rmsnorm(y_c, g_post_mlp[l])
    return x


def setup_inputs(seed=0):
    out = dict(first_inputs(seed))
    for name, value in second_inputs(seed + 1).items():
        if name != "x":
            out[name + "_2"] = value
    return out


def reference(
    x, attn_norm_g, w_in, b_forget, q_norm_a, k_norm_a, sink_logits, q_norm_b, k_norm_b, w_out,
    mlp_norm_g, w_up, w_down, c_2, ctx_2, c_ctx_2, w_mod_2, b_mod_2, g_pre_mix_2, g_post_mix_2,
    g_pre_mlp_2, g_post_mlp_2, w_in_2, pool_w_2, pool_scale_2, rpb_2, w_out_2, w_mlp_in_2,
    w_mlp_out_2,
):
    x = first_block(
        x, attn_norm_g, w_in, b_forget, q_norm_a, k_norm_a, sink_logits, q_norm_b, k_norm_b,
        w_out, mlp_norm_g, w_up, w_down,
    )
    return second_block(
        x, c_2, ctx_2, c_ctx_2, w_mod_2, b_mod_2, g_pre_mix_2, g_post_mix_2, g_pre_mlp_2,
        g_post_mlp_2, w_in_2, pool_w_2, pool_scale_2, rpb_2, w_out_2, w_mlp_in_2, w_mlp_out_2,
    )


_drawn_inputs = setup_inputs


def setup_inputs(seed=0):
    import zlib

    import numpy as np

    out = dict(_drawn_inputs(seed))
    spreads = {}
    factors = {'attn_norm_g': 4.817,
     'q_norm_a': 8.0,
     'k_norm_a': 8.0,
     'q_norm_b': 8.0,
     'k_norm_b': 8.0,
     'mlp_norm_g': 3.333,
     'ctx_2': 3.126,
     'b_mod_2': 3.074,
     'g_pre_mix_2': 16.209,
     'g_post_mix_2': 26.472,
     'g_post_mlp_2': 25.096,
     'pool_scale_2': 23.256,
     'rpb_2': 200.0,
     'sink_logits': 60.426,
     'c_ctx_2': 3.772,
     'g_pre_mlp_2': 7.008}
    for name, (base, spread) in spreads.items():
        noise = np.random.default_rng([zlib.crc32(name.encode()), seed]).standard_normal(out[name].shape)
        drawn = base * np.exp(spread * noise) if base else spread * noise
        out[name] = __import__('jax').numpy.asarray(drawn.astype(out[name].dtype))
    for name, factor in factors.items():
        out[name] = (out[name] * factor).astype(out[name].dtype)
    return out
```

```python
from contextlib import ExitStack

import numpy as np

import concourse.bass as bass
import concourse.mybir as mybir

F32 = mybir.dt.float32
F32R = mybir.dt.float32r
BF16 = mybir.dt.bfloat16
ALU = mybir.AluOpType
ACT = mybir.ActivationFunctionType
AXX = mybir.AxisListType.X

P = 128
D = 1024
S = 512
CTX = 256
DFF = 4096
HD = 64
NH = 8
KT = D // P
TT = S // P
CT = CTX // P
NC = 512
UK = 2
UQ = KT // UK
NCH = DFF // D
EPS = 1e-6
NEG = -1e30
QSCALE = HD ** -0.5

GR, GW = 8, 64
KH, KW = 8, 16
RPW = 2 * KW - 1
RPH = 2 * KH - 1
RUN = (KH - 1) * RPW + 32 + 16
RPAD = 16
RPB_LEN = 2 * RPAD + NH * RPH * RPW
KSTART = (0, 64, 192, 256)
KSHIFT = (16, 8, 8, 0)

IN1_COLS = ((0, 512), (512, 256), (768, 512), (1280, 512), (1792, 512))
KV_W = 264
N_IN1, N_OUT, N_MLP, N_IN2 = 5, 2, 4 * NCH, 4
SLAB_OUT1 = N_IN1
SLAB_MLP1 = SLAB_OUT1 + N_OUT
SLAB_IN2 = SLAB_MLP1 + N_MLP
SLAB_OUT2 = SLAB_IN2 + N_IN2
SLAB_MLP2 = SLAB_OUT2 + N_OUT
SLABS = SLAB_MLP2 + N_MLP

TILE_OUT1 = 4 * N_IN1
TILE_MLP1 = TILE_OUT1 + 2 * TT
TILE_IN2 = TILE_MLP1 + 4 * N_MLP
IN2_TILES = (4, 4, 4 + 4, CT + TT)
TILE_OUT2 = TILE_IN2 + sum(IN2_TILES)
TILE_MLP2 = TILE_OUT2 + 2 * TT


def slab_end(s):
    if s < SLAB_IN2:
        return 4 * (s + 1)
    if s < SLAB_OUT2:
        return TILE_IN2 + sum(IN2_TILES[:s - SLAB_IN2 + 1])
    return TILE_OUT2 + 4 * (s - SLAB_OUT2 + 1)


STAT_N1, STAT_N2, STAT_N3, STAT_CTX, STAT_TAIL, STAT_FIN = 0, 4, 8, 12, 14, 22
NT_1, NT_2, NT_3, NT_CTX, NT_4 = 0, 4, 8, 12, 14

U1 = [(n, kind, h) for n in range(TT) for kind in range(2) for h in range(NH)]
U2 = [(n, h) for n in range(TT) for h in range(NH)]
LAG_T, LAG_V, LAG_M = 2, 3, 4


def attention_order(units, per_tile, halves):
    steps = []
    for i in range(units + LAG_M + 1):
        step = []
        if 0 <= i - LAG_T < units:
            step.append(("T", i - LAG_T))
        if 0 <= i - LAG_V < units:
            step.append(("V", i - LAG_V))
        if i >= per_tile + LAG_M and (i - LAG_M) % per_tile == 0:
            step.append(("M", (i - LAG_M) // per_tile - 1))
        steps.append(step)
    turn = {}
    for step in steps:
        for what, k in step:
            if what == "T":
                turn[what, k] = len(turn)
            elif what == "M":
                for half in range(halves):
                    turn[what, k, half] = len(turn)
    return steps, turn


STEPS1, TURN1 = attention_order(len(U1), 2 * NH, 2)
STEPS2, TURN2 = attention_order(len(U2), NH, 1)


class Tally:

    def __init__(self):
        self.n = {}

    def up(self, sem, k=1):
        self.n[sem.name] = self.n.get(sem.name, 0) + k
        return self.n[sem.name]


def build(nc, t, out):
    ctx = ExitStack()
    with ctx:
        base = (nc.sbuf_base + 63) // 64 * 64
        top = [base]

        def at(name, shape, dtype, offset):
            return nc.alloc_sbuf_tensor_at(name, shape, dtype, offset=offset)

        def place(name, shape, dtype):
            a = top[0]
            size = int(np.prod(shape[1:])) * (2 if dtype == BF16 else 4)
            top[0] = a + (size + 31) // 32 * 32
            return at(name, shape, dtype, a)

        def region(kib):
            a = top[0]
            top[0] = a + kib * 1024
            return a

        K = 1024
        raw = [place(f"w_raw{q}", [P, UK, NC], F32) for q in range(UQ)]
        w_hi = [place(f"w_hi{s}", [P, KT, NC], F32R) for s in range(2)]
        w_lo = [place(f"w_lo{s}", [P, KT, NC], F32R) for s in range(2)]
        xt_hi = place("xt_hi", [P, KT, S], F32R)
        xt_lo = place("xt_lo", [P, KT, S], F32R)
        x = place("x", [P, TT, D], F32)
        H = region(32)
        ht_hi = at("ht_hi", [P, KT, S], F32R, H)
        ht_lo = at("ht_lo", [P, KT, S], F32R, H + 16 * K)
        q_a = at("q_a", [P, 4, S], F32, H)
        q_b = at("q_b", [P, 4, S], F32, H + 8 * K)
        k_b = at("k_b", [P, 4, S], F32, H + 16 * K)
        v_b = at("v_b", [P, TT, S], F32, H + 24 * K)
        pooled = at("pooled", [P, 4, S], F32, H)
        q_2 = at("q_2", [P, 4, S], F32, H + 8 * K)
        k_2 = at("k_2", [P, 4, S], F32, H + 16 * K)
        v_2 = at("v_2", [P, TT, S], F32, H + 24 * K)
        mod_scale = at("mod_scale", [P, D], F32, H + 16 * K)
        mod_shift = at("mod_shift", [P, D], F32, H + 20 * K)
        mod_gain = at("mod_gain", [P, D], F32, H + 24 * K)
        mix_gate = at("mix_gate", [P, D], F32, H)
        mix_gain = at("mix_gain", [P, D], F32, H + 4 * K)
        mlp_scale = at("mlp_scale", [P, D], F32, H + 8 * K)
        mlp_shift = at("mlp_shift", [P, D], F32, H + 12 * K)
        mlp_gain2 = at("mlp_gain2", [P, D], F32, H + 16 * K)
        A = region(16)
        mixed = at("mixed", [P, TT, D], F32, A)
        frow = at("frow", [NH, 6, S], F32, A)
        wm = [at(f"wm{i}", [P, UK, NC], F32, A + 4 * K * i) for i in range(2)]
        mod_acc = [[at(f"mod_acc{i}{j}", [P, NC], F32, A + 8 * K + 4 * K * i + 2 * K * j) for j in range(2)]
                   for i in range(2)]
        ct_hi = at("ct_hi", [P, KT, CTX], F32R, A)
        ct_lo = at("ct_lo", [P, KT, CTX], F32R, A + 8 * K)
        v_odd = at("v_odd", [P, TT - 1, S], F32, A)
        attn_2 = [at(f"attn_2{i}", [P, NC], F32, A + 6 * K + 2 * K * i) for i in range(2)]
        sub = at("sub", [P, TT, D], F32, A)
        T = region(8)
        xr = [at(f"xr{i}", [P, D], F32, T + 4 * K * i) for i in range(2)]
        qn = [at(f"qn{i}", [P, NC], F32, T + 2 * K * i) for i in range(2)]
        qsq = [at(f"qsq{i}", [P, NC], F32, T + 4 * K + 2 * K * i) for i in range(2)]
        prob = [at(f"prob{i}", [P, NC], F32, T + 2 * K * i) for i in range(2)]
        prob_t = [at(f"prob_t{i}", [P, 4, P], F32, T + 4 * K + 2 * K * i) for i in range(2)]
        hid = [at(f"hid{i}", [P, NC], F32, T + 2 * K * i) for i in range(2)]
        upad = at("upad", [P, 544], F32, T)
        wsum = [at(f"wsum{i}", [P, 544], F32, T + 2176 * (i + 1)) for i in range(2)]
        ident = place("ident", [P, P], F32)
        identb = place("identb", [P, P], BF16)
        J = top[0]
        junk = place("junk", [P, D], BF16)
        v_a = at("v_a", [P, TT, P], F32, J)
        pool_w = at("pool_w", [P, 4, P], F32, J)
        causal = place("causal", [P, P], BF16)
        window = place("window", [P, 3, 256], BF16)
        st = place("st", [P, 4, 32], F32)
        hst = place("hst", [P, 4, NH], F32)
        nmax = place("nmax", [P, NH], F32)
        den = place("den", [P, 2 * NH], F32)
        rden = place("rden", [P, 2 * NH], F32)
        gains = place("gains", [P, 4], F32)
        cvec = place("cvec", [P, 2, KT], F32)
        csil = place("csil", [P, 2, KT], F32)
        ctmp = place("ctmp", [P, 2, KT], F32)
        flog = place("flog", [P, TT, NH], F32)
        b_f = place("b_f", [NH, 1], F32)
        sink = place("sink", [1, NH], F32)
        ones_row = place("ones_row", [1, P], F32)
        ones_col = place("ones_col", [P, 1], F32)
        pscale = place("pscale", [P, 4], F32)
        edge = place("edge", [P, 4, 16], F32)
        E = top[0]
        gain1 = at("gain1", [P, D], F32, E)
        alibi = at("alibi", [P, NH, 256], BF16, E)
        k_a = at("k_a", [P, 2, S], F32, E + 4 * K)
        c_hi = at("c_hi", [NH, S], F32R, E + 8 * K)
        c_lo = at("c_lo", [NH, S], F32R, E + 10 * K)
        negsel = at("negsel", [NH, NH, P], F32R, E + 12 * K)
        gain2 = at("gain2", [P, D], F32, E)
        b_row = at("b_row", [1, 3, NC], F32, E + 4 * K)
        mod_row = [b_row, at("cmod_row", [1, 3, NC], F32, E + 10 * K)]
        cmod_scale = at("cmod_scale", [P, D], F32, E)
        cmod_shift = at("cmod_shift", [P, D], F32, E + 4 * K)
        cx = at("cx", [P, CT, D], F32, E + 8 * K)
        rpb_run = at("rpb_run", [P, NH, RUN], F32, E)
        k_c = at("k_c", [P, 4, CTX], F32, E + 8512)
        v_c = at("v_c", [P, CT, S], F32, E + 8512 + 4 * K)
        fin_gate = at("fin_gate", [P, D], F32, E)
        fin_gain = at("fin_gain", [P, D], F32, E + 4 * K)
        assert E + 17 * K <= nc.sbuf_usable_end, (E, nc.sbuf_usable_end)

        mods = nc.dram_tensor("mods", (2, 12 * NC), F32, kind="Internal").ap()

        def ps(name):
            return ctx.enter_context(nc.psum_tensor(name, [P, NC], F32))

        gp = [ps(f"gemm{i}") for i in range(4)]
        aux = [ps(f"aux{i}") for i in range(4)]

        sems = {}

        def sem(name):
            sems[name] = ctx.enter_context(nc.semaphore(name))
            return sems[name]

        x_loaded = [sem(f"x_loaded{m}") for m in range(TT)]
        ident_loaded = sem("ident_loaded")
        gain1_loaded, gain2_loaded = sem("gain1_loaded"), sem("gain2_loaded")
        heads_loaded, vec_loaded = sem("heads_loaded"), sem("vec_loaded")
        alibi_loaded, negsel_loaded = sem("alibi_loaded"), sem("negsel_loaded")
        mod_loaded, cx_loaded = sem("mod_loaded"), sem("cx_loaded")
        rpb_loaded, pool_loaded = sem("rpb_loaded"), sem("pool_loaded")
        tail_loaded, fin_loaded = sem("tail_loaded"), sem("fin_loaded")
        v_shifted, out_stored = sem("v_shifted"), sem("out_stored")
        raw_loaded = [sem(f"raw_loaded{q}") for q in range(UQ)]
        hi_split, unit_split = sem("hi_split"), sem("unit_split")
        gemm_done, gemm_free = sem("gemm_done"), sem("gemm_free")
        ones_ready, negsel_ready = sem("ones_ready"), sem("negsel_ready")
        ssq_done, ms_done, ln_done, rs0_done, rs_done = (sem(n) for n in (
            "ssq_done", "ms_done", "ln_done", "rs0_done", "rs_done"))
        xr_step, xr_ready = sem("xr_step"), sem("xr_ready")
        xr_turned, xt_hi_done, xt_lo_done = sem("xr_turned"), sem("xt_hi_done"), sem("xt_lo_done")
        hsq_done, hms_done, hln_done, hrs0_done, hrs_done = (sem(n) for n in (
            "hsq_done", "hms_done", "hln_done", "hrs0_done", "hrs_done"))
        qn_ready, qn_turned, qk_stored = sem("qn_ready"), sem("qn_turned"), sem("qk_stored")
        v_copied, f_copied, f_turned, f_step, f_act = (sem(n) for n in (
            "v_copied", "f_copied", "f_turned", "f_step", "f_act"))
        c_hi_done, c_ready = sem("c_hi_done"), sem("c_ready")
        score_done, bias_added, max_done, exp_done = (sem(n) for n in (
            "score_done", "bias_added", "max_done", "exp_done"))
        turned, turn_read, turn_hi, pv_done, rden_done, heads_out = (sem(n) for n in (
            "turned", "turn_read", "turn_hi", "pv_done", "rden_done", "heads_out"))
        relu_done, hid_ready, hid_hi, hid_lo = (sem(n) for n in ("relu_done", "hid_ready", "hid_hi", "hid_lo"))
        silu_step, silu_act, wm_used, mod_summed, mod_rowed, mod_stored = (sem(n) for n in (
            "silu_step", "silu_act", "wm_used", "mod_summed", "mod_rowed", "mod_stored"))
        wm_loaded = [sem(f"wm_loaded{i}") for i in range(2)]
        b_loaded = sem("b_loaded")
        pool_step, pool_done, pool_mixed, pool_hi = (sem(n) for n in (
            "pool_step", "pool_done", "pool_mixed", "pool_hi"))
        mod_made, tail_step, fin_step = sem("mod_made"), sem("tail_step"), sem("fin_step")

        GATE_CREDIT = 1

        def perm_in(ap):
            return ap.rearrange("p (r b c) -> p r b c", b=GW // 8, c=8)

        @block_fn(nc, ctx, "sync")
        def _(sp):
            sp.dma_start(ident[:], t["c_ident"]).then_inc(ident_loaded, 16)
            for m in range(TT):
                sp.dma_start(x[:, m, :], t["x"][m * P:(m + 1) * P, :]).then_inc(x_loaded[m], 16)

            def unit(q, src, width, wait):
                if wait is not None:
                    sp.wait_ge(unit_split, wait)
                sp.dma_start(raw[q][:, :, 0:width], src).then_inc(raw_loaded[q], 16)

            def rows(w, r0, q):
                return w[r0 + q * UK * P:r0 + (q + 1) * UK * P, :].rearrange("(k p) n -> p k n", p=P)

            def slab(s, w, c0, width):
                for q in range(UQ):
                    wait = 4 * (s - 1) + q + 1 if s else None
                    unit(q, rows(w, 0, q)[:, :, c0:c0 + width], width, wait)

            for s, (c0, width) in enumerate(IN1_COLS):
                if s == 1:
                    for q in range(UQ):
                        src = rows(t["w_in"], 0, q)
                        sp.wait_ge(unit_split, q + 1)
                        sp.dma_start(raw[q][:, :, 0:256], src[:, :, c0:c0 + 256]).then_inc(raw_loaded[q], 16)
                        sp.dma_start(raw[q][:, :, 256:KV_W], src[:, :, 2304:2312]).then_inc(raw_loaded[q], 16)
                else:
                    slab(s, t["w_in"], c0, width)
            for j in range(N_OUT):
                slab(SLAB_OUT1 + j, t["w_out"], j * NC, NC)

            def mlp(s0, up, down):
                with sp.Fori(0, NCH) as i:
                    for a in range(2):
                        for q in range(UQ):
                            src = rows(up, 0, q)[:, :, bass.ds(i * D + a * NC, NC)]
                            unit(q, src, NC, i * 16 + (4 * (s0 + a - 1) + q + 1))
                    down_r = down.rearrange("(c u k p) n -> c u p k n", c=NCH, k=UK, p=P)
                    for a in range(2):
                        for q in range(UQ):
                            src = down_r[bass.ds(i, 1), q, :, :, a * NC:(a + 1) * NC]
                            src = src.rearrange("o p k n -> (o p) k n")
                            unit(q, src, NC, i * 16 + (4 * (s0 + a + 1) + q + 1))

            mlp(SLAB_MLP1, t["w_up"], t["w_down"])
            for j, c0 in enumerate((0, 512, 1024, 1536)):
                slab(SLAB_IN2 + j, t["w_in_2"], c0, NC)
            for j in range(N_OUT):
                slab(SLAB_OUT2 + j, t["w_out_2"], j * NC, NC)
            mlp(SLAB_MLP2, t["w_mlp_in_2"], t["w_mlp_out_2"])
            for m in range(TT):
                sp.wait_ge(fin_step, 2 * (m + 1))
                sp.dma_start(out[m * P:(m + 1) * P, :], x[:, m, :]).then_inc(out_stored, 16)
            sp.wait_ge(out_stored, 16 * TT)

        @block_fn(nc, ctx, "gpsimd")
        def _(pool):
            def low(s, q, width, wait):
                pool.wait_ge(hi_split, wait)
                ks = slice(UK * q, UK * (q + 1))
                pool.tensor_tensor(w_lo[s % 2][:, ks, 0:width], raw[q][:, :, 0:width],
                                   w_hi[s % 2][:, ks, 0:width].bitcast(F32), ALU.subtract).then_inc(unit_split, 1)

            for s in range(N_IN1):
                for q in range(UQ):
                    low(s, q, KV_W if s == 1 else NC, 4 * s + q + 1)
            with pool.Fori(0, (SLABS - N_IN1) // 2) as i:
                for a in range(2):
                    for q in range(UQ):
                        low(N_IN1 + a, q, NC, i * 8 + (4 * (N_IN1 + a) + q + 1))

        @block_fn(nc, ctx, "scalar")
        def _(act):
            tally = Tally()

            def did(ins, s):
                ins.then_inc(s, 1)
                act.wait_ge(s, tally.up(s))

            def load(dst, src, s):
                act.dma_start(dst, src).then_inc(s, 16)

            def spread(v, n=D):
                return v.partition_broadcast(P)

            act.preload_act_table_set("natural_log_exp_and_others")
            load(gain1[:], spread(t["attn_norm_g"]), gain1_loaded)
            load(gains[0:HD, 0:1], t["q_norm_a"].rearrange("(p a) -> p a", a=1), heads_loaded)
            load(gains[HD:P, 0:1], t["q_norm_a"].rearrange("(p a) -> p a", a=1), heads_loaded)
            load(gains[0:HD, 1:2], t["k_norm_a"].rearrange("(p a) -> p a", a=1), heads_loaded)
            load(gains[HD:P, 1:2], t["k_norm_a"].rearrange("(p a) -> p a", a=1), heads_loaded)
            load(gains[0:HD, 2:3], t["q_norm_b"].rearrange("(p a) -> p a", a=1), heads_loaded)
            load(gains[HD:P, 2:3], t["q_norm_b"].rearrange("(p a) -> p a", a=1), heads_loaded)
            load(gains[0:HD, 3:4], t["k_norm_b"].rearrange("(p a) -> p a", a=1), heads_loaded)
            load(gains[HD:P, 3:4], t["k_norm_b"].rearrange("(p a) -> p a", a=1), heads_loaded)
            load(b_f[:], t["b_forget"].rearrange("(p a) -> p a", a=1), vec_loaded)
            load(sink[:], t["sink_logits"].rearrange("(a n) -> a n", a=1), vec_loaded)
            load(cvec[:, 0, :], t["c"], vec_loaded)
            load(cvec[:, 1, :], t["c_ctx"], vec_loaded)
            load(identb[:], t["c_identb"], vec_loaded)
            load(causal[:], t["c_causal"], vec_loaded)
            load(window[:], t["c_window"], vec_loaded)
            load(edge[:], t["c_edge"], vec_loaded)
            load(pscale[:], t["pool_scale"], vec_loaded)
            load(frow[:, 0:2, :].rearrange("h a s -> h (a s)"), t["c_negsel"], negsel_loaded)

            def high(s, q, width=NC, loaded=None, free=None):
                act.wait_ge(raw_loaded[q], loaded)
                if free is not None:
                    act.wait_ge(gemm_done, free)
                act.activation(w_hi[s % 2][:, UK * q:UK * (q + 1), 0:width], raw[q][:, :, 0:width],
                               ACT.Copy).then_inc(hi_split, 1)

            def arrived(s):
                return 16 * (s + 1) + (16 if s >= 1 else 0)

            def high_of(s, q):
                high(s, q, KV_W if s == 1 else NC, arrived(s), slab_end(s - 2) if s >= 2 else None)

            def stat(k, ready, src, width=D):
                if ready is not None:
                    act.wait_ge(*ready)
                did(act.activation(junk[:, 0:width], src, ACT.Square, accum_out=st[:, 0, k:k + 1]), ssq_done)
                act.wait_ge(ms_done, k + 1)
                did(act.activation(st[:, 2, k:k + 1], st[:, 1, k:k + 1], ACT.Ln), ln_done)
                did(act.activation(st[:, 3, k:k + 1], st[:, 2, k:k + 1], ACT.Exp, scale=-0.5), rs0_done)

            def xt_high(n, cols, permute=False, dst=None):
                for half in range(2):
                    act.wait_ge(xr_turned, 2 * n + half + 1)
                    did(act.activation(token_cols(xt_hi if dst is None else dst, half, cols, permute),
                                       bank_cols(aux[(2 * n + half) % 4], permute), ACT.Copy), xt_hi_done)

            for m in range(TT):
                stat(STAT_N1 + m, (x_loaded[m], 16), x[:, m, :])
                if m >= 1:
                    high_of(0, m - 1)
                    xt_high(NT_1 + m - 1, m - 1)
            high_of(0, UQ - 1)
            xt_high(NT_1 + 3, 3)
            act.wait_ge(xr_ready, 4)
            load(alibi[:], t["c_alibi"], alibi_loaded)
            act.wait_ge(vec_loaded, 16 * 9)
            did(act.activation(ctmp[:], cvec[:], ACT.Exp, scale=-1.0), silu_act)
            act.wait_ge(negsel_loaded, 16)
            did(act.activation(negsel[:].rearrange("h g p -> h (g p)"),
                               frow[:, 0:2, :].rearrange("h a s -> h (a s)"), ACT.Copy), negsel_ready)

            act.wait_ge(heads_loaded, 16 * 8)

            def head_gain(u):
                kind, m = u // 4, u % 4
                dst = (q_a, k_a, q_b, k_b)[kind]
                pairs = 2 if kind == 1 else 4
                act.wait_ge(qn_turned, u + 1)
                did(act.activation(dst[:, 0:pairs, m * P:(m + 1) * P],
                                   aux[u % 4][:, 0:pairs * P].rearrange("p (h s) -> p h s", h=pairs),
                                   ACT.Copy, scale=gains[:, kind:kind + 1]), qk_stored)

            for g in range(4 * N_IN1):
                s, m = g // 4, g % 4
                if g < 16:
                    heads = 2 if s == 1 else NH
                    act.wait_ge(gemm_done, g + 1)
                    if g >= 2:
                        act.wait_ge(hms_done, g - 1)
                    did(act.activation(qsq[g % 2][:, 0:heads * HD], gp[g % 4][:, 0:heads * HD], ACT.Square), hsq_done)
                    act.wait_ge(hms_done, g + 1)
                    did(act.activation(hst[:, 2, 0:heads], hst[:, 1, 0:heads], ACT.Ln), hln_done)
                    did(act.activation(hst[:, 3, 0:heads], hst[:, 2, 0:heads], ACT.Exp, scale=-0.5), hrs0_done)
                if 1 <= g <= 16:
                    head_gain(g - 1)
                high_of(s + 1, m)
                if g == 10:
                    act.wait_ge(f_step, 3)
                    did(act.activation(frow[:, 3, :], frow[:, 2, :], ACT.Exp, scale=-1.0), f_act)
                    act.wait_ge(f_step, 4)
                    did(act.activation(frow[:, 3, :], frow[:, 3, :], ACT.Ln), f_act)
                if g == 11:
                    act.wait_ge(f_step, 7)
                    did(act.activation(c_hi[:], frow[:, 5, :], ACT.Copy), c_hi_done)

            def exp_unit(i, cols, column):
                act.wait_ge(max_done, i + 1)
                if i >= 2:
                    act.wait_ge(turned, turn[("T", i - 2)] + 1)
                if i >= 16:
                    act.wait_ge(rden_done, i // 8 - 1)
                lo, hi = cols
                did(act.activation(prob[i % 2][:, lo:hi] if hi <= NC else None, gp[i % 4][:, lo:hi], ACT.Exp,
                                   bias=nmax[:, i % 8:i % 8 + 1], accum_out=den[:, column:column + 1]), exp_done)

            turn = TURN1
            for i, step in enumerate(STEPS1):
                if i < len(U1):
                    n, kind, h = U1[i]
                    exp_unit(i, score_cols(n, kind), i % 16)
                for what, k in step:
                    if what == "M":
                        for half in range(2):
                            w = turn[("M", k, half)]
                            act.wait_ge(turned, w + 1)
                            did(act.activation(xt_hi[:, 4 * half:4 * half + 4, k * P:(k + 1) * P],
                                               aux[w % 2][:].rearrange("p (k s) -> p k s", k=4), ACT.Copy), turn_hi)
            load(gain2[:], spread(t["mlp_norm_g"]), gain2_loaded)

            for j in range(N_OUT):
                for m in range(TT):
                    if j:
                        stat(STAT_N2 + m, (gemm_free, TILE_OUT1 + 4 * j + m + 1), x[:, m, :])
                        if m:
                            xt_high(NT_2 + m - 1, m - 1)
                    else:
                        act.wait_ge(gemm_done, TILE_OUT1 + 4 * j + m + 1)
                    high_of(SLAB_OUT1 + j + 1, m)
            xt_high(NT_2 + 3, 3)

            def mlp(s0, t0, mod):
                hi0 = tally.n.get(hid_hi.name, 0)
                def chunk(i, last=False):
                    if mod:
                        load(b_row[:].rearrange("o a n -> o (a n)"),
                             t["b_mod"].rearrange("(a n) -> a n", a=1)[:, bass.ds(i * 3 * NC, 3 * NC)], b_loaded)
                        for u in range(2):
                            act.wait_ge(wm_used, i * 48 + GATE_CREDIT)
                            wm_load(act, u, i)
                    for c in range(16):
                        if c < 8:
                            act.wait_ge(hid_ready, i * 8 + (hi0 + c + 1))
                            act.activation(ht_hi[:, c, :], hid[c % 2][:], ACT.Copy).then_inc(hid_hi, 1)
                        a, q = c // 4, c % 4
                        s = s0 + a + 1
                        if not (last and a == 3):
                            act.wait_ge(raw_loaded[q], i * 64 + arrived(s))
                            act.wait_ge(gemm_done, i * 16 + slab_end(s - 2))
                            act.activation(w_hi[s % 2][:, UK * q:UK * (q + 1), :], raw[q][:, :, :],
                                           ACT.Copy).then_inc(hi_split, 1)
                        if mod and 1 <= c <= 10:
                            act.wait_ge(wm_used, i * 48 + (GATE_CREDIT + 4 * c))
                            wm_load(act, c + 1, i)
                    if mod:
                        act.wait_ge(mod_rowed, i * 6 + 6)
                        for j in range(2):
                            act.dma_start(mods[j:j + 1, bass.ds(i * 3 * NC, 3 * NC)],
                                          mod_row[j][:].rearrange("o a n -> o (a n)")).then_inc(mod_stored, 16)
                        act.wait_ge(mod_stored, i * 32 + 32)

                peel = s0 == SLAB_MLP2
                with act.Fori(0, NCH - peel) as i:
                    chunk(i)
                if peel:
                    chunk(NCH - 1, True)
                tally.up(hid_hi, 8 * NCH)

            def wm_load(eng, u, i):
                src = t["w_mod"].rearrange("(u k p) n -> u p k n", k=UK, p=P)[
                    u % 4, :, :, bass.ds(i * 3 * NC + (u // 4) * NC, NC)]
                eng.dma_start(wm[u % 2][:], src).then_inc(wm_loaded[u % 2], 16)

            mlp(SLAB_MLP1, TILE_MLP1, True)

            act.wait_ge(gemm_free, TILE_IN2)
            act.wait_ge(mod_stored, 32 * NCH)

            def mod(j, k):
                return spread(mods[j, k * D:(k + 1) * D])

            load(mod_scale[:], mod(0, 1), mod_loaded)
            load(mod_gain[:], spread(t["g_pre_mix"]), mod_loaded)
            load(mod_shift[:], mod(0, 0), mod_loaded)
            load(cmod_scale[:], mod(1, 1), cx_loaded)
            load(cmod_shift[:], mod(1, 0), cx_loaded)
            load(cx[:], t["ctx"].rearrange("(m p) d -> p m d", p=P), cx_loaded)
            for m in range(TT):
                stat(STAT_N3 + m, None, x[:, m, :])
                if m:
                    xt_high(NT_3 + m - 1, m - 1, True)
            xt_high(NT_3 + 3, 3, True)
            act.wait_ge(cx_loaded, 48)
            for m in range(CT):
                stat(STAT_CTX + m, None, cx[:, m, :])
                if m:
                    xt_high(NT_CTX, 0, False, ct_hi)
            for q in range(UQ):
                high_of(SLAB_IN2 + 1, q)
            xt_high(NT_CTX + 1, 1, False, ct_hi)
            act.wait_ge(xr_ready, NT_CTX + CT)
            act.wait_ge(mod_made, 2)
            for b in range(2):
                for h in range(NH):
                    off = RPB_LEN - 1 - (RPAD + h * RPH * RPW + (KH - 1) * RPW - 1 + RUN - 1) + 8 * b
                    act.dma_start(rpb_run[64 * b:64 * b + 64, h, :],
                                  bass.AP(tensor=t["rpb"].tensor, offset=off, ap=[[RPW, GR], [1, 8], [1, RUN]])
                                  ).then_inc(rpb_loaded, 16)
            load(pool_w[:], t["pool_w"].rearrange("g c d -> c g d"), pool_loaded)
            for q in range(UQ):
                act.wait_ge(gemm_done, slab_end(SLAB_IN2 + 1) - 3 + q)
                high_of(SLAB_IN2 + 2, q)
            for q in range(UQ):
                act.wait_ge(gemm_done, slab_end(SLAB_IN2 + 2) - 3 + q)
                high_of(SLAB_IN2 + 3, q)
            for q in range(UQ):
                high_of(SLAB_OUT2, q)
            act.wait_ge(gemm_free, TILE_OUT2)
            load(v_odd[0:64, :, :], v_2[64:P, 0:TT - 1, :], v_shifted)
            load(v_odd[64:P, :, :], v_2[0:64, 1:TT, :], v_shifted)

            turn = TURN2
            t0, e0, d0 = len(TURN1), len(U1), 2 * TT
            for i, step in enumerate(STEPS2):
                if i < len(U2):
                    k = e0 + i
                    act.wait_ge(max_done, k + 1)
                    if i >= 2:
                        act.wait_ge(turned, t0 + turn[("T", i - 2)] + 1)
                    if i >= 16:
                        act.wait_ge(rden_done, d0 + i // 8 - 1)
                    did(act.activation(prob[i % 2][:], gp[i % 4][:], ACT.Exp, bias=nmax[:, i % 8:i % 8 + 1],
                                       accum_out=den[:, i % 16:i % 16 + 1]), exp_done)
                for what, k in step:
                    if what == "M":
                        w = turn[("M", k, 0)]
                        act.wait_ge(turned, t0 + w + 1)
                        did(act.activation(grid_cols(xt_hi, k), grid_bank(aux[w % 2]), ACT.Copy), turn_hi)

            load(mix_gate[:], mod(0, 2), tail_loaded)
            load(mix_gain[:], spread(t["g_post_mix"]), tail_loaded)
            load(mlp_scale[:], mod(0, 4), tail_loaded)
            load(mlp_shift[:], mod(0, 3), tail_loaded)
            load(mlp_gain2[:], spread(t["g_pre_mlp"]), tail_loaded)
            for j in range(N_OUT):
                for m in range(TT):
                    g = TILE_OUT2 + 4 * j + m
                    if j:
                        stat(STAT_TAIL + 2 * m, (gemm_free, g + 1), sub[:, m, :])
                        stat(STAT_TAIL + 2 * m + 1, (tail_step, 2 * (m + 1)), x[:, m, :])
                        if m:
                            xt_high(NT_4 + m - 1, m - 1)
                    else:
                        act.wait_ge(gemm_done, g + 1)
                    high_of(SLAB_OUT2 + j + 1, m)
            xt_high(NT_4 + 3, 3)
            load(fin_gate[:], mod(0, 5), fin_loaded)
            load(fin_gain[:], spread(t["g_post_mlp"]), fin_loaded)
            mlp(SLAB_MLP2, TILE_MLP2, False)
            act.wait_ge(gemm_free, slab_end(SLABS - 1))
            for m in range(TT):
                stat(STAT_FIN + m, None, sub[:, m, :])

        @block_fn(nc, ctx, "tensor")
        def _(pe):
            def product(g, bank, lhs, rhs, n, wait_free=True, reg=None):
                if wait_free:
                    pe.wait_ge(gemm_free, g - 3 if reg is None else reg * 16 + (g - 3))
                for k in range(KT):
                    (lh, ll), (rh, rl) = lhs(k), rhs(k)
                    pe.matmul(bank[:, 0:n], lh, rh, start=(k == 0), stop=False)
                    pe.matmul(bank[:, 0:n], lh, rl, start=False, stop=False)
                    mm = pe.matmul(bank[:, 0:n], ll, rh, start=False, stop=(k == KT - 1))
                mm.then_inc(gemm_done, 1)

            def tokens(hi, lo, m):
                return lambda k: (hi[:, k, m * P:(m + 1) * P], lo[:, k, m * P:(m + 1) * P])

            def all_tokens(hi, lo, n=S):
                return lambda k: (hi[:, k, 0:n], lo[:, k, 0:n])

            def w_cols(s, n=NC, c0=0):
                return lambda k: (w_hi[s % 2][:, k, c0:c0 + n], w_lo[s % 2][:, k, c0:c0 + n])

            def turn_rows(n, permute=False, grid=False):
                pe.wait_ge(xr_ready, n + 1)
                for half in range(2):
                    a = 2 * n + half
                    if a >= 4:
                        pe.wait_ge(xt_lo_done, a - 3)
                    for j in range(4):
                        src = xr[n % 2][:, (4 * half + j) * P:(4 * half + j + 1) * P]
                        dst = aux[a % 4][:, j * P:(j + 1) * P]
                        idn = ident[:]
                        if permute:
                            dst = dst.rearrange("p (b r c) -> p r b c", r=2, c=8)
                        mm = pe.transpose(dst, src, idn)
                    mm.then_inc(xr_turned, 1)

            pe.wait_ge(ident_loaded, 16)
            for m in range(TT):
                turn_rows(NT_1 + m)

            def split_ready(s):
                pe.wait_ge(unit_split, 4 * (s + 1))

            def turn_heads(u):
                pe.wait_ge(qn_ready, u + 1)
                if u >= 4:
                    pe.wait_ge(qk_stored, u - 3)
                pairs = 2 if u // 4 == 1 else 4
                for j in range(pairs):
                    mm = pe.transpose(aux[u % 4][:, j * P:(j + 1) * P], qn[u % 2][:, j * P:(j + 1) * P], ident[:])
                mm.then_inc(qn_turned, 1)

            for g in range(4 * N_IN1):
                s, m = g // 4, g % 4
                if m == 0:
                    split_ready(s)
                if g < 4:
                    pe.wait_ge(xt_lo_done, 2 * (NT_1 + m + 1))
                product(g, gp[g % 4], tokens(xt_hi, xt_lo, m), w_cols(s, KV_W if s == 1 else NC),
                        KV_W if s == 1 else NC, wait_free=g >= 4)
                if 1 <= g <= 16:
                    if g == 5:
                        pe.wait_ge(xt_lo_done, 2 * TT)
                    turn_heads(g - 1)
                if g == 8:
                    pe.wait_ge(f_copied, TT)
                    pe.wait_ge(qk_stored, 8)
                    for k in range(TT):
                        mm = pe.transpose(aux[3][0:NH, k * P:(k + 1) * P], flog[:, k, :], ident[:])
                    mm.then_inc(f_turned, 1)
                if g == 11:
                    pe.wait_ge(f_step, 1)

            pe.wait_ge(gemm_free, 4 * N_IN1)
            pe.wait_ge(qk_stored, 16)
            pe.wait_ge(c_ready, 1)
            pe.wait_ge(negsel_ready, 1)
            pe.wait_ge(ones_ready, 1)
            pe.wait_ge(vec_loaded, 16 * 9)
            pe.wait_ge(alibi_loaded, 16)
            for i, step in enumerate(STEPS1):
                if i < len(U1):
                    n, kind, h = U1[i]
                    o = HD * (h % 2)
                    rows = slice(o, o + HD)
                    bank = gp[i % 4]
                    if i >= 4:
                        pe.wait_ge(exp_done, i - 3)
                    if kind == 0:
                        lo = 0 if n else P
                        swap = 0 if (h // 4) == (h % 2) else 1
                        pe.matmul(bank[:, 256:257], ones_row[:], sink[0:1, h:h + 1], start=True, stop=True)
                        pe.matmul(bank[:, lo:256], q_a[rows, h // 2, n * P:(n + 1) * P],
                                  k_a[rows, swap, (n - 1) * P + lo:(n + 1) * P], start=True, stop=False)
                        mm = pe.matmul(bank[:, lo:256], identb[:], alibi[:, h, lo:256], start=False, stop=True)
                    else:
                        w = (n + 1) * P
                        pe.matmul(bank[:, 0:w], q_b[rows, h // 2, n * P:(n + 1) * P], k_b[rows, h // 2, 0:w],
                                  start=True, stop=False)
                        pe.matmul(bank[:, 0:w], negsel[:, h, :], c_hi[:, 0:w], start=False, stop=False)
                        pe.matmul(bank[:, 0:w], negsel[:, h, :], c_lo[:, 0:w], start=False, stop=False)
                        mm = pe.matmul(bank[:, w - P:w], identb[:], causal[:], start=False, stop=True)
                    mm.then_inc(score_done, 1)
                for what, k in step:
                    if what == "M":
                        pe.wait_ge(heads_out, 2 * (k + 1))
                        for half in range(2):
                            w = TURN1[("M", k, half)]
                            pe.wait_ge(turn_read, w - 1)
                            for j in range(4):
                                mm = pe.transpose(aux[w % 2][:, j * P:(j + 1) * P],
                                                  mixed[:, k, (4 * half + j) * P:(4 * half + j + 1) * P], ident[:])
                            mm.then_inc(turned, 1)
                        continue
                    n, kind, h = U1[k]
                    blocks = score_blocks(n, kind)
                    if what == "T":
                        w = TURN1[("T", k)]
                        pe.wait_ge(exp_done, k + 1)
                        if w >= 2:
                            pe.wait_ge(turn_read, w - 1)
                        for b in blocks:
                            mm = pe.transpose(aux[w % 2][:, b * P:(b + 1) * P],
                                              prob[k % 2][:, b * P:(b + 1) * P], ident[:])
                        mm.then_inc(turned, 1)
                    else:
                        pe.wait_ge(turn_read, TURN1[("T", k)] + 1)
                        if k % 8 == 0 and k >= 16:
                            pe.wait_ge(heads_out, k // 8 - 1)
                        for b in blocks:
                            v = (v_a[:, n - 1 + b, (h // 4) * HD:(h // 4 + 1) * HD] if kind == 0
                                 else v_b[:, b, h * HD:(h + 1) * HD])
                            mm = pe.matmul(aux[2 + (k // 8) % 2][:, h * HD:(h + 1) * HD],
                                           prob_t[k % 2][:, b, :], v, start=(b == blocks[0]), stop=(b == blocks[-1]))
                        mm.then_inc(pv_done, 1)

            for j in range(N_OUT):
                split_ready(SLAB_OUT1 + j)
                for m in range(TT):
                    if j == 0:
                        pe.wait_ge(turn_read, TURN1[("M", m, 1)] + 1)
                    g = TILE_OUT1 + 4 * j + m
                    product(g, gp[g % 4], tokens(xt_hi, xt_lo, m), w_cols(SLAB_OUT1 + j), NC)
                    if j and m:
                        if m == 1:
                            pe.wait_ge(heads_out, 2 * TT)
                        turn_rows(NT_2 + m - 1)
            turn_rows(NT_2 + 3)

            def mlp(s0, t0, hid0, mod):
                with pe.Fori(0, NCH) as i:
                    for c in range(8):
                        s = s0 + c // 4
                        if c % 4 == 0:
                            pe.wait_ge(unit_split, i * 16 + 4 * (s + 1))
                        product(t0 + c, gp[(t0 + c) % 4], w_cols(s, P, (c % 4) * P),
                                all_tokens(xt_hi, xt_lo), S, reg=i)
                        if mod and c == 6:
                            sum_mod(0, i)
                    pe.wait_ge(hid_lo, i * 8 + (hid0 + 8))
                    for c in range(8, 16):
                        s = s0 + c // 4
                        if c % 4 == 0:
                            pe.wait_ge(unit_split, i * 16 + 4 * (s + 1))
                        product(t0 + c, gp[(t0 + c) % 4], tokens(ht_hi, ht_lo, c % 4), w_cols(s), NC, reg=i)
                        if mod and c in (10, 14):
                            sum_mod(c // 4 - 1, i)

            def sum_mod(k, i):
                pe.wait_ge(wm_used, i * 48 + (GATE_CREDIT + 16 * (k + 1)))
                if k:
                    pe.wait_ge(mod_rowed, i * 6 + 2 * k)
                for j in range(2):
                    mm = pe.matmul(aux[j][0:1, :], ones_col[:], mod_acc[j][k % 2][:], start=True, stop=True)
                mm.then_inc(mod_summed, 1)

            pe.wait_ge(xt_lo_done, 2 * (NT_2 + TT))
            mlp(SLAB_MLP1, TILE_MLP1, 0, True)

            pe.wait_ge(mod_rowed, 6 * NCH)
            for m in range(TT):
                turn_rows(NT_3 + m, permute=True)
            pe.wait_ge(xt_lo_done, 2 * (NT_3 + TT))
            g = TILE_IN2
            split_ready(SLAB_IN2)
            for j in range(4):
                product(g, gp[g % 4], w_cols(SLAB_IN2, P, j * P), all_tokens(xt_hi, xt_lo), S)
                g += 1
                if j in (1, 2):
                    turn_rows(NT_CTX + j - 1)
            split_ready(SLAB_IN2 + 1)
            for j in range(4):
                product(g, gp[g % 4], w_cols(SLAB_IN2 + 1, P, j * P), all_tokens(xt_hi, xt_lo), S)
                g += 1
            split_ready(SLAB_IN2 + 2)
            for j in range(4):
                product(g, gp[g % 4], w_cols(SLAB_IN2 + 2, P, j * P), all_tokens(xt_hi, xt_lo), S)
                g += 1
            pe.wait_ge(xt_lo_done, 2 * (NT_CTX + CT))
            for j in range(4):
                product(g, gp[g % 4], w_cols(SLAB_IN2 + 2, P, j * P), all_tokens(ct_hi, ct_lo, CTX), CTX)
                g += 1
            split_ready(SLAB_IN2 + 3)
            for m in range(CT):
                product(g, gp[g % 4], tokens(ct_hi, ct_lo, m), w_cols(SLAB_IN2 + 3), NC)
                g += 1
            for m in range(TT):
                product(g, gp[g % 4], tokens(xt_hi, xt_lo, m), w_cols(SLAB_IN2 + 3), NC)
                g += 1

            pe.wait_ge(pool_done, 4)
            pe.wait_ge(pool_loaded, 16)
            for j in range(4):
                mm = pe.matmul(aux[j][:], pool_w[:, j, :], pooled[:, j, :], start=True, stop=True)
                mm.then_inc(pool_mixed, 1)

            pe.wait_ge(gemm_free, TILE_OUT2)
            pe.wait_ge(v_shifted, 32)
            t0, e0, v0, h0 = len(TURN1), len(U1), len(U1), 2 * TT
            for i, step in enumerate(STEPS2):
                if i == 2:
                    pe.wait_ge(pool_step, POOL_STEPS + 8)
                if i < len(U2):
                    n, h = U2[i]
                    o = HD * (h % 2)
                    rows, pair, bank = slice(o, o + HD), h // 2, gp[i % 4]
                    if i >= 4:
                        pe.wait_ge(exp_done, e0 + i - 3)
                    q = q_2[rows, pair, n * P:(n + 1) * P]
                    pe.matmul(bank[:, 0:256], q, k_2[rows, pair, KSTART[n]:KSTART[n] + 256], start=True, stop=False)
                    pe.matmul(bank[:, 0:256], identb[:], window[:, (n + 1) // 2 if n < 3 else 2, :],
                              start=False, stop=True)
                    pe.matmul(bank[:, 256:512], q, k_c[rows, pair, :], start=True, stop=True).then_inc(score_done, 1)
                for what, k in step:
                    if what == "M":
                        pe.wait_ge(heads_out, h0 + k + 1)
                        w = TURN2[("M", k, 0)]
                        pe.wait_ge(turn_read, t0 + w - 1)
                        for j in range(4):
                            dst = aux[w % 2][:, j * P:(j + 1) * P].rearrange("p (r b c) -> p b r c", b=2, c=8)
                            mm = pe.transpose(dst, attn_2[k % 2][:, j * P:(j + 1) * P], ident[:])
                        mm.then_inc(turned, 1)
                        continue
                    n, h = U2[k]
                    if what == "T":
                        w = TURN2[("T", k)]
                        pe.wait_ge(exp_done, e0 + k + 1)
                        if w >= 2:
                            pe.wait_ge(turn_read, t0 + w - 1)
                        for b in range(4):
                            mm = pe.transpose(aux[w % 2][:, b * P:(b + 1) * P],
                                              prob[k % 2][:, b * P:(b + 1) * P], ident[:])
                        mm.then_inc(turned, 1)
                    else:
                        pe.wait_ge(turn_read, t0 + TURN2[("T", k)] + 1)
                        if k % 8 == 0 and k >= 16:
                            pe.wait_ge(heads_out, h0 + k // 8 - 1)
                        cols = slice(h * HD, (h + 1) * HD)
                        for b in range(4):
                            if b >= 2:
                                v = v_c[:, b - 2, cols]
                            elif KSTART[n] % P == 0:
                                v = v_2[:, KSTART[n] // P + b, cols]
                            else:
                                v = v_odd[:, KSTART[n] // P + b, cols]
                            mm = pe.matmul(aux[2 + (k // 8) % 2][:, cols], prob_t[k % 2][:, b, :], v,
                                           start=(b == 0), stop=(b == 3))
                        mm.then_inc(pv_done, 1)

            for j in range(N_OUT):
                split_ready(SLAB_OUT2 + j)
                for m in range(TT):
                    if j == 0 and m == 0:
                        pe.wait_ge(turn_read, t0 + TURN2[("M", TT - 1, 0)] + 1)
                    g = TILE_OUT2 + 4 * j + m
                    product(g, gp[g % 4], tokens(xt_hi, xt_lo, m), w_cols(SLAB_OUT2 + j), NC)
                    if j and m:
                        turn_rows(NT_4 + m - 1)
            turn_rows(NT_4 + 3)
            pe.wait_ge(xt_lo_done, 2 * (NT_4 + TT))
            mlp(SLAB_MLP2, TILE_MLP2, 8 * NCH, False)

        @block_fn(nc, ctx, "vector")
        def _(dve):
            tally = Tally()

            def did(ins, s):
                ins.then_inc(s, 1)
                dve.wait_ge(s, tally.up(s))

            dve.memset(ones_col[:], 1.0)
            did(dve.memset(ones_row[:], 1.0), ones_ready)

            def refine(ms, rs0, tmp, s):
                did(dve.tensor_tensor(tmp, ms, rs0, ALU.mult), s)
                did(dve.tensor_tensor(tmp, tmp, rs0, ALU.mult), s)
                did(dve.tensor_scalar(tmp, tmp, -0.5, 1.5, ALU.mult, ALU.add), s)
                did(dve.tensor_tensor(rs0, rs0, tmp, ALU.mult), s)

            def stat(k, width=D):
                dve.wait_ge(ssq_done, k + 1)
                did(dve.tensor_scalar(st[:, 1, k:k + 1], st[:, 0, k:k + 1], 1.0 / width, EPS, ALU.mult, ALU.add),
                    ms_done)
                dve.wait_ge(rs0_done, k + 1)
                refine(st[:, 1, k:k + 1], st[:, 3, k:k + 1], st[:, 2, k:k + 1], rs_done)

            def scaled(n, k, src, gain, shift=None):
                if n >= 2:
                    dve.wait_ge(xr_turned, 2 * (n - 1))
                ins = dve.scalar_tensor_tensor(xr[n % 2][:], src, st[:, 3, k:k + 1], gain, ALU.mult, ALU.mult)
                if shift is None:
                    did(ins, xr_ready)
                else:
                    did(ins, xr_step)
                    did(dve.tensor_tensor(xr[n % 2][:], xr[n % 2][:], shift, ALU.add), xr_ready)

            def xt_low(n, cols, permute=False, dst=None):
                hi, lo = (xt_hi, xt_lo) if dst is None else dst
                for half in range(2):
                    dve.wait_ge(xt_hi_done, 2 * n + half + 1)
                    did(dve.tensor_tensor(token_cols(lo, half, cols, permute),
                                          bank_cols(aux[(2 * n + half) % 4], permute),
                                          token_cols(hi, half, cols, permute).bitcast(F32), ALU.subtract), xt_lo_done)

            dve.wait_ge(gain1_loaded, 16)
            for m in range(TT):
                stat(STAT_N1 + m)
                scaled(NT_1 + m, STAT_N1 + m, x[:, m, :], gain1[:])
                if m:
                    xt_low(NT_1 + m - 1, m - 1)
            xt_low(NT_1 + 3, 3)
            dve.wait_ge(silu_act, 1)
            did(dve.tensor_scalar(ctmp[:], ctmp[:], 1.0, None, ALU.add), silu_step)
            did(dve.reciprocal(csil[:], ctmp[:]), silu_step)
            did(dve.tensor_tensor(csil[:], csil[:], cvec[:], ALU.mult), silu_step)
            dve.wait_ge(heads_loaded, 16 * 8)
            did(dve.tensor_scalar(gains[:, 0:1], gains[:, 0:1], QSCALE, None, ALU.mult), silu_step)
            did(dve.tensor_scalar(gains[:, 2:3], gains[:, 2:3], QSCALE, None, ALU.mult), silu_step)

            for g in range(4 * N_IN1):
                s, m = g // 4, g % 4
                bank = gp[g % 4]
                dve.wait_ge(gemm_done, g + 1)
                if g >= 16:
                    did(dve.tensor_copy(v_b[:, m, :], bank[:]), gemm_free)
                    continue
                heads = 2 if s == 1 else NH
                dve.wait_ge(hsq_done, g + 1)
                did(dve.tensor_reduce(hst[:, 0, 0:heads], qsq[g % 2][:, 0:heads * HD].rearrange(
                    "p (h d) -> p h d", d=HD), AXX, ALU.add), rs_done)
                did(dve.tensor_scalar(hst[:, 1, 0:heads], hst[:, 0, 0:heads], 1.0 / HD, EPS, ALU.mult, ALU.add),
                    hms_done)
                dve.wait_ge(hrs0_done, g + 1)
                refine(hst[:, 1, 0:heads], hst[:, 3, 0:heads], hst[:, 2, 0:heads], hrs_done)
                if g >= 2:
                    dve.wait_ge(qn_turned, g - 1)
                if s == 1:
                    did(dve.tensor_copy(v_a[:, m, :], bank[:, P:2 * P]), v_copied)
                    did(dve.tensor_copy(flog[:, m, :], bank[:, 256:KV_W]), f_copied)
                    for j, col in ((0, 0), (1, HD), (1, P), (0, P + HD)):
                        did(dve.tensor_scalar(qn[g % 2][:, col:col + HD], bank[:, j * HD:(j + 1) * HD],
                                              hst[:, 3, j:j + 1], None, ALU.mult), v_copied)
                    did(dve.tensor_copy(hst[:, 0, 0:1], hst[:, 3, 0:1]), gemm_free)
                    did(dve.tensor_copy(hst[:, 0, 0:1], hst[:, 3, 0:1]), qn_ready)
                else:
                    did(dve.tensor_tensor(qn[g % 2][:].rearrange("p (h d) -> p h d", d=HD),
                                          bank[:].rearrange("p (h d) -> p h d", d=HD),
                                          hst[:, 3, :].unsqueeze(2).broadcast_to([P, NH, HD]), ALU.mult), gemm_free)
                    did(dve.tensor_copy(hst[:, 0, 0:1], hst[:, 3, 0:1]), qn_ready)
                if g == 9:
                    dve.wait_ge(f_turned, 1)
                    dve.wait_ge(vec_loaded, 16 * 9)
                    dve.wait_ge(negsel_ready, 1)
                    did(dve.tensor_scalar(frow[:, 0, :], aux[3][0:NH, :], b_f[:], None, ALU.add), f_step)
                    did(dve.tensor_scalar(frow[:, 1, :], frow[:, 0, :], -1.0, None, ALU.mult), f_step)
                    did(dve.tensor_tensor(frow[:, 2, :], frow[:, 0, :], frow[:, 1, :], ALU.max), f_step)
                if g == 10:
                    dve.wait_ge(f_act, 1)
                    did(dve.tensor_scalar(frow[:, 3, :], frow[:, 3, :], 1.0, None, ALU.add), f_step)
                    dve.wait_ge(f_act, 2)
                    did(dve.scalar_tensor_tensor(frow[:, 4, :], frow[:, 0, :], 0.0, frow[:, 3, :],
                                                 ALU.min, ALU.subtract), f_step)
                    did(dve.memset(frow[:, 1, :], 1.0), f_step)
                    did(dve.tensor_tensor_scan(frow[:, 5, :], frow[:, 1, :], frow[:, 4, :], 0.0,
                                               ALU.mult, ALU.add), f_step)
            dve.wait_ge(c_hi_done, 1)
            did(dve.tensor_tensor(c_lo[:], frow[:, 5, :], c_hi[:].bitcast(F32), ALU.subtract), c_ready)

            def copy_turn(k, w, first, n_blocks, t0):
                dve.wait_ge(turned, t0 + w + 1)
                did(dve.tensor_copy(prob_t[k % 2][:, first:first + n_blocks, :],
                                    aux[w % 2][:, first * P:(first + n_blocks) * P].rearrange(
                                        "p (b s) -> p b s", b=n_blocks)), turn_read)

            def heads_tile(b, v0, e0, dst):
                dve.wait_ge(exp_done, e0 + 8 * b + 8)
                cols = slice(8 * (b % 2), 8 * (b % 2) + 8)
                did(dve.reciprocal(rden[:, cols], den[:, cols]), rden_done)
                dve.wait_ge(pv_done, v0 + 8 * b + 8)
                did(dve.tensor_tensor(dst.rearrange("p (h d) -> p h d", d=HD),
                                      aux[2 + b % 2][:].rearrange("p (h d) -> p h d", d=HD),
                                      rden[:, cols].unsqueeze(2).broadcast_to([P, NH, HD]), ALU.mult), heads_out)

            for i, step in enumerate(STEPS1):
                if i < len(U1):
                    n, kind, h = U1[i]
                    lo, hi = score_cols(n, kind)
                    dve.wait_ge(score_done, i + 1)
                    if i >= 8:
                        dve.wait_ge(exp_done, i - 7)
                    did(dve.tensor_reduce(nmax[:, i % 8:i % 8 + 1], gp[i % 4][:, lo:hi], AXX, ALU.max, negate=True),
                        max_done)
                for what, k in step:
                    if what == "T":
                        n, kind, h = U1[k]
                        blocks = score_blocks(n, kind)
                        if k >= 2:
                            dve.wait_ge(pv_done, k - 1)
                        copy_turn(k, TURN1[("T", k)], blocks[0], len(blocks), 0)
                    elif what == "V" and k % 8 == 7:
                        n, kind, h = U1[k]
                        heads_tile(k // 8, 0, 0, mixed[:, n, kind * S:(kind + 1) * S])
                    elif what == "M":
                        for half in range(2):
                            w = TURN1[("M", k, half)]
                            dve.wait_ge(turn_hi, 2 * k + half + 1)
                            hi_cols = xt_hi[:, 4 * half:4 * half + 4, k * P:(k + 1) * P]
                            did(dve.tensor_tensor(xt_lo[:, 4 * half:4 * half + 4, k * P:(k + 1) * P],
                                                  aux[w % 2][:].rearrange("p (k s) -> p k s", k=4),
                                                  hi_cols.bitcast(F32), ALU.subtract), turn_read)

            for j in range(N_OUT):
                for m in range(TT):
                    g = TILE_OUT1 + 4 * j + m
                    dve.wait_ge(gemm_done, g + 1)
                    cols = x[:, m, j * NC:(j + 1) * NC]
                    did(dve.tensor_tensor(cols, cols, gp[g % 4][:], ALU.add), gemm_free)
                    if j:
                        if m == 0:
                            dve.wait_ge(gain2_loaded, 16)
                        stat(STAT_N2 + m)
                        scaled(NT_2 + m, STAT_N2 + m, x[:, m, :], gain2[:])
                        if m:
                            xt_low(NT_2 + m - 1, m - 1)
            xt_low(NT_2 + 3, 3)

            def mlp(t0, acc, mod):
                l0 = tally.n.get(hid_lo.name, 0)

                def low(c, i):
                    dve.wait_ge(hid_hi, i * 8 + (l0 + c + 1))
                    dve.tensor_tensor(ht_lo[:, c, :], hid[c % 2][:], ht_hi[:, c, :].bitcast(F32),
                                      ALU.subtract).then_inc(hid_lo, 1)

                with dve.Fori(0, NCH) as i:
                    for c in range(16):
                        g = t0 + c
                        bank = gp[g % 4]
                        dve.wait_ge(gemm_done, i * 16 + (g + 1))
                        if c < 8:
                            if c >= 2:
                                dve.wait_ge(hid_lo, i * 8 + (l0 + c - 1))
                            dve.tensor_scalar(hid[c % 2][:], bank[:], 0.0, None, ALU.max).then_inc(gemm_free, 1)
                            dve.wait_ge(gemm_free, i * 16 + (g + 1))
                            dve.tensor_tensor(hid[c % 2][:], hid[c % 2][:], hid[c % 2][:], ALU.mult
                                              ).then_inc(hid_ready, 1)
                            if c:
                                low(c - 1, i)
                            if c == 7:
                                low(c, i)
                        else:
                            if c == 8:
                                dve.wait_ge(hid_lo, i * 8 + (l0 + 8))
                            cols = acc[:, c % 4, (c // 4 - 2) * NC:(c // 4 - 1) * NC]
                            dve.tensor_tensor(cols, cols, bank[:], ALU.add).then_inc(gemm_free, 1)
                        if mod and c < 12:
                            modulate(c, i)
                        if mod and c in (7, 11, 15):
                            mod_rows(c // 4 - 1, i)
                    if mod:
                        dve.wait_ge(mod_stored, i * 32 + 32)
                tally.up(hid_lo, 8 * NCH)
                tally.up(gemm_free, 16 * NCH)
                dve.wait_ge(gemm_free, t0 + 16 * NCH)

            def modulate(u, i):
                k = u // 4
                dve.wait_ge(wm_loaded[u % 2], i * 96 + 16 * (u // 2 + 1))
                for e in range(4):
                    row, j = e // 2, e % 2
                    kt = (u % 4) * UK + row
                    acc = mod_acc[j][k % 2][:]
                    w = wm[u % 2][:, row, :]
                    if 4 * u + e >= 2:
                        dve.wait_ge(wm_used, i * 48 + (GATE_CREDIT + 4 * u + e - 1))
                    if kt == 0:
                        ins = dve.tensor_scalar(acc, w, csil[:, j, kt:kt + 1], None, ALU.mult)
                    else:
                        ins = dve.scalar_tensor_tensor(acc, w, csil[:, j, kt:kt + 1], acc, ALU.mult, ALU.add)
                    ins.then_inc(wm_used, 1)

            def mod_rows(k, i):
                if k == 0:
                    dve.wait_ge(b_loaded, i * 16 + 16)
                dve.wait_ge(mod_summed, i * 3 + (k + 1))
                for j in (1, 0):
                    if j == 0:
                        dve.wait_ge(mod_rowed, i * 6 + (2 * k + 1))
                    dve.tensor_tensor(mod_row[j][:, k, :], aux[j][0:1, :], b_row[:, k, :], ALU.add
                                      ).then_inc(mod_rowed, 1)

            did(dve.tensor_copy(ctmp[:, 0, :], csil[:, 0, :]), wm_used)
            mlp(TILE_MLP1, x, True)

            dve.wait_ge(mod_loaded, 48)
            did(dve.scalar_tensor_tensor(mod_scale[:], mod_scale[:], 1.0, mod_gain[:], ALU.add, ALU.mult), mod_made)
            for m in range(TT):
                stat(STAT_N3 + m)
                scaled(NT_3 + m, STAT_N3 + m, x[:, m, :], mod_scale[:], mod_shift[:])
                if m:
                    xt_low(NT_3 + m - 1, m - 1, True)
            xt_low(NT_3 + 3, 3, True)
            dve.wait_ge(cx_loaded, 48)
            did(dve.scalar_tensor_tensor(cmod_scale[:], cmod_scale[:], 1.0, mod_gain[:], ALU.add, ALU.mult), mod_made)
            for m in range(CT):
                stat(STAT_CTX + m)
                scaled(NT_CTX + m, STAT_CTX + m, cx[:, m, :], cmod_scale[:], cmod_shift[:])
                if m:
                    xt_low(NT_CTX, 0, False, (ct_hi, ct_lo))
            xt_low(NT_CTX + 1, 1, False, (ct_hi, ct_lo))

            g = TILE_IN2
            did(dve.memset(upad[:], 0.0), pool_step)
            for j in range(4):
                win = 2 ** (j + 1)
                dve.wait_ge(gemm_done, g + 1)
                grid = upad[:, 8:8 + S].rearrange("p (r b c) -> p b r c", r=GR, c=8)
                did(dve.tensor_copy(grid, gp[g % 4][:].rearrange("p (b r c) -> p b r c", r=GR, c=8)), gemm_free)
                src, width = upad, 528
                for e in range(j + 1):
                    width -= 2 ** e
                    did(dve.tensor_tensor(wsum[e % 2][:, 0:width], src[:, 0:width],
                                          src[:, 2 ** e:2 ** e + width], ALU.add), pool_step)
                    src = wsum[e % 2]
                first = 8 - win // 2
                left, right = src[:, first:first + 8], src[:, first + S - 8:first + S]
                dve.wait_ge(vec_loaded, 16 * 9)
                did(dve.tensor_tensor(left, left, edge[:, j, 0:8], ALU.mult), pool_step)
                did(dve.tensor_tensor(right, right, edge[:, j, 8:16], ALU.mult), pool_step)
                did(dve.scalar_tensor_tensor(pooled[:, j, :], src[:, first:first + S], 1.0 / win,
                                             upad[:, 8:8 + S], ALU.mult, ALU.subtract), pool_done)
                g += 1
            assert tally.n[pool_step.name] == POOL_STEPS
            for j in range(4):
                dve.wait_ge(gemm_done, g + 1)
                did(dve.tensor_scalar(q_2[:, j, :], gp[g % 4][:], QSCALE, None, ALU.mult), gemm_free)
                g += 1
            for j in range(4):
                dve.wait_ge(gemm_done, g + 1)
                did(dve.tensor_copy(k_2[:, j, :], gp[g % 4][:]), gemm_free)
                g += 1
            for j in range(4):
                dve.wait_ge(gemm_done, g + 1)
                did(dve.tensor_copy(k_c[:, j, :], gp[g % 4][:, 0:CTX]), gemm_free)
                g += 1
            for m in range(CT):
                dve.wait_ge(gemm_done, g + 1)
                did(dve.tensor_copy(v_c[:, m, :], gp[g % 4][:]), gemm_free)
                g += 1
            for m in range(TT):
                dve.wait_ge(gemm_done, g + 1)
                did(dve.tensor_copy(v_2[:, m, :], gp[g % 4][:]), gemm_free)
                g += 1
            for j in range(4):
                dve.wait_ge(pool_mixed, j + 1)
                did(dve.tensor_scalar(xt_hi[:, j, :], aux[j][:], pscale[:, j:j + 1], None, ALU.mult), pool_step)
                did(dve.scalar_tensor_tensor(xt_lo[:, j, :], aux[j][:], pscale[:, j:j + 1],
                                             xt_hi[:, j, :].bitcast(F32), ALU.mult, ALU.subtract), pool_step)

            dve.wait_ge(rpb_loaded, 16 * 2 * NH)
            t0, e0, v0 = len(TURN1), len(U1), len(U1)
            for i, step in enumerate(STEPS2):
                if i < len(U2):
                    n, h = U2[i]
                    bank = gp[i % 4]
                    dve.wait_ge(score_done, e0 + i + 1)
                    if i >= 8:
                        dve.wait_ge(exp_done, e0 + i - 7)
                    local = bank[:, 0:256].rearrange("p (b r c) -> p b r c", r=KH, c=8)
                    run = rpb_run[:, h, RUN - 1 - KSHIFT[n]:RUN - KSHIFT[n]]
                    run = bass.AP(tensor=run.tensor, offset=run.offset,
                                  ap=[list(run.ap[0]), [-8, 4], [-RPW, KH], [-1, 8]])
                    did(dve.tensor_tensor(local, local, run, ALU.add), bias_added)
                    did(dve.tensor_reduce(nmax[:, i % 8:i % 8 + 1], bank[:], AXX, ALU.max, negate=True), max_done)
                for what, k in step:
                    if what == "T":
                        if k >= 2:
                            dve.wait_ge(pv_done, v0 + k - 1)
                        copy_turn(k, TURN2[("T", k)], 0, 4, t0)
                    elif what == "V" and k % 8 == 7:
                        if k >= 16:
                            dve.wait_ge(turned, t0 + TURN2[("M", k // 8 - 2, 0)] + 1)
                        heads_tile(k // 8, v0, e0, attn_2[(k // 8) % 2][:])
                    elif what == "M":
                        w = TURN2[("M", k, 0)]
                        dve.wait_ge(turn_hi, 2 * TT + k + 1)
                        did(dve.tensor_tensor(grid_cols(xt_lo, k), grid_bank(aux[w % 2]),
                                              grid_cols(xt_hi, k).bitcast(F32), ALU.subtract), turn_read)

            dve.wait_ge(tail_loaded, 16 * 5)
            for j in range(N_OUT):
                for m in range(TT):
                    g = TILE_OUT2 + 4 * j + m
                    dve.wait_ge(gemm_done, g + 1)
                    did(dve.tensor_copy(sub[:, m, j * NC:(j + 1) * NC], gp[g % 4][:]), gemm_free)
                    if j == 0 and m == 0:
                        did(dve.tensor_tensor(mix_gate[:], mix_gate[:], mix_gain[:], ALU.mult), mod_made)
                        did(dve.scalar_tensor_tensor(mlp_scale[:], mlp_scale[:], 1.0, mlp_gain2[:],
                                                     ALU.add, ALU.mult), mod_made)
                    if j:
                        stat(STAT_TAIL + 2 * m)
                        k = STAT_TAIL + 2 * m
                        did(dve.scalar_tensor_tensor(sub[:, m, :], sub[:, m, :], st[:, 3, k:k + 1], mix_gate[:],
                                                     ALU.mult, ALU.mult), tail_step)
                        did(dve.tensor_tensor(x[:, m, :], x[:, m, :], sub[:, m, :], ALU.add), tail_step)
                        stat(k + 1)
                        scaled(NT_4 + m, k + 1, x[:, m, :], mlp_scale[:], mlp_shift[:])
                        did(dve.memset(sub[:, m, :], 0.0), xr_step)
                        if m:
                            xt_low(NT_4 + m - 1, m - 1)
            xt_low(NT_4 + 3, 3)
            mlp(TILE_MLP2, sub, False)
            dve.wait_ge(fin_loaded, 32)
            did(dve.tensor_tensor(fin_gate[:], fin_gate[:], fin_gain[:], ALU.mult), mod_made)
            for m in range(TT):
                k = STAT_FIN + m
                stat(k)
                did(dve.scalar_tensor_tensor(sub[:, m, :], sub[:, m, :], st[:, 3, k:k + 1], fin_gate[:],
                                             ALU.mult, ALU.mult), fin_step)
                did(dve.tensor_tensor(x[:, m, :], x[:, m, :], sub[:, m, :], ALU.add), fin_step)


POOL_STEPS = 1 + (1 + 2 + 3 + 4) + 2 * 4


def score_cols(n, kind):
    return ((0 if n else P), 257) if kind == 0 else (0, (n + 1) * P)


def score_blocks(n, kind):
    return ([0, 1] if n else [1]) if kind == 0 else list(range(n + 1))


def token_cols(dst, half, m, permute):
    if not permute:
        return dst[:, 4 * half:4 * half + 4, m * P:(m + 1) * P]
    return dst[:, 4 * half:4 * half + 4, :].rearrange("p k (b s) -> p k b s", s=64)[:, :, :, 16 * m:16 * m + 16]


def bank_cols(bank, permute):
    if not permute:
        return bank[:].rearrange("p (k s) -> p k s", k=4)
    return bank[:].rearrange("p (k b s) -> p k b s", k=4, s=16)


def grid_cols(dst, n):
    return dst[:, 4:8, :].rearrange("p k (r s) -> p k r s", s=GW)[:, :, :, 16 * n:16 * n + 16]


def grid_bank(bank):
    return bank[:].rearrange("p (k r s) -> p k r s", k=4, s=16)


_BLOCKS = {}


def block_fn(nc, ctx, engine):
    if id(nc) not in _BLOCKS:
        _BLOCKS[id(nc)] = ctx.enter_context(nc.Block())
    block = _BLOCKS[id(nc)]
    return {"sync": block.sync, "gpsimd": block.gpsimd, "scalar": block.scalar, "tensor": block.tensor,
            "vector": block.vector}[engine]


def constants():
    bf = np.dtype("bfloat16")
    q = np.arange(P)[:, None]
    k = np.arange(256)[None, :]
    dist = q + P - k
    band = (dist >= 0) & (dist < 128)
    alibi = np.stack([np.where(band, -(2.0 ** -(h + 1)) * dist, NEG) for h in range(NH)], axis=1)
    causal = np.where(np.arange(P)[None, :] <= q, 0.0, NEG)
    window = np.zeros((P, 3, 256))
    for v, (n, kc0) in enumerate(((0, 0), (1, 8), (3, 32))):
        for p in range(P):
            qc = 16 * n + 8 * (p // 64) + p % 8
            kc = kc0 + 8 * (np.arange(256) // 64) + np.arange(256) % 8
            first = min(max(qc - KW // 2, 0), GW - KW)
            window[p, v] = np.where((kc >= first) & (kc < first + KW), 0.0, NEG)
    edge = np.ones((4, 16))
    for g in range(4):
        w = 2 ** (g + 1)
        lo, hi = w // 2, w - 1 - w // 2
        for c, tok in enumerate(list(range(8)) + list(range(S - 8, S))):
            edge[g, c] = w / (min(tok + hi + 1, S) - max(tok - lo, 0))
    negsel = np.zeros((NH, NH, P))
    for h in range(NH):
        negsel[h, h] = -1.0
    return {
        "c_ident": np.eye(P, dtype=np.float32),
        "c_identb": np.eye(P).astype(bf),
        "c_alibi": alibi.astype(bf),
        "c_causal": causal.astype(bf),
        "c_window": window.astype(bf),
        "c_edge": np.broadcast_to(edge.astype(np.float32), (P, 4, 16)).copy(),
        "c_negsel": negsel.reshape(NH, NH * P).astype(np.float32),
    }


def kernel(**inputs):
    import concourse.bacc as bacc
    from concourse.bass_utils import run_bass_kernel_spmd

    def f(name, shape=None):
        a = np.ascontiguousarray(inputs[name])
        return a if shape is None else a.reshape(shape)

    def by_partition(name):
        return np.ascontiguousarray(f(name).reshape(-1, P).T)

    rpb = np.zeros(RPB_LEN, np.float32)
    rpb[RPAD:-RPAD] = f("rpb_2").reshape(-1)[::-1]
    arrays = {
        "x": f("x", (S, D)), "attn_norm_g": f("attn_norm_g"), "w_in": f("w_in"), "b_forget": f("b_forget"),
        "q_norm_a": f("q_norm_a"), "k_norm_a": f("k_norm_a"), "sink_logits": f("sink_logits"),
        "q_norm_b": f("q_norm_b"), "k_norm_b": f("k_norm_b"), "w_out": f("w_out"), "mlp_norm_g": f("mlp_norm_g"),
        "w_up": f("w_up"), "w_down": f("w_down"), "c": by_partition("c_2"), "ctx": f("ctx_2", (CTX, D)),
        "c_ctx": by_partition("c_ctx_2"), "w_mod": f("w_mod_2", (D, 6 * D)), "b_mod": f("b_mod_2", (6 * D,)),
        "g_pre_mix": f("g_pre_mix_2", (D,)), "g_post_mix": f("g_post_mix_2", (D,)),
        "g_pre_mlp": f("g_pre_mlp_2", (D,)), "g_post_mlp": f("g_post_mlp_2", (D,)),
        "w_in_2": f("w_in_2", (D, 2048)), "pool_w": f("pool_w_2", (4, P, P)), "pool_scale": by_partition("pool_scale_2"),
        "rpb": rpb, "w_out_2": f("w_out_2", (D, D)), "w_mlp_in_2": f("w_mlp_in_2", (D, DFF)),
        "w_mlp_out_2": f("w_mlp_out_2", (DFF, D)),
    }
    arrays.update(constants())
    nc = bacc.Bacc("TRN2", target_bir_lowering=False, num_devices=1)
    t = {}
    for name, a in arrays.items():
        t[name] = nc.dram_tensor(f"in_{name}", a.shape, mybir.dt.from_np(a.dtype), kind="ExternalInput").ap()
    out = nc.dram_tensor("out", (S, D), F32, kind="ExternalOutput").ap()
    build(nc, t, out)
    r = run_bass_kernel_spmd(nc, [{f"in_{name}": a for name, a in arrays.items()}], core_ids=[0])
    return r.results[0]["out"].reshape(1, S, D)
```

```python
from contextlib import ExitStack

import numpy as np

import concourse.bass as bass
import concourse.mybir as mybir

F32 = mybir.dt.float32
F32R = mybir.dt.float32r
BF16 = mybir.dt.bfloat16
ALU = mybir.AluOpType
ACT = mybir.ActivationFunctionType
AXX = mybir.AxisListType.X

P = 128
D = 1024
S = 512
CTX = 256
DFF = 4096
HD = 64
NH = 8
KT = D // P
TT = S // P
CT = CTX // P
NC = 512
UK = 2
UQ = KT // UK
NCH = DFF // D
EPS = 1e-6
NEG = -1e30
QSCALE = HD ** -0.5
LN_SCALE = 2.0 ** (2 / 3)

GR, GW = 8, 64
KH, KW = 8, 16
RPW = 2 * KW - 1
RPH = 2 * KH - 1
RUN = (KH - 1) * RPW + 32 + 16
CR = 32 + NH
RPAD = 16
RPB_LEN = 2 * RPAD + NH * RPH * RPW
KSTART = (0, 64, 192, 256)
KSHIFT = (16, 8, 8, 0)

IN1_COLS = ((0, 512), (512, 256), (768, 512), (1280, 512), (1792, 512))
KV_W = 264
N_IN1, N_OUT, N_MLP, N_IN2 = 5, 2, 4 * NCH, 4
SLAB_OUT1 = N_IN1
SLAB_MLP1 = SLAB_OUT1 + N_OUT
SLAB_IN2 = SLAB_MLP1 + N_MLP
SLAB_OUT2 = SLAB_IN2 + N_IN2
SLAB_MLP2 = SLAB_OUT2 + N_OUT
SLABS = SLAB_MLP2 + N_MLP

TILE_OUT1 = 4 * N_IN1
TILE_MLP1 = TILE_OUT1 + 2 * TT
TILE_IN2 = TILE_MLP1 + 4 * N_MLP
IN2_TILES = (4, 4, 4 + 4, CT + TT)
TILE_OUT2 = TILE_IN2 + sum(IN2_TILES)
TILE_MLP2 = TILE_OUT2 + 2 * TT


def slab_end(s):
    if s < SLAB_IN2:
        return 4 * (s + 1)
    if s < SLAB_OUT2:
        return TILE_IN2 + sum(IN2_TILES[:s - SLAB_IN2 + 1])
    return TILE_OUT2 + 4 * (s - SLAB_OUT2 + 1)


def freed(g):
    for t0, before in ((TILE_MLP2, 8 * NCH), (TILE_MLP1, 0)):
        if t0 <= g < t0 + 16 * NCH:
            return t0 - before + 8 * ((g - t0) // 16) + max((g - t0) % 16 - 7, 0)
    return g + 1 - (8 * NCH if g >= TILE_MLP1 else 0)


STAT_N1, STAT_N2, STAT_CTX, STAT_N3, STAT_TAIL, STAT_FIN = 0, 4, 8, 10, 14, 22
NT_1, NT_2, NT_CTX, NT_3, NT_4 = 0, 4, 8, 10, 14
MB = 12 * NC // ((NCH - 1) * NC)
MB_UNITS = MB * UQ
EARLY = S // 2

U1 = [(n, kind, h) for n in range(TT) for kind in range(2) for h in range(NH)]
U2 = [(n, h) for n in range(TT) for h in range(NH)]
LAG_T, LAG_V, LAG_M = 2, 3, 4


def attention_order(units, per_tile, halves):
    steps = []
    for i in range(units + LAG_M + 1):
        step = []
        if 0 <= i - LAG_T < units:
            step.append(("T", i - LAG_T))
        if 0 <= i - LAG_V < units:
            step.append(("V", i - LAG_V))
        if i >= per_tile + LAG_M and (i - LAG_M) % per_tile == 0:
            step.append(("M", (i - LAG_M) // per_tile - 1))
        steps.append(step)
    turn = {}
    for step in steps:
        for what, k in step:
            if what == "T":
                turn[what, k] = len(turn)
            elif what == "M":
                for half in range(halves):
                    turn[what, k, half] = len(turn)
    return steps, turn


STEPS1, TURN1 = attention_order(len(U1), 2 * NH, 2)
STEPS2, TURN2 = attention_order(len(U2), NH, 1)


class Tally:

    def __init__(self):
        self.n = {}

    def up(self, sem, k=1):
        self.n[sem.name] = self.n.get(sem.name, 0) + k
        return self.n[sem.name]


def build(nc, t, out):
    ctx = ExitStack()
    with ctx:
        base = (nc.sbuf_base + 63) // 64 * 64
        top = [base]

        def at(name, shape, dtype, offset):
            return nc.alloc_sbuf_tensor_at(name, shape, dtype, offset=offset)

        def place(name, shape, dtype):
            a = top[0]
            size = int(np.prod(shape[1:])) * (2 if dtype == BF16 else 4)
            top[0] = a + (size + 31) // 32 * 32
            return at(name, shape, dtype, a)

        def region(kib):
            a = top[0]
            top[0] = a + kib * 1024
            return a

        K = 1024
        raw = [place(f"w_raw{q}", [P, UK, NC], F32) for q in range(UQ)]
        w_hi = [place(f"w_hi{s}", [P, KT, NC], F32R) for s in range(2)]
        w_lo = [place(f"w_lo{s}", [P, KT, NC], F32R) for s in range(2)]
        xt_hi = place("xt_hi", [P, KT, S], F32R)
        xt_lo = place("xt_lo", [P, KT, S], F32R)
        x = place("x", [P, TT, D], F32)
        H = region(32)
        ht_hi = at("ht_hi", [P, KT, S], F32R, H)
        ht_lo = at("ht_lo", [P, KT, S], F32R, H + 16 * K)
        q_a = at("q_a", [P, 4, S], F32, H)
        q_b = at("q_b", [P, 4, S], F32, H + 8 * K)
        k_b = at("k_b", [P, 4, S], F32, H + 16 * K)
        v_b = at("v_b", [P, TT, S], F32, H + 24 * K)
        pooled = at("pooled", [P, 4, S], F32, H)
        q_2 = at("q_2", [P, 4, S], F32, H + 8 * K)
        k_2 = at("k_2", [P, 4, S], F32, H + 16 * K)
        v_2 = at("v_2", [P, TT, S], F32, H + 24 * K)
        mix_gate = at("mix_gate", [P, D], F32, H)
        mix_gain = at("mix_gain", [P, D], F32, H + 4 * K)
        mlp_scale = at("mlp_scale", [P, D], F32, H + 8 * K)
        mlp_shift = at("mlp_shift", [P, D], F32, H + 12 * K)
        mlp_gain2 = at("mlp_gain2", [P, D], F32, H + 16 * K)
        A = region(16)
        mixed = at("mixed", [P, TT, D], F32, A)
        frow = at("frow", [CR, 6, S], F32, A)
        sel_raw = at("sel_raw", [CR, NH, P], F32, A + 12 * K)
        wm = [at(f"wm{i}", [P, UK, NC], F32, A + 4 * K * i) for i in range(2)]
        mod_acc = [[at(f"mod_acc{i}{j}", [P, NC], F32, A + 8 * K + 4 * K * i + 2 * K * j) for j in range(2)]
                   for i in range(2)]
        ct_hi = at("ct_hi", [P, KT, CTX], F32R, A)
        ct_lo = at("ct_lo", [P, KT, CTX], F32R, A + 8 * K)
        v_odd = at("v_odd", [P, TT - 1, S], F32, A)
        q_pad2 = at("q_pad2", [P, 4, P], F32, A + 10 * K)
        attn_2 = [at(f"attn_2{i}", [P, NC], F32, A + 6 * K + 2 * K * i) for i in range(2)]
        sub = at("sub", [P, TT, D], F32, A)
        T = region(8)
        xr = [at(f"xr{i}", [P, D], F32, T + 4 * K * i) for i in range(2)]
        qn = [at(f"qn{i}", [P, NC], F32, T + 2 * K * i) for i in range(2)]
        qsq = [at(f"qsq{i}", [P, NC], F32, T + 4 * K + 2 * K * i) for i in range(2)]
        prob = [at(f"prob{i}", [P, NC], F32, T + 2 * K * i) for i in range(2)]
        prob_t = [at(f"prob_t{i}", [P, 4, P], F32, T + 4 * K + 2 * K * i) for i in range(2)]
        relu = [at(f"relu{i}", [P, NC], F32, T + 2 * K * i) for i in range(2)]
        hid = [at(f"hid{i}", [P, NC], F32, T + 4 * K + 2 * K * i) for i in range(2)]
        upad = at("upad", [P, 544], F32, T)
        wsum = [at(f"wsum{i}", [P, 544], F32, T + 2176 * (i + 1)) for i in range(2)]
        ident = place("ident", [P, P], F32)
        identb = place("identb", [P, P], BF16)
        J = top[0]
        junk = place("junk", [P, D], BF16)
        v_a = at("v_a", [P, TT, P], F32, J)
        pool_w = at("pool_w", [P, 4, P], F32, J)
        causal = place("causal", [P, P], BF16)
        window = place("window", [P, 3, 256], BF16)
        st = place("st", [P, 4, 32], F32)
        half_sq = place("half_sq", [P, TT], F32)
        hst = place("hst", [P, 4, NH], F32)
        nmax = place("nmax", [P, NH], F32)
        den = place("den", [P, 2 * NH], F32)
        rden = place("rden", [P, 2 * NH], F32)
        gains = place("gains", [P, 4], F32)
        cvec = place("cvec", [P, 2, KT], F32)
        csil = place("csil", [P, 2, KT], F32)
        ctmp = place("ctmp", [P, 2, KT], F32)
        flog = place("flog", [P, TT, NH], F32)
        b_f = place("b_f", [NH, 1], F32)
        sink = place("sink", [1, NH], F32)
        ones_row = place("ones_row", [1, P], F32)
        ones_col = place("ones_col", [P, 1], F32)
        pscale = place("pscale", [P, 4], F32)
        edge = place("edge", [P, 4, 16], F32)
        E = top[0]
        gain1 = at("gain1", [P, D], F32, E)
        alibi = at("alibi", [P, NH, 256], BF16, E)
        k_a = at("k_a", [P, 2, S], F32, E + 4 * K)
        c_parts = at("c_parts", [CR, S], F32R, E + 8 * K)
        q_pad1 = at("q_pad1", [P, 4, P], F32, E + 10 * K)
        negsel = at("negsel", [CR, NH, P], F32R, E + 12 * K)
        gain2 = at("gain2", [P, D], F32, E)
        b_row = at("b_row", [1, MB, NC], F32, E)
        mod_row = [b_row, at("cmod_row", [1, MB, NC], F32, E + 8 * K)]
        mod_gain = at("mod_gain", [P, D], F32, E)
        cmod_scale = at("cmod_scale", [P, D], F32, E + 4 * K)
        cmod_shift = at("cmod_shift", [P, D], F32, E + 8 * K)
        mod_scale = at("mod_scale", [P, D], F32, E + 12 * K)
        mod_shift = at("mod_shift", [P, D], F32, E + 4 * K)
        rpb_run = at("rpb_run", [P, NH, RUN], F32, E)
        k_c = at("k_c", [P, 4, CTX], F32, E + 8512)
        v_c = at("v_c", [P, CT, S], F32, E + 8512 + 4 * K)
        fin_gate = at("fin_gate", [P, D], F32, E)
        fin_gain = at("fin_gain", [P, D], F32, E + 4 * K)
        assert E + 17 * K <= nc.sbuf_usable_end, (E, nc.sbuf_usable_end)

        mods = nc.dram_tensor("mods", (2, 12 * NC), F32, kind="Internal").ap()

        def ps(name):
            return ctx.enter_context(nc.psum_tensor(name, [P, NC], F32))

        gp = [ps(f"gemm{i}") for i in range(4)]
        aux = [ps(f"aux{i}") for i in range(4)]

        sems = {}

        def sem(name):
            sems[name] = ctx.enter_context(nc.semaphore(name))
            return sems[name]

        x_loaded = [sem(f"x_loaded{m}") for m in range(TT)]
        ident_loaded = sem("ident_loaded")
        gain1_loaded, gain2_loaded = sem("gain1_loaded"), sem("gain2_loaded")
        heads_loaded, vec_loaded = sem("heads_loaded"), sem("vec_loaded")
        alibi_loaded, negsel_loaded = sem("alibi_loaded"), sem("negsel_loaded")
        mod_loaded, cmod_loaded, shift_loaded = sem("mod_loaded"), sem("cmod_loaded"), sem("shift_loaded")
        cx_loaded = [sem(f"cx_loaded{m}") for m in range(CT)]
        rpb_loaded, pool_loaded = sem("rpb_loaded"), sem("pool_loaded")
        tail_loaded, fin_loaded = sem("tail_loaded"), sem("fin_loaded")
        v_shifted, out_stored = sem("v_shifted"), sem("out_stored")
        raw_loaded = [sem(f"raw_loaded{q}") for q in range(UQ)]
        hi_split, unit_split = sem("hi_split"), sem("unit_split")
        gemm_done, gemm_free = sem("gemm_done"), sem("gemm_free")
        ones_ready, negsel_ready = sem("ones_ready"), sem("negsel_ready")
        ssq_done, ms_done, ln_done, rs0_done, rs_done = (sem(n) for n in (
            "ssq_done", "ms_done", "ln_done", "rs0_done", "rs_done"))
        xr_step, xr_ready = sem("xr_step"), sem("xr_ready")
        xr_turned, xt_hi_done, xt_lo_done = sem("xr_turned"), sem("xt_hi_done"), sem("xt_lo_done")
        hsq_done, hms_done, hln_done, hrs0_done, hrs_done = (sem(n) for n in (
            "hsq_done", "hms_done", "hln_done", "hrs0_done", "hrs_done"))
        qn_ready, qn_turned, qk_stored = sem("qn_ready"), sem("qn_turned"), sem("qk_stored")
        v_copied, f_copied, f_turned, f_step, f_act = (sem(n) for n in (
            "v_copied", "f_copied", "f_turned", "f_step", "f_act"))
        c_hi_done, c_ready = sem("c_hi_done"), sem("c_ready")
        score_done, bias_added, max_done, exp_done = (sem(n) for n in (
            "score_done", "bias_added", "max_done", "exp_done"))
        turned, turn_read, turn_hi, pv_done, rden_done, heads_out = (sem(n) for n in (
            "turned", "turn_read", "turn_hi", "pv_done", "rden_done", "heads_out"))
        pads_clear, q_padded = sem("pads_clear"), sem("q_padded")
        relu_done, hid_ready, hid_hi, hid_lo = (sem(n) for n in ("relu_done", "hid_ready", "hid_hi", "hid_lo"))
        silu_step, silu_act, wm_used, mod_summed, mod_rowed, mod_stored = (sem(n) for n in (
            "silu_step", "silu_act", "wm_used", "mod_summed", "mod_rowed", "mod_stored"))
        wm_loaded = [sem(f"wm_loaded{i}") for i in range(2)]
        b_loaded = sem("b_loaded")
        pool_step, pool_done, pool_mixed, pool_hi = (sem(n) for n in (
            "pool_step", "pool_done", "pool_mixed", "pool_hi"))
        mod_made, tail_step, fin_step = sem("mod_made"), sem("tail_step"), sem("fin_step")

        GATE_CREDIT = 1

        def perm_in(ap):
            return ap.rearrange("p (r b c) -> p r b c", b=GW // 8, c=8)

        @block_fn(nc, ctx, "sync")
        def _(sp):
            sp.dma_start(ident[:], t["c_ident"]).then_inc(ident_loaded, 16)
            for m in range(TT):
                sp.dma_start(x[:, m, :], t["x"][m * P:(m + 1) * P, :]).then_inc(x_loaded[m], 16)

            def unit(q, src, width, wait):
                if wait is not None:
                    sp.wait_ge(unit_split, wait)
                sp.dma_start(raw[q][:, :, 0:width], src).then_inc(raw_loaded[q], 16)

            def rows(w, r0, q):
                return w[r0 + q * UK * P:r0 + (q + 1) * UK * P, :].rearrange("(k p) n -> p k n", p=P)

            def slab(s, w, c0, width):
                for q in range(UQ):
                    wait = 4 * (s - 1) + q + 1 if s else None
                    unit(q, rows(w, 0, q)[:, :, c0:c0 + width], width, wait)

            for s, (c0, width) in enumerate(IN1_COLS):
                if s == 1:
                    for q in range(UQ):
                        src = rows(t["w_in"], 0, q)
                        sp.wait_ge(unit_split, q + 1)
                        sp.dma_start(raw[q][:, :, 0:256], src[:, :, c0:c0 + 256]).then_inc(raw_loaded[q], 16)
                        sp.dma_start(raw[q][:, :, 256:KV_W], src[:, :, 2304:2312]).then_inc(raw_loaded[q], 16)
                else:
                    slab(s, t["w_in"], c0, width)
            for j in range(N_OUT):
                slab(SLAB_OUT1 + j, t["w_out"], j * NC, NC)

            def mlp(s0, up, down):
                with sp.Fori(0, NCH) as i:
                    for a in range(2):
                        for q in range(UQ):
                            src = rows(up, 0, q)[:, :, bass.ds(i * D + a * NC, NC)]
                            unit(q, src, NC, i * 16 + (4 * (s0 + a - 1) + q + 1))
                    down_r = down.rearrange("(c u k p) n -> c u p k n", c=NCH, k=UK, p=P)
                    for a in range(2):
                        for q in range(UQ):
                            src = down_r[bass.ds(i, 1), q, :, :, a * NC:(a + 1) * NC]
                            src = src.rearrange("o p k n -> (o p) k n")
                            unit(q, src, NC, i * 16 + (4 * (s0 + a + 1) + q + 1))

            mlp(SLAB_MLP1, t["w_up"], t["w_down"])
            for j, c0 in enumerate((0, 512, 1024, 1536)):
                slab(SLAB_IN2 + j, t["w_in_2"], c0, NC)
            for j in range(N_OUT):
                slab(SLAB_OUT2 + j, t["w_out_2"], j * NC, NC)
            mlp(SLAB_MLP2, t["w_mlp_in_2"], t["w_mlp_out_2"])
            for m in range(TT):
                sp.wait_ge(fin_step, 2 * (m + 1))
                sp.dma_start(out[m * P:(m + 1) * P, :], x[:, m, :]).then_inc(out_stored, 16)
            sp.wait_ge(out_stored, 16 * TT)

        @block_fn(nc, ctx, "gpsimd")
        def _(pool):
            def low(s, q, width, wait):
                pool.wait_ge(hi_split, wait)
                ks = slice(UK * q, UK * (q + 1))
                pool.tensor_tensor(w_lo[s % 2][:, ks, 0:width], raw[q][:, :, 0:width],
                                   w_hi[s % 2][:, ks, 0:width].bitcast(F32), ALU.subtract).then_inc(unit_split, 1)

            def lows(first, slabs):
                with pool.Fori(0, slabs // 2) as i:
                    for a in range(2):
                        for q in range(UQ):
                            low(first + a, q, NC, i * 8 + (4 * (first + a) + q + 1))
                if slabs % 2:
                    for q in range(UQ):
                        low(first + slabs - 1, q, NC, 4 * (first + slabs - 1) + q + 1)

            def clear_pads(q_pad, count):
                pool.memset(q_pad[:], 0.0).then_inc(pads_clear, 1)
                pool.wait_ge(pads_clear, count)

            def pad_queries(q_pad, i, i0, q):
                if i >= 4:
                    pool.wait_ge(score_done, i0 + i - 3)
                o = HD * (i % 2)
                pool.tensor_copy(q_pad[o:o + HD, i % 4, :], q).then_inc(q_padded, 1)
                pool.wait_ge(q_padded, i0 + i + 1)

            clear_pads(q_pad1, 1)
            for s in range(N_IN1 + 1):
                for q in range(UQ):
                    low(s, q, KV_W if s == 1 else NC, 4 * s + q + 1)
            pool.wait_ge(qk_stored, 16)
            for i, (n, kind, h) in enumerate(U1):
                o = HD * (h % 2)
                pad_queries(q_pad1, i, 0, (q_b if kind else q_a)[o:o + HD, h // 2, n * P:(n + 1) * P])
            lows(SLAB_OUT1 + 1, SLAB_OUT2 - SLAB_OUT1)
            pool.wait_ge(gemm_done, TILE_OUT2 - TT)
            clear_pads(q_pad2, 2)
            pool.wait_ge(gemm_free, freed(TILE_IN2 + 7))
            for i, (n, h) in enumerate(U2):
                o = HD * (h % 2)
                pad_queries(q_pad2, i, len(U1), q_2[o:o + HD, h // 2, n * P:(n + 1) * P])
            lows(SLAB_OUT2 + 1, SLABS - SLAB_OUT2 - 1)

        @block_fn(nc, ctx, "scalar")
        def _(act):
            tally = Tally()

            def did(ins, s):
                ins.then_inc(s, 1)
                act.wait_ge(s, tally.up(s))

            def load(dst, src, s):
                act.dma_start(dst, src).then_inc(s, 16)

            def spread(v, n=D):
                return v.partition_broadcast(P)

            act.preload_act_table_set("natural_log_exp_and_others")
            load(gain1[:], spread(t["attn_norm_g"]), gain1_loaded)
            load(gains[0:HD, 0:1], t["q_norm_a"].rearrange("(p a) -> p a", a=1), heads_loaded)
            load(gains[HD:P, 0:1], t["q_norm_a"].rearrange("(p a) -> p a", a=1), heads_loaded)
            load(gains[0:HD, 1:2], t["k_norm_a"].rearrange("(p a) -> p a", a=1), heads_loaded)
            load(gains[HD:P, 1:2], t["k_norm_a"].rearrange("(p a) -> p a", a=1), heads_loaded)
            load(gains[0:HD, 2:3], t["q_norm_b"].rearrange("(p a) -> p a", a=1), heads_loaded)
            load(gains[HD:P, 2:3], t["q_norm_b"].rearrange("(p a) -> p a", a=1), heads_loaded)
            load(gains[0:HD, 3:4], t["k_norm_b"].rearrange("(p a) -> p a", a=1), heads_loaded)
            load(gains[HD:P, 3:4], t["k_norm_b"].rearrange("(p a) -> p a", a=1), heads_loaded)
            load(b_f[:], t["b_forget"].rearrange("(p a) -> p a", a=1), vec_loaded)
            load(sink[:], t["sink_logits"].rearrange("(a n) -> a n", a=1), vec_loaded)
            load(cvec[:, 0, :], t["c"], vec_loaded)
            load(cvec[:, 1, :], t["c_ctx"], vec_loaded)
            load(identb[:], t["c_identb"], vec_loaded)
            load(causal[:], t["c_causal"], vec_loaded)
            load(window[:], t["c_window"], vec_loaded)
            load(edge[:], t["c_edge"], vec_loaded)
            load(pscale[:], t["pool_scale"], vec_loaded)
            load(sel_raw[:].rearrange("h g p -> h (g p)"), t["c_negsel"], negsel_loaded)

            def high(s, q, width=NC, loaded=None, free=None):
                act.wait_ge(raw_loaded[q], loaded)
                if free is not None:
                    act.wait_ge(gemm_done, free)
                act.activation(w_hi[s % 2][:, UK * q:UK * (q + 1), 0:width], raw[q][:, :, 0:width],
                               ACT.Copy).then_inc(hi_split, 1)

            def arrived(s):
                return 16 * (s + 1) + (16 if s >= 1 else 0)

            def high_of(s, q):
                high(s, q, KV_W if s == 1 else NC, arrived(s), slab_end(s - 2) if s >= 2 else None)

            def squares(ready, src, dst):
                if ready is not None:
                    act.wait_ge(*ready)
                did(act.activation(junk[:, 0:src.shape[-1]], src, ACT.Square, accum_out=dst), ssq_done)

            def first_root(k):
                act.wait_ge(ms_done, k + 1)
                did(act.activation(st[:, 2, k:k + 1], st[:, 1, k:k + 1], ACT.Ln, scale=-LN_SCALE), ln_done)
                did(act.activation(st[:, 3, k:k + 1], st[:, 2, k:k + 1], ACT.Exp, scale=-0.5), rs0_done)

            def stat(k, ready, src):
                squares(ready, src, st[:, 0, k:k + 1])
                first_root(k)

            def xt_high(n, cols, permute=False, dst=None):
                for half in range(2):
                    act.wait_ge(xr_turned, 2 * n + half + 1)
                    did(act.activation(token_cols(xt_hi if dst is None else dst, half, cols, permute),
                                       bank_cols(aux[(2 * n + half) % 4], permute), ACT.Copy), xt_hi_done)

            for m in range(TT):
                stat(STAT_N1 + m, (x_loaded[m], 16), x[:, m, :])
                if m in (1, 2):
                    high_of(0, 2 * m - 2)
                    high_of(0, 2 * m - 1)
                if m >= 1:
                    xt_high(NT_1 + m - 1, m - 1)
            xt_high(NT_1 + 3, 3)
            act.wait_ge(xr_ready, 4)
            load(alibi[:], t["c_alibi"], alibi_loaded)
            act.wait_ge(vec_loaded, 16 * 9)
            did(act.activation(ctmp[:], cvec[:], ACT.Exp, scale=-1.0), silu_act)
            act.wait_ge(negsel_loaded, 16)
            did(act.activation(negsel[:], sel_raw[:], ACT.Copy), negsel_ready)

            act.wait_ge(heads_loaded, 16 * 8)

            def head_gain(u):
                kind, m = u // 4, u % 4
                dst = (q_a, k_a, q_b, k_b)[kind]
                pairs = 2 if kind == 1 else 4
                act.wait_ge(qn_turned, u + 1)
                did(act.activation(dst[:, 0:pairs, m * P:(m + 1) * P],
                                   aux[u % 4][:, 0:pairs * P].rearrange("p (h s) -> p h s", h=pairs),
                                   ACT.Copy, scale=gains[:, kind:kind + 1]), qk_stored)

            for g in range(4 * N_IN1):
                s, m = g // 4, g % 4
                high_of(s + 1, m)
                if g < 16:
                    heads = 2 if s == 1 else NH
                    act.wait_ge(gemm_done, g + 1)
                    if g >= 2:
                        act.wait_ge(hms_done, g - 1)
                    did(act.activation(qsq[g % 2][:, 0:heads * HD], gp[g % 4][:, 0:heads * HD], ACT.Square), hsq_done)
                    act.wait_ge(hms_done, g + 1)
                    did(act.activation(hst[:, 2, 0:heads], hst[:, 1, 0:heads], ACT.Ln,
                                       scale=-LN_SCALE), hln_done)
                    did(act.activation(hst[:, 3, 0:heads], hst[:, 2, 0:heads], ACT.Exp, scale=-0.5), hrs0_done)
                if 1 <= g <= 16:
                    head_gain(g - 1)
                if g == 10:
                    act.wait_ge(f_step, 3)
                    did(act.activation(frow[0:NH, 3, :], frow[0:NH, 2, :], ACT.Exp, scale=-1.0), f_act)
                    act.wait_ge(f_step, 4)
                    did(act.activation(frow[0:NH, 3, :], frow[0:NH, 3, :], ACT.Ln), f_act)
                if g == 11:
                    act.wait_ge(f_step, 8)
                    did(act.activation(c_parts[:], frow[:, 0, :], ACT.Copy), c_hi_done)
                    did(act.activation(c_parts[0:NH, :], frow[0:NH, 5, :], ACT.Copy), c_hi_done)

            def exp_unit(i, cols, column):
                act.wait_ge(max_done, i + 1)
                if i >= 2:
                    act.wait_ge(turned, turn[("T", i - 2)] + 1)
                if i >= 16:
                    act.wait_ge(rden_done, i // 8 - 1)
                lo, hi = cols
                did(act.activation(prob[i % 2][:, lo:hi] if hi <= NC else None, gp[i % 4][:, lo:hi], ACT.Exp,
                                   bias=nmax[:, i % 8:i % 8 + 1], accum_out=den[:, column:column + 1]), exp_done)

            turn = TURN1
            for i, step in enumerate(STEPS1):
                if i < len(U1):
                    n, kind, h = U1[i]
                    exp_unit(i, score_cols(n, kind), i % 16)
                for what, k in step:
                    if what == "M":
                        for half in range(2):
                            w = turn[("M", k, half)]
                            act.wait_ge(turned, w + 1)
                            did(act.activation(xt_hi[:, 4 * half:4 * half + 4, k * P:(k + 1) * P],
                                               aux[w % 2][:].rearrange("p (k s) -> p k s", k=4), ACT.Copy), turn_hi)
            load(gain2[:], spread(t["mlp_norm_g"]), gain2_loaded)

            for j in range(N_OUT):
                for m in range(TT):
                    high_of(SLAB_OUT1 + j + 1, m)
                    if j:
                        stat(STAT_N2 + m, (gemm_free, TILE_OUT1 + 4 * j + m + 1), x[:, m, :])
                        if m:
                            xt_high(NT_2 + m - 1, m - 1)
            xt_high(NT_2 + 3, 3)

            def mlp(s0, t0, up0, mod, last_down):
                def split(c, i):
                    s, q = s0 + c // 4 + 1, c % 4
                    act.wait_ge(raw_loaded[q], i * 64 + arrived(s))
                    act.wait_ge(gemm_done, i * 16 + slab_end(s - 2))
                    act.activation(w_hi[s % 2][:, UK * q:UK * (q + 1), :], raw[q][:, :, :],
                                   ACT.Copy).then_inc(hi_split, 1)

                def squared_relu(c, i):
                    act.wait_ge(gemm_done, i * 16 + (t0 + c + 1))
                    if c >= 2:
                        act.wait_ge(hid_ready, i * 8 + (up0 + c - 1))
                        act.wait_ge(hid_hi, i * 8 + (up0 + c - 1))
                    act.activation(relu[c % 2][:], gp[(t0 + c) % 4][:], ACT.Relu).then_inc(relu_done, 1)
                    act.wait_ge(relu_done, i * 8 + (up0 + c + 1))
                    act.activation(ht_hi[:, c, :], relu[c % 2][:], ACT.Square).then_inc(hid_hi, 1)

                def up(i, mod):
                    for c in range(4):
                        split(c, i)
                    for c in range(8):
                        if c >= 4:
                            split(c, i)
                        if mod:
                            mod_loads(c, i)
                        squared_relu(c, i)
                    act.wait_ge(hid_ready, i * 8 + (up0 + 8))
                    act.wait_ge(hid_hi, i * 8 + (up0 + 8))

                def chunk(i, mod):
                    if mod:
                        act.wait_ge(wm_used, i * (4 * MB_UNITS) + GATE_CREDIT)
                        for u in range(2):
                            wm_load(u, i)
                    up(i, mod)
                    for c in range(8, 16):
                        split(c, i)
                        if mod:
                            mod_loads(c, i)
                    if mod:
                        act.wait_ge(mod_rowed, i * (2 * MB) + 2 * MB)
                        for j in range(2):
                            act.dma_start(mods[j:j + 1, bass.ds(i * MB * NC, MB * NC)],
                                          mod_row[j][:].rearrange("o a n -> o (a n)")).then_inc(mod_stored, 16)
                        act.wait_ge(mod_stored, i * 32 + 32)

                chunk(0, mod)
                with act.Fori(1, NCH - 1) as i:
                    chunk(i, mod)
                if mod:
                    first_loads()
                up(NCH - 1, False)
                last_down(lambda c: split(c, NCH - 1))

            def mod_loads(c, i):
                if c == 2:
                    act.dma_start(b_row[:].rearrange("o a n -> o (a n)"),
                                  t["b_mod"].rearrange("(a n) -> a n", a=1)[:, bass.ds(i * MB * NC, MB * NC)]
                                  ).then_inc(b_loaded, 16)
                if c >= 1:
                    for u in range(mod_units(c - 2) + 2, min(mod_units(c - 1) + 2, MB_UNITS)):
                        act.wait_ge(wm_used, i * (4 * MB_UNITS) + (GATE_CREDIT + 4 * (u - 1)))
                        wm_load(u, i)

            def wm_load(u, i):
                src = t["w_mod"].rearrange("(u k p) n -> u p k n", k=UK, p=P)[
                    u % 4, :, :, bass.ds(i * MB * NC + (u // 4) * NC, NC)]
                act.dma_start(wm[u % 2][:], src).then_inc(wm_loaded[u % 2], 16)

            def mod(j, k):
                return spread(mods[j, k * D:(k + 1) * D])

            def first_loads():
                load(mod_gain[:], spread(t["g_pre_mix"]), cmod_loaded)
                load(cmod_scale[:], mod(1, 1), cmod_loaded)
                load(cmod_shift[:], mod(1, 0), cmod_loaded)
                load(mod_scale[:], mod(0, 1), mod_loaded)

            def norms_of_block_2(split):
                act.wait_ge(hid_lo, 8 * NCH)
                for m in range(CT):
                    load(xr[m][:], t["ctx"][m * P:(m + 1) * P, :], cx_loaded[m])
                for c in range(8, 12):
                    split(c)
                    m = c - 8
                    if m < CT:
                        stat(STAT_CTX + m, (cx_loaded[m], 16), xr[m][:])
                    if 1 <= m <= CT:
                        xt_high(NT_CTX + m - 1, m - 1, False, ct_hi)
                    if m == CT:
                        act.wait_ge(xr_ready, NT_CTX + CT)
                        load(mod_shift[:], mod(0, 0), shift_loaded)
                for m in range(TT):
                    split(12 + m)
                    stat(STAT_N3 + m, (gemm_free, freed(TILE_IN2 - TT + m)), x[:, m, :])
                    if m:
                        xt_high(NT_3 + m - 1, m - 1, True)
                xt_high(NT_3 + 3, 3, True)

            mlp(SLAB_MLP1, TILE_MLP1, 0, True, norms_of_block_2)

            for q in range(UQ):
                high_of(SLAB_IN2 + 1, q)
            act.wait_ge(xr_ready, NT_3 + TT)
            for b in range(2):
                for h in range(NH):
                    off = RPB_LEN - 1 - (RPAD + h * RPH * RPW + (KH - 1) * RPW - 1 + RUN - 1) + 8 * b
                    act.dma_start(rpb_run[64 * b:64 * b + 64, h, :],
                                  bass.AP(tensor=t["rpb"].tensor, offset=off, ap=[[RPW, GR], [1, 8], [1, RUN]])
                                  ).then_inc(rpb_loaded, 16)
            load(pool_w[:], t["pool_w"].rearrange("g c d -> c g d"), pool_loaded)
            for s in (SLAB_IN2 + 2, SLAB_IN2 + 3, SLAB_OUT2):
                for q in range(UQ):
                    high_of(s, q)
            act.wait_ge(gemm_free, freed(TILE_OUT2 - 1))
            load(v_odd[0:64, :, :], v_2[64:P, 0:TT - 1, :], v_shifted)
            load(v_odd[64:P, :, :], v_2[0:64, 1:TT, :], v_shifted)

            turn = TURN2
            t0, e0, d0 = len(TURN1), len(U1), 2 * TT
            for i, step in enumerate(STEPS2):
                if i < len(U2):
                    k = e0 + i
                    act.wait_ge(max_done, k + 1)
                    if i >= 2:
                        act.wait_ge(turned, t0 + turn[("T", i - 2)] + 1)
                    if i >= 16:
                        act.wait_ge(rden_done, d0 + i // 8 - 1)
                    did(act.activation(prob[i % 2][:], gp[i % 4][:], ACT.Exp, bias=nmax[:, i % 8:i % 8 + 1],
                                       accum_out=den[:, i % 16:i % 16 + 1]), exp_done)
                for what, k in step:
                    if what == "M":
                        w = turn[("M", k, 0)]
                        act.wait_ge(turned, t0 + w + 1)
                        did(act.activation(grid_cols(xt_hi, k), grid_bank(aux[w % 2]), ACT.Copy), turn_hi)

            load(mix_gate[:], mod(0, 2), tail_loaded)
            load(mix_gain[:], spread(t["g_post_mix"]), tail_loaded)
            load(mlp_scale[:], mod(0, 4), tail_loaded)
            load(mlp_shift[:], mod(0, 3), tail_loaded)
            load(mlp_gain2[:], spread(t["g_pre_mlp"]), tail_loaded)
            for j in range(N_OUT):
                for m in range(TT):
                    g = TILE_OUT2 + 4 * j + m
                    high_of(SLAB_OUT2 + j + 1, m)
                    k = STAT_TAIL + 2 * m
                    squares((gemm_done, g + 1), gp[g % 4][:], (st[:, 0, k:k + 1], half_sq[:, m:m + 1])[j])
                    if j:
                        first_root(k)
                        if m:
                            xt_high(NT_4 + m - 1, m - 1)
                        stat(k + 1, (tail_step, 2 * (m + 1)), x[:, m, :])
            xt_high(NT_4 + 3, 3)
            load(fin_gate[:], mod(0, 5), fin_loaded)
            load(fin_gain[:], spread(t["g_post_mlp"]), fin_loaded)

            def last_norm(split):
                for c in range(8, 12):
                    split(c)
                for m in range(TT):
                    stat(STAT_FIN + m, (gemm_free, freed(TILE_MLP2 + 16 * NCH - TT + m)), sub[:, m, :])

            mlp(SLAB_MLP2, TILE_MLP2, 8 * NCH, False, last_norm)

        @block_fn(nc, ctx, "tensor")
        def _(pe):
            def passes(bank, lhs, rhs, last_k=None, mid=None):
                for k in range(KT):
                    if k == KT // 2 and mid is not None:
                        mid()
                    if k == KT - 1 and last_k is not None:
                        pe.wait_ge(*last_k)
                    (lh, ll), (rh, rl) = lhs(k), rhs(k)
                    pe.matmul(bank, lh, rh, start=(k == 0), stop=False)
                    pe.matmul(bank, lh, rl, start=False, stop=False)
                    mm = pe.matmul(bank, ll, rh, start=False, stop=(k == KT - 1))
                return mm

            def product(g, bank, lhs, rhs, n, wait_free=True, mid=None):
                if wait_free:
                    pe.wait_ge(gemm_free, freed(g - 4))
                passes(bank[:, 0:n], lhs, rhs, mid=mid).then_inc(gemm_done, 1)

            def early_and_late(nt, col, banks, early, late, wait_bank, turns, permute=False):
                pe.wait_ge(xt_lo_done, 2 * (nt + 2))
                for j in range(4):
                    wait_bank(j)
                    mid = (lambda: turn_rows(nt + 2 + turns.index(j), permute)) if j in turns else None
                    passes(early(banks[j]), col(j), lambda k: (early(xt_hi[:, k, :]), early(xt_lo[:, k, :])),
                           mid=mid)
                pe.wait_ge(xt_lo_done, 2 * (nt + TT))
                for j in range(4):
                    passes(late(banks[j]), col(j), lambda k: (late(xt_hi[:, k, :]), late(xt_lo[:, k, :]))
                           ).then_inc(gemm_done, 1)

            def tokens(hi, lo, m):
                return lambda k: (hi[:, k, m * P:(m + 1) * P], lo[:, k, m * P:(m + 1) * P])

            def all_tokens(hi, lo, n=S):
                return lambda k: (hi[:, k, 0:n], lo[:, k, 0:n])

            def w_cols(s, n=NC, c0=0):
                return lambda k: (w_hi[s % 2][:, k, c0:c0 + n], w_lo[s % 2][:, k, c0:c0 + n])

            def turn_rows(n, permute=False, grid=False):
                pe.wait_ge(xr_ready, n + 1)
                for half in range(2):
                    a = 2 * n + half
                    if a >= 4:
                        pe.wait_ge(xt_lo_done, a - 3)
                    for j in range(4):
                        src = xr[n % 2][:, (4 * half + j) * P:(4 * half + j + 1) * P]
                        dst = aux[a % 4][:, j * P:(j + 1) * P]
                        idn = ident[:]
                        if permute:
                            dst = dst.rearrange("p (b r c) -> p r b c", r=2, c=8)
                        mm = pe.transpose(dst, src, idn)
                    mm.then_inc(xr_turned, 1)

            pe.wait_ge(ident_loaded, 16)
            turn_rows(NT_1)
            turn_rows(NT_1 + 1)

            def split_ready(s):
                pe.wait_ge(unit_split, 4 * (s + 1))

            def turn_heads(u):
                pe.wait_ge(qn_ready, u + 1)
                if u >= 4:
                    pe.wait_ge(qk_stored, u - 3)
                pairs = 2 if u // 4 == 1 else 4
                for j in range(pairs):
                    mm = pe.transpose(aux[u % 4][:, j * P:(j + 1) * P], qn[u % 2][:, j * P:(j + 1) * P], ident[:])
                mm.then_inc(qn_turned, 1)

            for g in range(4 * N_IN1):
                s, m = g // 4, g % 4
                if m == 0:
                    split_ready(s)
                if g < 4:
                    pe.wait_ge(xt_lo_done, 2 * (NT_1 + m + 1))
                product(g, gp[g % 4], tokens(xt_hi, xt_lo, m), w_cols(s, KV_W if s == 1 else NC),
                        KV_W if s == 1 else NC, wait_free=g >= 4)
                if g < TT - 2:
                    turn_rows(NT_1 + g + 2)
                if 1 <= g <= 16:
                    if g == 5:
                        pe.wait_ge(xt_lo_done, 2 * TT)
                    turn_heads(g - 1)
                if g == 8:
                    pe.wait_ge(f_copied, TT)
                    pe.wait_ge(qk_stored, 8)
                    for k in range(TT):
                        mm = pe.transpose(aux[3][0:NH, k * P:(k + 1) * P], flog[:, k, :], ident[:])
                    mm.then_inc(f_turned, 1)
                if g == 11:
                    pe.wait_ge(f_step, 1)

            pe.wait_ge(gemm_free, 4 * N_IN1)
            pe.wait_ge(pads_clear, 1)
            pe.wait_ge(qk_stored, 16)
            pe.wait_ge(c_ready, 1)
            pe.wait_ge(negsel_ready, 1)
            pe.wait_ge(ones_ready, 1)
            pe.wait_ge(vec_loaded, 16 * 9)
            pe.wait_ge(alibi_loaded, 16)
            for i, step in enumerate(STEPS1):
                if i < len(U1):
                    n, kind, h = U1[i]
                    bank = gp[i % 4]
                    if i >= 4:
                        pe.wait_ge(exp_done, i - 3)
                    pe.wait_ge(q_padded, i + 1)
                    if kind == 0:
                        lo = 0 if n else P
                        swap = 0 if (h // 4) == (h % 2) else 1
                        pe.matmul(bank[:, 256:257], ones_row[:], sink[0:1, h:h + 1], start=True, stop=True)
                        pe.matmul(bank[:, lo:256], q_pad1[:, i % 4, :],
                                  k_a[:, swap, (n - 1) * P + lo:(n + 1) * P], start=True, stop=False)
                        mm = pe.matmul(bank[:, lo:256], identb[:], alibi[:, h, lo:256], start=False, stop=True)
                    else:
                        w = (n + 1) * P
                        pe.matmul(bank[:, 0:w], q_pad1[:, i % 4, :], k_b[:, h // 2, 0:w],
                                  start=True, stop=False)
                        pe.matmul(bank[:, 0:w], negsel[:, h, :], c_parts[:, 0:w], start=False, stop=False)
                        mm = pe.matmul(bank[:, w - P:w], identb[:], causal[:], start=False, stop=True)
                    mm.then_inc(score_done, 1)
                for what, k in step:
                    if what == "M":
                        pe.wait_ge(heads_out, 2 * (k + 1))
                        for half in range(2):
                            w = TURN1[("M", k, half)]
                            pe.wait_ge(turn_read, w - 1)
                            for j in range(4):
                                mm = pe.transpose(aux[w % 2][:, j * P:(j + 1) * P],
                                                  mixed[:, k, (4 * half + j) * P:(4 * half + j + 1) * P], ident[:])
                            mm.then_inc(turned, 1)
                        continue
                    n, kind, h = U1[k]
                    blocks = score_blocks(n, kind)
                    if what == "T":
                        w = TURN1[("T", k)]
                        pe.wait_ge(exp_done, k + 1)
                        if w >= 2:
                            pe.wait_ge(turn_read, w - 1)
                        for b in blocks:
                            mm = pe.transpose(aux[w % 2][:, b * P:(b + 1) * P],
                                              prob[k % 2][:, b * P:(b + 1) * P], ident[:])
                        mm.then_inc(turned, 1)
                    else:
                        pe.wait_ge(turn_read, TURN1[("T", k)] + 1)
                        if k % 8 == 0 and k >= 16:
                            pe.wait_ge(heads_out, k // 8 - 1)
                        for b in blocks:
                            v = (v_a[:, n - 1 + b, (h // 4) * HD:(h // 4 + 1) * HD] if kind == 0
                                 else v_b[:, b, h * HD:(h + 1) * HD])
                            mm = pe.matmul(aux[2 + (k // 8) % 2][:, h * HD:(h + 1) * HD],
                                           prob_t[k % 2][:, b, :], v, start=(b == blocks[0]), stop=(b == blocks[-1]))
                        mm.then_inc(pv_done, 1)

            for j in range(N_OUT):
                split_ready(SLAB_OUT1 + j)
                for m in range(TT):
                    if j == 0:
                        pe.wait_ge(turn_read, TURN1[("M", m, 1)] + 1)
                    g = TILE_OUT1 + 4 * j + m
                    if j and m == 2:
                        pe.wait_ge(heads_out, 2 * TT)
                    product(g, gp[g % 4], tokens(xt_hi, xt_lo, m), w_cols(SLAB_OUT1 + j), NC,
                            mid=(lambda: turn_rows(NT_2 + m - 2)) if j and m >= 2 else None)

            def mlp(s0, t0, up0, nt, mod, turns, mid):
                f0 = freed(t0 - 1)

                def bank_free(c, i):
                    if 4 <= c < 12:
                        pe.wait_ge(relu_done, i * 8 + (up0 + c - 3))
                    else:
                        pe.wait_ge(gemm_free, i * 8 + (f0 + (c - 3 if c < 4 else c - 11)))

                def chunk(i, mod, mid, turns=None):
                    def weights(c):
                        if c % 4 == 0:
                            pe.wait_ge(unit_split, i * 16 + 4 * (s0 + c // 4 + 1))

                    weights(0)
                    if turns is not None:
                        early_and_late(nt, lambda j: w_cols(s0, P, j * P), [gp[(t0 + j) % 4] for j in range(4)],
                                       lambda ap: ap[:, 0:EARLY], lambda ap: ap[:, EARLY:S],
                                       lambda j: bank_free(j, i), turns)
                    for c in range(0 if turns is None else 4, 8):
                        weights(c)
                        bank_free(c, i)
                        passes(gp[(t0 + c) % 4][:], w_cols(s0 + c // 4, P, (c % 4) * P), all_tokens(xt_hi, xt_lo)
                               ).then_inc(gemm_done, 1)
                        if mod and c in SUM_AFTER:
                            sum_mod(SUM_AFTER.index(c), i)
                    for c in range(8, 16):
                        weights(c)
                        bank_free(c, i)
                        if c == 8:
                            pe.wait_ge(hid_lo, i * 8 + (up0 + 7))
                        passes(gp[(t0 + c) % 4][:], tokens(ht_hi, ht_lo, c % 4), w_cols(s0 + c // 4),
                               (hid_lo, i * 8 + (up0 + 8)) if c == 8 else None,
                               None if mid is None else (lambda: mid(c))).then_inc(gemm_done, 1)
                        if mod and c in SUM_AFTER:
                            sum_mod(SUM_AFTER.index(c), i)

                chunk(0, mod, None, turns)
                with pe.Fori(1, NCH - 1) as i:
                    chunk(i, mod, None)
                chunk(NCH - 1, False, mid)

            def sum_mod(k, i):
                pe.wait_ge(wm_used, i * (4 * MB_UNITS) + (GATE_CREDIT + 16 * (k + 1)))
                if k:
                    pe.wait_ge(mod_rowed, i * (2 * MB) + 2 * k)
                for j in range(2):
                    mm = pe.matmul(aux[j][0:1, :], ones_col[:], mod_acc[j][k % 2][:], start=True, stop=True)
                mm.then_inc(mod_summed, 1)

            def turns_of_block_2(c):
                if c in (10, 11):
                    if c == 10:
                        pe.wait_ge(mod_rowed, 2 * MB * (NCH - 1))
                    turn_rows(NT_CTX + c - 10)
                elif c >= 14:
                    turn_rows(NT_3 + c - 14, permute=True)

            mlp(SLAB_MLP1, TILE_MLP1, 0, NT_2, True, (0, 2), turns_of_block_2)

            g = TILE_IN2

            def wait_bank(j):
                pe.wait_ge(gemm_free, freed(TILE_IN2 + j - 4))

            split_ready(SLAB_IN2)
            early_and_late(NT_3, lambda j: w_cols(SLAB_IN2, P, j * P), [gp[(g + j) % 4] for j in range(4)],
                           lambda ap: ap[:, 0:S].rearrange("p (b s) -> p b s", s=64)[:, :, 0:32],
                           lambda ap: ap[:, 0:S].rearrange("p (b s) -> p b s", s=64)[:, :, 32:64],
                           wait_bank, (0, 2), permute=True)
            g += 4
            split_ready(SLAB_IN2 + 1)
            for j in range(4):
                product(g, gp[g % 4], w_cols(SLAB_IN2 + 1, P, j * P), all_tokens(xt_hi, xt_lo), S)
                g += 1
            split_ready(SLAB_IN2 + 2)
            for j in range(4):
                product(g, gp[g % 4], w_cols(SLAB_IN2 + 2, P, j * P), all_tokens(xt_hi, xt_lo), S)
                g += 1
            for j in range(4):
                product(g, gp[g % 4], w_cols(SLAB_IN2 + 2, P, j * P), all_tokens(ct_hi, ct_lo, CTX), CTX)
                g += 1
            split_ready(SLAB_IN2 + 3)
            for m in range(CT):
                product(g, gp[g % 4], tokens(ct_hi, ct_lo, m), w_cols(SLAB_IN2 + 3), NC)
                g += 1
            for m in range(TT):
                product(g, gp[g % 4], tokens(xt_hi, xt_lo, m), w_cols(SLAB_IN2 + 3), NC)
                g += 1

            pe.wait_ge(pool_done, 4)
            pe.wait_ge(pool_loaded, 16)
            for j in range(4):
                mm = pe.matmul(aux[j][:], pool_w[:, j, :], pooled[:, j, :], start=True, stop=True)
                mm.then_inc(pool_mixed, 1)

            pe.wait_ge(gemm_free, freed(TILE_OUT2 - 1))
            pe.wait_ge(pads_clear, 2)
            t0, e0, v0, h0 = len(TURN1), len(U1), len(U1), 2 * TT
            for i, step in enumerate(STEPS2):
                if i == 2:
                    pe.wait_ge(pool_step, POOL_STEPS + 8)
                if i < len(U2):
                    n, h = U2[i]
                    pair, bank = h // 2, gp[i % 4]
                    if i >= 4:
                        pe.wait_ge(exp_done, e0 + i - 3)
                    pe.wait_ge(q_padded, e0 + i + 1)
                    q = q_pad2[:, i % 4, :]
                    pe.matmul(bank[:, 0:256], q, k_2[:, pair, KSTART[n]:KSTART[n] + 256], start=True, stop=False)
                    pe.matmul(bank[:, 0:256], identb[:], window[:, (n + 1) // 2 if n < 3 else 2, :],
                              start=False, stop=True)
                    pe.matmul(bank[:, 256:512], q, k_c[:, pair, :], start=True, stop=True).then_inc(score_done, 1)
                for what, k in step:
                    if what == "M":
                        pe.wait_ge(heads_out, h0 + k + 1)
                        w = TURN2[("M", k, 0)]
                        pe.wait_ge(turn_read, t0 + w - 1)
                        for j in range(4):
                            dst = aux[w % 2][:, j * P:(j + 1) * P].rearrange("p (r b c) -> p b r c", b=2, c=8)
                            mm = pe.transpose(dst, attn_2[k % 2][:, j * P:(j + 1) * P], ident[:])
                        mm.then_inc(turned, 1)
                        continue
                    n, h = U2[k]
                    if what == "T":
                        w = TURN2[("T", k)]
                        pe.wait_ge(exp_done, e0 + k + 1)
                        if w >= 2:
                            pe.wait_ge(turn_read, t0 + w - 1)
                        for b in range(4):
                            mm = pe.transpose(aux[w % 2][:, b * P:(b + 1) * P],
                                              prob[k % 2][:, b * P:(b + 1) * P], ident[:])
                        mm.then_inc(turned, 1)
                    else:
                        pe.wait_ge(turn_read, t0 + TURN2[("T", k)] + 1)
                        if k % 8 == 0 and k >= 16:
                            pe.wait_ge(heads_out, h0 + k // 8 - 1)
                        cols = slice(h * HD, (h + 1) * HD)
                        if (n, h) == (1, 0):
                            pe.wait_ge(v_shifted, 32)
                        for b in range(4):
                            if b >= 2:
                                v = v_c[:, b - 2, cols]
                            elif KSTART[n] % P == 0:
                                v = v_2[:, KSTART[n] // P + b, cols]
                            else:
                                v = v_odd[:, KSTART[n] // P + b, cols]
                            mm = pe.matmul(aux[2 + (k // 8) % 2][:, cols], prob_t[k % 2][:, b, :], v,
                                           start=(b == 0), stop=(b == 3))
                        mm.then_inc(pv_done, 1)

            for j in range(N_OUT):
                split_ready(SLAB_OUT2 + j)
                for m in range(TT):
                    if j == 0 and m == 0:
                        pe.wait_ge(turn_read, t0 + TURN2[("M", TT - 1, 0)] + 1)
                    g = TILE_OUT2 + 4 * j + m
                    product(g, gp[g % 4], tokens(xt_hi, xt_lo, m), w_cols(SLAB_OUT2 + j), NC,
                            mid=(lambda: turn_rows(NT_4)) if j and m == 3 else None)
            turn_rows(NT_4 + 1)
            mlp(SLAB_MLP2, TILE_MLP2, 8 * NCH, NT_4, False, (1, 3), None)

        @block_fn(nc, ctx, "vector")
        def _(dve):
            tally = Tally()

            def did(ins, s):
                ins.then_inc(s, 1)
                dve.wait_ge(s, tally.up(s))

            dve.memset(ones_col[:], 1.0)
            did(dve.memset(ones_row[:], 1.0), ones_ready)

            def refine_heads(neg_ms, u, tmp):
                did(dve.tensor_tensor(tmp, neg_ms, u, ALU.mult), hrs_done)
                did(dve.tensor_tensor(tmp, tmp, u, ALU.mult), hrs_done)
                did(dve.scalar_tensor_tensor(u, tmp, 3 / LN_SCALE, u, ALU.add, ALU.mult), hrs_done)

            def mean_square(k, squares):
                dve.wait_ge(ssq_done, squares)
                did(dve.tensor_scalar(st[:, 1, k:k + 1], st[:, 0, k:k + 1], -1.0 / D, -EPS, ALU.mult, ALU.add),
                    ms_done)

            def refine(k):
                dve.wait_ge(rs0_done, k + 1)
                u = st[:, 3, k:k + 1]
                did(dve.tensor_scalar(st[:, 2, k:k + 1], st[:, 1, k:k + 1], u, u, ALU.mult, ALU.mult), rs_done)
                did(dve.scalar_tensor_tensor(u, st[:, 2, k:k + 1], 3 / LN_SCALE, u, ALU.add, ALU.mult), rs_done)

            def stat(k, squares=None):
                mean_square(k, k + 1 if squares is None else squares)
                refine(k)

            def scaled(n, k, src, gain, shift=None):
                if n >= 2:
                    dve.wait_ge(xr_turned, 2 * (n - 1))
                ins = dve.scalar_tensor_tensor(xr[n % 2][:], src, st[:, 3, k:k + 1], gain, ALU.mult, ALU.mult)
                if shift is None:
                    did(ins, xr_ready)
                else:
                    did(ins, xr_step)
                    did(dve.tensor_tensor(xr[n % 2][:], xr[n % 2][:], shift, ALU.add), xr_ready)

            def xt_low(n, cols, permute=False, dst=None):
                hi, lo = (xt_hi, xt_lo) if dst is None else dst
                for half in range(2):
                    dve.wait_ge(xt_hi_done, 2 * n + half + 1)
                    did(dve.tensor_tensor(token_cols(lo, half, cols, permute),
                                          bank_cols(aux[(2 * n + half) % 4], permute),
                                          token_cols(hi, half, cols, permute).bitcast(F32), ALU.subtract), xt_lo_done)

            dve.wait_ge(gain1_loaded, 16)
            for m in range(TT):
                stat(STAT_N1 + m)
                scaled(NT_1 + m, STAT_N1 + m, x[:, m, :], gain1[:])
                if m:
                    xt_low(NT_1 + m - 1, m - 1)
            xt_low(NT_1 + 3, 3)
            dve.wait_ge(silu_act, 1)
            did(dve.tensor_scalar(ctmp[:], ctmp[:], 1.0, None, ALU.add), silu_step)
            did(dve.reciprocal(csil[:], ctmp[:]), silu_step)
            did(dve.tensor_tensor(csil[:], csil[:], cvec[:], ALU.mult), silu_step)
            dve.wait_ge(heads_loaded, 16 * 8)
            did(dve.tensor_scalar(gains[:, 0:1], gains[:, 0:1], QSCALE, None, ALU.mult), silu_step)
            did(dve.tensor_scalar(gains[:, 2:3], gains[:, 2:3], QSCALE, None, ALU.mult), silu_step)

            for g in range(4 * N_IN1):
                s, m = g // 4, g % 4
                bank = gp[g % 4]
                dve.wait_ge(gemm_done, g + 1)
                if g >= 16:
                    did(dve.tensor_copy(v_b[:, m, :], bank[:]), gemm_free)
                    continue
                heads = 2 if s == 1 else NH
                dve.wait_ge(hsq_done, g + 1)
                did(dve.tensor_reduce(hst[:, 0, 0:heads], qsq[g % 2][:, 0:heads * HD].rearrange(
                    "p (h d) -> p h d", d=HD), AXX, ALU.add), rs_done)
                did(dve.tensor_scalar(hst[:, 1, 0:heads], hst[:, 0, 0:heads], -1.0 / HD, -EPS, ALU.mult, ALU.add),
                    hms_done)
                dve.wait_ge(hrs0_done, g + 1)
                refine_heads(hst[:, 1, 0:heads], hst[:, 3, 0:heads], hst[:, 2, 0:heads])
                if g >= 2:
                    dve.wait_ge(qn_turned, g - 1)
                if s == 1:
                    did(dve.tensor_copy(v_a[:, m, :], bank[:, P:2 * P]), v_copied)
                    did(dve.tensor_copy(flog[:, m, :], bank[:, 256:KV_W]), f_copied)
                    for j, col in ((0, 0), (1, HD), (1, P), (0, P + HD)):
                        did(dve.tensor_scalar(qn[g % 2][:, col:col + HD], bank[:, j * HD:(j + 1) * HD],
                                              hst[:, 3, j:j + 1], None, ALU.mult), v_copied)
                    did(dve.tensor_copy(hst[:, 0, 0:1], hst[:, 3, 0:1]), gemm_free)
                    did(dve.tensor_copy(hst[:, 0, 0:1], hst[:, 3, 0:1]), qn_ready)
                else:
                    did(dve.tensor_tensor(qn[g % 2][:].rearrange("p (h d) -> p h d", d=HD),
                                          bank[:].rearrange("p (h d) -> p h d", d=HD),
                                          hst[:, 3, :].unsqueeze(2).broadcast_to([P, NH, HD]), ALU.mult), gemm_free)
                    did(dve.tensor_copy(hst[:, 0, 0:1], hst[:, 3, 0:1]), qn_ready)
                if g == 9:
                    dve.wait_ge(f_turned, 1)
                    dve.wait_ge(vec_loaded, 16 * 9)
                    did(dve.tensor_scalar(frow[0:NH, 0, :], aux[3][0:NH, :], b_f[:], None, ALU.add), f_step)
                    did(dve.tensor_scalar(frow[0:NH, 1, :], frow[0:NH, 0, :], -1.0, None, ALU.mult), f_step)
                    did(dve.tensor_tensor(frow[0:NH, 2, :], frow[0:NH, 0, :], frow[0:NH, 1, :], ALU.max), f_step)
                if g == 10:
                    dve.wait_ge(f_act, 1)
                    did(dve.tensor_scalar(frow[0:NH, 3, :], frow[0:NH, 3, :], 1.0, None, ALU.add), f_step)
                    dve.wait_ge(f_act, 2)
                    did(dve.scalar_tensor_tensor(frow[0:NH, 4, :], frow[0:NH, 0, :], 0.0, frow[0:NH, 3, :],
                                                 ALU.min, ALU.subtract), f_step)
                    did(dve.memset(frow[0:NH, 1, :], 1.0), f_step)
                    did(dve.tensor_tensor_scan(frow[0:NH, 5, :], frow[0:NH, 1, :], frow[0:NH, 4, :], 0.0,
                                               ALU.mult, ALU.add), f_step)
                    did(dve.memset(frow[:, 0, :], 0.0), f_step)
            dve.wait_ge(c_hi_done, 2)
            did(dve.tensor_tensor(c_parts[32:CR, :], frow[0:NH, 5, :], c_parts[0:NH, :].bitcast(F32),
                                  ALU.subtract), c_ready)

            def copy_turn(k, w, first, n_blocks, t0):
                dve.wait_ge(turned, t0 + w + 1)
                did(dve.tensor_copy(prob_t[k % 2][:, first:first + n_blocks, :],
                                    aux[w % 2][:, first * P:(first + n_blocks) * P].rearrange(
                                        "p (b s) -> p b s", b=n_blocks)), turn_read)

            def heads_tile(b, v0, e0, dst):
                dve.wait_ge(exp_done, e0 + 8 * b + 8)
                cols = slice(8 * (b % 2), 8 * (b % 2) + 8)
                did(dve.reciprocal(rden[:, cols], den[:, cols]), rden_done)
                dve.wait_ge(pv_done, v0 + 8 * b + 8)
                did(dve.tensor_tensor(dst.rearrange("p (h d) -> p h d", d=HD),
                                      aux[2 + b % 2][:].rearrange("p (h d) -> p h d", d=HD),
                                      rden[:, cols].unsqueeze(2).broadcast_to([P, NH, HD]), ALU.mult), heads_out)

            for i, step in enumerate(STEPS1):
                if i < len(U1):
                    n, kind, h = U1[i]
                    lo, hi = score_cols(n, kind)
                    dve.wait_ge(score_done, i + 1)
                    if i >= 8:
                        dve.wait_ge(exp_done, i - 7)
                    did(dve.tensor_reduce(nmax[:, i % 8:i % 8 + 1], gp[i % 4][:, lo:hi], AXX, ALU.max, negate=True),
                        max_done)
                for what, k in step:
                    if what == "T":
                        n, kind, h = U1[k]
                        blocks = score_blocks(n, kind)
                        if k >= 2:
                            dve.wait_ge(pv_done, k - 1)
                        copy_turn(k, TURN1[("T", k)], blocks[0], len(blocks), 0)
                    elif what == "V" and k % 8 == 7:
                        n, kind, h = U1[k]
                        heads_tile(k // 8, 0, 0, mixed[:, n, kind * S:(kind + 1) * S])
                    elif what == "M":
                        for half in range(2):
                            w = TURN1[("M", k, half)]
                            dve.wait_ge(turn_hi, 2 * k + half + 1)
                            hi_cols = xt_hi[:, 4 * half:4 * half + 4, k * P:(k + 1) * P]
                            did(dve.tensor_tensor(xt_lo[:, 4 * half:4 * half + 4, k * P:(k + 1) * P],
                                                  aux[w % 2][:].rearrange("p (k s) -> p k s", k=4),
                                                  hi_cols.bitcast(F32), ALU.subtract), turn_read)

            for j in range(N_OUT):
                for m in range(TT):
                    g = TILE_OUT1 + 4 * j + m
                    dve.wait_ge(gemm_done, g + 1)
                    cols = x[:, m, j * NC:(j + 1) * NC]
                    did(dve.tensor_tensor(cols, cols, gp[g % 4][:], ALU.add), gemm_free)
                    if j:
                        if m == 0:
                            dve.wait_ge(gain2_loaded, 16)
                        stat(STAT_N2 + m)
                        scaled(NT_2 + m, STAT_N2 + m, x[:, m, :], gain2[:])
                        if m:
                            xt_low(NT_2 + m - 1, m - 1)
            xt_low(NT_2 + 3, 3)

            def mlp(t0, acc, up0, mod, after, fresh=False):
                f0 = freed(t0 - 1)

                def chunk(i, mod, after, fresh=False):
                    for c in range(16):
                        bank = gp[(t0 + c) % 4]
                        if c < 8:
                            dve.wait_ge(relu_done, i * 8 + (up0 + c + 1))
                            if c >= 2:
                                dve.wait_ge(hid_lo, i * 8 + (up0 + c - 1))
                            dve.tensor_tensor(hid[c % 2][:], relu[c % 2][:], relu[c % 2][:], ALU.mult
                                              ).then_inc(hid_ready, 1)
                            dve.wait_ge(hid_hi, i * 8 + (up0 + c + 1))
                            dve.wait_ge(hid_ready, i * 8 + (up0 + c + 1))
                            dve.tensor_tensor(ht_lo[:, c, :], hid[c % 2][:], ht_hi[:, c, :].bitcast(F32),
                                              ALU.subtract).then_inc(hid_lo, 1)
                        else:
                            dve.wait_ge(gemm_done, i * 16 + (t0 + c + 1))
                            if c == 8:
                                dve.wait_ge(hid_lo, i * 8 + (up0 + 8))
                            cols = acc[:, c % 4, (c // 4 - 2) * NC:(c // 4 - 1) * NC]
                            if fresh:
                                dve.tensor_copy(cols, bank[:]).then_inc(gemm_free, 1)
                            else:
                                dve.tensor_tensor(cols, cols, bank[:], ALU.add).then_inc(gemm_free, 1)
                            if after is not None:
                                dve.wait_ge(gemm_free, i * 8 + (f0 + c - 7))
                                after(c)
                        if mod:
                            if c - 1 in SUM_AFTER:
                                mod_rows(SUM_AFTER.index(c - 1), i)
                            for e in range(4 * mod_units(c - 1), 4 * mod_units(c)):
                                modulate(e, i)

                chunk(0, mod, None, fresh)
                with dve.Fori(1, NCH - 1) as i:
                    chunk(i, mod, None)
                dve.wait_ge(gemm_free, f0 + 8 * (NCH - 1))
                tally.up(gemm_free, 8 * NCH)
                chunk(NCH - 1, False, after)

            def modulate(e, i):
                u, row, j = e // 4, e % 4 // 2, e % 2
                k, kt = u // UQ, (u % UQ) * UK + row
                acc = mod_acc[j][k % 2][:]
                w = wm[u % 2][:, row, :]
                if e % 4 == 0:
                    dve.wait_ge(wm_loaded[u % 2], i * (8 * MB_UNITS) + 16 * (u // 2 + 1))
                if e >= 2:
                    dve.wait_ge(wm_used, i * (4 * MB_UNITS) + (GATE_CREDIT + e - 1))
                if kt == 0:
                    ins = dve.tensor_scalar(acc, w, csil[:, j, kt:kt + 1], None, ALU.mult)
                else:
                    ins = dve.scalar_tensor_tensor(acc, w, csil[:, j, kt:kt + 1], acc, ALU.mult, ALU.add)
                ins.then_inc(wm_used, 1)

            def mod_rows(k, i):
                if k == 0:
                    dve.wait_ge(b_loaded, i * 16 + 16)
                dve.wait_ge(mod_summed, i * MB + (k + 1))
                for j in (1, 0):
                    if j == 0:
                        dve.wait_ge(mod_rowed, i * (2 * MB) + (2 * k + 1))
                    dve.tensor_tensor(mod_row[j][:, k, :], aux[j][0:1, :], b_row[:, k, :], ALU.add
                                      ).then_inc(mod_rowed, 1)

            def norms_of_block_2(c):
                m = c - 8
                if m == 0:
                    dve.wait_ge(cmod_loaded, 48)
                    did(dve.scalar_tensor_tensor(cmod_scale[:], cmod_scale[:], 1.0, mod_gain[:], ALU.add, ALU.mult),
                        mod_made)
                    dve.wait_ge(mod_loaded, 16)
                    did(dve.scalar_tensor_tensor(mod_scale[:], mod_scale[:], 1.0, mod_gain[:], ALU.add, ALU.mult),
                        mod_made)
                if m < CT:
                    stat(STAT_CTX + m)
                    scaled(NT_CTX + m, STAT_CTX + m, xr[m][:], cmod_scale[:], cmod_shift[:])
                if 1 <= m <= CT:
                    xt_low(NT_CTX + m - 1, m - 1, False, (ct_hi, ct_lo))
                m = c - 12
                if m >= 0:
                    if m == 0:
                        dve.wait_ge(shift_loaded, 16)
                    stat(STAT_N3 + m)
                    scaled(NT_3 + m, STAT_N3 + m, x[:, m, :], mod_scale[:], mod_shift[:])
                    if m:
                        xt_low(NT_3 + m - 1, m - 1, True)

            did(dve.tensor_copy(ctmp[:, 0, :], csil[:, 0, :]), wm_used)
            mlp(TILE_MLP1, x, 0, True, norms_of_block_2)
            xt_low(NT_3 + 3, 3, True)

            g = TILE_IN2
            did(dve.memset(upad[:], 0.0), pool_step)
            for j in range(4):
                win = 2 ** (j + 1)
                dve.wait_ge(gemm_done, g + 1)
                grid = upad[:, 8:8 + S].rearrange("p (r b c) -> p b r c", r=GR, c=8)
                did(dve.tensor_copy(grid, gp[g % 4][:].rearrange("p (b r c) -> p b r c", r=GR, c=8)), gemm_free)
                src, width = upad, 528
                for e in range(j + 1):
                    width -= 2 ** e
                    did(dve.tensor_tensor(wsum[e % 2][:, 0:width], src[:, 0:width],
                                          src[:, 2 ** e:2 ** e + width], ALU.add), pool_step)
                    src = wsum[e % 2]
                first = 8 - win // 2
                left, right = src[:, first:first + 8], src[:, first + S - 8:first + S]
                dve.wait_ge(vec_loaded, 16 * 9)
                did(dve.tensor_tensor(left, left, edge[:, j, 0:8], ALU.mult), pool_step)
                did(dve.tensor_tensor(right, right, edge[:, j, 8:16], ALU.mult), pool_step)
                did(dve.scalar_tensor_tensor(pooled[:, j, :], src[:, first:first + S], 1.0 / win,
                                             upad[:, 8:8 + S], ALU.mult, ALU.subtract), pool_done)
                g += 1
            assert tally.n[pool_step.name] == POOL_STEPS
            for j in range(4):
                dve.wait_ge(gemm_done, g + 1)
                did(dve.tensor_scalar(q_2[:, j, :], gp[g % 4][:], QSCALE, None, ALU.mult), gemm_free)
                g += 1
            for j in range(4):
                dve.wait_ge(gemm_done, g + 1)
                did(dve.tensor_copy(k_2[:, j, :], gp[g % 4][:]), gemm_free)
                g += 1
            for j in range(4):
                dve.wait_ge(gemm_done, g + 1)
                did(dve.tensor_copy(k_c[:, j, :], gp[g % 4][:, 0:CTX]), gemm_free)
                g += 1
            for m in range(CT):
                dve.wait_ge(gemm_done, g + 1)
                did(dve.tensor_copy(v_c[:, m, :], gp[g % 4][:]), gemm_free)
                g += 1
            for m in range(TT):
                dve.wait_ge(gemm_done, g + 1)
                did(dve.tensor_copy(v_2[:, m, :], gp[g % 4][:]), gemm_free)
                g += 1
            for j in range(4):
                dve.wait_ge(pool_mixed, j + 1)
                did(dve.tensor_scalar(xt_hi[:, j, :], aux[j][:], pscale[:, j:j + 1], None, ALU.mult), pool_step)
                did(dve.scalar_tensor_tensor(xt_lo[:, j, :], aux[j][:], pscale[:, j:j + 1],
                                             xt_hi[:, j, :].bitcast(F32), ALU.mult, ALU.subtract), pool_step)

            dve.wait_ge(rpb_loaded, 16 * 2 * NH)
            t0, e0, v0 = len(TURN1), len(U1), len(U1)
            for i, step in enumerate(STEPS2):
                if i < len(U2):
                    n, h = U2[i]
                    bank = gp[i % 4]
                    dve.wait_ge(score_done, e0 + i + 1)
                    if i >= 8:
                        dve.wait_ge(exp_done, e0 + i - 7)
                    local = bank[:, 0:256].rearrange("p (b r c) -> p b r c", r=KH, c=8)
                    run = rpb_run[:, h, RUN - 1 - KSHIFT[n]:RUN - KSHIFT[n]]
                    run = bass.AP(tensor=run.tensor, offset=run.offset,
                                  ap=[list(run.ap[0]), [-8, 4], [-RPW, KH], [-1, 8]])
                    did(dve.tensor_tensor(local, local, run, ALU.add), bias_added)
                    did(dve.tensor_reduce(nmax[:, i % 8:i % 8 + 1], bank[:], AXX, ALU.max, negate=True), max_done)
                for what, k in step:
                    if what == "T":
                        if k >= 2:
                            dve.wait_ge(pv_done, v0 + k - 1)
                        copy_turn(k, TURN2[("T", k)], 0, 4, t0)
                    elif what == "V" and k % 8 == 7:
                        if k >= 16:
                            dve.wait_ge(turned, t0 + TURN2[("M", k // 8 - 2, 0)] + 1)
                        heads_tile(k // 8, v0, e0, attn_2[(k // 8) % 2][:])
                    elif what == "M":
                        w = TURN2[("M", k, 0)]
                        dve.wait_ge(turn_hi, 2 * TT + k + 1)
                        did(dve.tensor_tensor(grid_cols(xt_lo, k), grid_bank(aux[w % 2]),
                                              grid_cols(xt_hi, k).bitcast(F32), ALU.subtract), turn_read)

            dve.wait_ge(tail_loaded, 16 * 5)
            did(dve.tensor_tensor(mix_gate[:], mix_gate[:], mix_gain[:], ALU.mult), mod_made)
            did(dve.scalar_tensor_tensor(mlp_scale[:], mlp_scale[:], 1.0, mlp_gain2[:], ALU.add, ALU.mult), mod_made)

            for j in range(N_OUT):
                for m in range(TT):
                    g = TILE_OUT2 + 4 * j + m
                    k = STAT_TAIL + 2 * m
                    cols = slice(j * NC, (j + 1) * NC)
                    dve.wait_ge(gemm_done, g + 1)
                    if j:
                        dve.wait_ge(ssq_done, tail_squares(m, 0))
                        did(dve.tensor_tensor(st[:, 0, k:k + 1], st[:, 0, k:k + 1], half_sq[:, m:m + 1], ALU.add),
                            tail_step)
                        mean_square(k, tail_squares(m, 0))
                    else:
                        dve.wait_ge(ssq_done, STAT_TAIL + m + 1)
                    did(dve.tensor_tensor(sub[:, m, cols], gp[g % 4][:], mix_gate[:, cols], ALU.mult), gemm_free)
                    if j:
                        refine(k)
                        did(dve.scalar_tensor_tensor(x[:, m, :], sub[:, m, :], st[:, 3, k:k + 1], x[:, m, :],
                                                     ALU.mult, ALU.add), tail_step)
                        if m:
                            xt_low(NT_4 + m - 1, m - 1)
                        stat(k + 1, tail_squares(m, 1))
                        scaled(NT_4 + m, k + 1, x[:, m, :], mlp_scale[:], mlp_shift[:])
            xt_low(NT_4 + 3, 3)

            def last_norm(c):
                m = c - 12
                if m < 0:
                    return
                if m == 0:
                    dve.wait_ge(fin_loaded, 32)
                    did(dve.tensor_tensor(fin_gate[:], fin_gate[:], fin_gain[:], ALU.mult), mod_made)
                k = STAT_FIN + m
                stat(k, k + 1 + TT)
                did(dve.scalar_tensor_tensor(sub[:, m, :], sub[:, m, :], st[:, 3, k:k + 1], fin_gate[:],
                                             ALU.mult, ALU.mult), fin_step)
                did(dve.tensor_tensor(x[:, m, :], x[:, m, :], sub[:, m, :], ALU.add), fin_step)

            mlp(TILE_MLP2, sub, 8 * NCH, False, last_norm, fresh=True)


SUM_AFTER = (4, 7, 11, 14)


MOD_DONE = (1, 3, 4, 5, 7, 8, 8, 8, 9, 11, 12, 14, 15, 16, 16, 16)


def mod_units(c):
    return MOD_DONE[c] if c >= 0 else 0


POOL_STEPS = 1 + (1 + 2 + 3 + 4) + 2 * 4


def tail_squares(m, second):
    return STAT_TAIL + TT + 2 * m + 1 + second


def score_cols(n, kind):
    return ((0 if n else P), 257) if kind == 0 else (0, (n + 1) * P)


def score_blocks(n, kind):
    return ([0, 1] if n else [1]) if kind == 0 else list(range(n + 1))


def token_cols(dst, half, m, permute):
    if not permute:
        return dst[:, 4 * half:4 * half + 4, m * P:(m + 1) * P]
    return dst[:, 4 * half:4 * half + 4, :].rearrange("p k (b s) -> p k b s", s=64)[:, :, :, 16 * m:16 * m + 16]


def bank_cols(bank, permute):
    if not permute:
        return bank[:].rearrange("p (k s) -> p k s", k=4)
    return bank[:].rearrange("p (k b s) -> p k b s", k=4, s=16)


def grid_cols(dst, n):
    return dst[:, 4:8, :].rearrange("p k (r s) -> p k r s", s=GW)[:, :, :, 16 * n:16 * n + 16]


def grid_bank(bank):
    return bank[:].rearrange("p (k r s) -> p k r s", k=4, s=16)


_BLOCKS = {}


def block_fn(nc, ctx, engine):
    if id(nc) not in _BLOCKS:
        _BLOCKS[id(nc)] = ctx.enter_context(nc.Block())
    block = _BLOCKS[id(nc)]
    return {"sync": block.sync, "gpsimd": block.gpsimd, "scalar": block.scalar, "tensor": block.tensor,
            "vector": block.vector}[engine]


def constants():
    bf = np.dtype("bfloat16")
    q = np.arange(P)[:, None]
    k = np.arange(256)[None, :]
    dist = q + P - k
    band = (dist >= 0) & (dist < 128)
    alibi = np.stack([np.where(band, -(2.0 ** -(h + 1)) * dist, NEG) for h in range(NH)], axis=1)
    causal = np.where(np.arange(P)[None, :] <= q, 0.0, NEG)
    window = np.zeros((P, 3, 256))
    for v, (n, kc0) in enumerate(((0, 0), (1, 8), (3, 32))):
        for p in range(P):
            qc = 16 * n + 8 * (p // 64) + p % 8
            kc = kc0 + 8 * (np.arange(256) // 64) + np.arange(256) % 8
            first = min(max(qc - KW // 2, 0), GW - KW)
            window[p, v] = np.where((kc >= first) & (kc < first + KW), 0.0, NEG)
    edge = np.ones((4, 16))
    for g in range(4):
        w = 2 ** (g + 1)
        lo, hi = w // 2, w - 1 - w // 2
        for c, tok in enumerate(list(range(8)) + list(range(S - 8, S))):
            edge[g, c] = w / (min(tok + hi + 1, S) - max(tok - lo, 0))
    negsel = np.zeros((CR, NH, P))
    for h in range(NH):
        negsel[h, h] = negsel[32 + h, h] = -1.0
    return {
        "c_ident": np.eye(P, dtype=np.float32),
        "c_identb": np.eye(P).astype(bf),
        "c_alibi": alibi.astype(bf),
        "c_causal": causal.astype(bf),
        "c_window": window.astype(bf),
        "c_edge": np.broadcast_to(edge.astype(np.float32), (P, 4, 16)).copy(),
        "c_negsel": negsel.reshape(CR, NH * P).astype(np.float32),
    }


def kernel(**inputs):
    import concourse.bacc as bacc
    from concourse.bass_utils import run_bass_kernel_spmd

    def f(name, shape=None):
        a = np.ascontiguousarray(inputs[name])
        return a if shape is None else a.reshape(shape)

    def by_partition(name):
        return np.ascontiguousarray(f(name).reshape(-1, P).T)

    rpb = np.zeros(RPB_LEN, np.float32)
    rpb[RPAD:-RPAD] = f("rpb_2").reshape(-1)[::-1]
    arrays = {
        "x": f("x", (S, D)), "attn_norm_g": f("attn_norm_g"), "w_in": f("w_in"), "b_forget": f("b_forget"),
        "q_norm_a": f("q_norm_a"), "k_norm_a": f("k_norm_a"), "sink_logits": f("sink_logits"),
        "q_norm_b": f("q_norm_b"), "k_norm_b": f("k_norm_b"), "w_out": f("w_out"), "mlp_norm_g": f("mlp_norm_g"),
        "w_up": f("w_up"), "w_down": f("w_down"), "c": by_partition("c_2"), "ctx": f("ctx_2", (CTX, D)),
        "c_ctx": by_partition("c_ctx_2"), "w_mod": f("w_mod_2", (D, 6 * D)), "b_mod": f("b_mod_2", (6 * D,)),
        "g_pre_mix": f("g_pre_mix_2", (D,)), "g_post_mix": f("g_post_mix_2", (D,)),
        "g_pre_mlp": f("g_pre_mlp_2", (D,)), "g_post_mlp": f("g_post_mlp_2", (D,)),
        "w_in_2": f("w_in_2", (D, 2048)), "pool_w": f("pool_w_2", (4, P, P)), "pool_scale": by_partition("pool_scale_2"),
        "rpb": rpb, "w_out_2": f("w_out_2", (D, D)), "w_mlp_in_2": f("w_mlp_in_2", (D, DFF)),
        "w_mlp_out_2": f("w_mlp_out_2", (DFF, D)),
    }
    arrays.update(constants())
    nc = bacc.Bacc("TRN2", target_bir_lowering=False, num_devices=1)
    t = {}
    for name, a in arrays.items():
        t[name] = nc.dram_tensor(f"in_{name}", a.shape, mybir.dt.from_np(a.dtype), kind="ExternalInput").ap()
    out = nc.dram_tensor("out", (S, D), F32, kind="ExternalOutput").ap()
    build(nc, t, out)
    r = run_bass_kernel_spmd(nc, [{f"in_{name}": a for name, a in arrays.items()}], core_ids=[0])
    return r.results[0]["out"].reshape(1, S, D)
```

```python
from contextlib import ExitStack

import numpy as np

import concourse.bass as bass
import concourse.mybir as mybir

F32 = mybir.dt.float32
F32R = mybir.dt.float32r
BF16 = mybir.dt.bfloat16
ALU = mybir.AluOpType
ACT = mybir.ActivationFunctionType
AXX = mybir.AxisListType.X

P = 128
D = 1024
S = 512
CTX = 256
DFF = 4096
HD = 64
NH = 8
KT = D // P
TT = S // P
CT = CTX // P
NC = 512
UK = 2
UQ = KT // UK
NCH = DFF // D
EPS = 1e-6
NEG = -1e30
QSCALE = HD ** -0.5
LN_SCALE = 2.0 ** (2 / 3)

GR, GW = 8, 64
KH, KW = 8, 16
RPW = 2 * KW - 1
RPH = 2 * KH - 1
RUN = (KH - 1) * RPW + 32 + 16
CR = 32 + NH
RPAD = 16
RPB_LEN = 2 * RPAD + NH * RPH * RPW
KSTART = (0, 64, 192, 256)
KSHIFT = (16, 8, 8, 0)

IN1_COLS = ((0, 512), (512, 256), (768, 512), (1280, 512), (1792, 512))
KV_W = 264
N_IN1, N_OUT, N_MLP, N_IN2 = 5, 2, 4 * NCH, 4
SLAB_OUT1 = N_IN1
SLAB_MLP1 = SLAB_OUT1 + N_OUT
SLAB_IN2 = SLAB_MLP1 + N_MLP
SLAB_OUT2 = SLAB_IN2 + N_IN2
SLAB_MLP2 = SLAB_OUT2 + N_OUT
SLABS = SLAB_MLP2 + N_MLP

TILE_OUT1 = 4 * N_IN1
TILE_MLP1 = TILE_OUT1 + 2 * TT
TILE_IN2 = TILE_MLP1 + 4 * N_MLP
IN2_TILES = (4, 4, 4 + 4, CT + TT)
TILE_OUT2 = TILE_IN2 + sum(IN2_TILES)
TILE_MLP2 = TILE_OUT2 + 2 * TT
OUT2_ORDER = ((0, 0), (1, 0), (0, 1), (1, 1), (0, 2), (0, 3), (1, 2), (1, 3))
POOL_SPLIT_IN = (13, 15, 17, 19)
SPLIT_IN_ATTENTION = (4, 6, 8, 10)


def slab_end(s):
    if s < SLAB_IN2:
        return 4 * (s + 1)
    if s < SLAB_OUT2:
        return TILE_IN2 + sum(IN2_TILES[:s - SLAB_IN2 + 1])
    if s == SLAB_OUT2:
        return TILE_OUT2 + OUT2_ORDER.index((0, TT - 1)) + 1
    return TILE_OUT2 + 4 * (s - SLAB_OUT2 + 1)


def freed(g):
    for t0, before in ((TILE_MLP2, 8 * NCH), (TILE_MLP1, 0)):
        if t0 <= g < t0 + 16 * NCH:
            return t0 - before + 8 * ((g - t0) // 16) + max((g - t0) % 16 - 7, 0)
    return g + 1 - (8 * NCH if g >= TILE_MLP1 else 0)


STAT_N1, STAT_N2, STAT_CTX, STAT_N3, STAT_TAIL, STAT_FIN = 0, 4, 8, 10, 14, 22
NT_1, NT_2, NT_CTX, NT_3, NT_4 = 0, 4, 8, 10, 14
MB = 12 * NC // ((NCH - 1) * NC)
MB_UNITS = MB * UQ
assert MB * NC == 2 * D


def vectors(i):
    return 2 if isinstance(i, int) else 1


def before(i, one):
    return 0 if isinstance(i, int) else i * one + one


EARLY = S // 2

U1 = [(n, kind, h) for n in range(TT) for kind in range(2) for h in range(NH)]
U2 = [(n, h) for n in range(TT) for h in range(NH)]
LAG_T, LAG_V, LAG_M = 2, 3, 4


def attention_order(units, per_tile, halves):
    steps = []
    for i in range(units + LAG_M + 1):
        step = []
        if 0 <= i - LAG_T < units:
            step.append(("T", i - LAG_T))
        if 0 <= i - LAG_V < units:
            step.append(("V", i - LAG_V))
        if i >= per_tile + LAG_M and (i - LAG_M) % per_tile == 0:
            step.append(("M", (i - LAG_M) // per_tile - 1))
        steps.append(step)
    turn = {}
    for step in steps:
        for what, k in step:
            if what == "T":
                turn[what, k] = len(turn)
            elif what == "M":
                for half in range(halves):
                    turn[what, k, half] = len(turn)
    return steps, turn


STEPS1, TURN1 = attention_order(len(U1), 2 * NH, 2)
STEPS2, TURN2 = attention_order(len(U2), NH, 1)


class Tally:

    def __init__(self):
        self.n = {}

    def up(self, sem, k=1):
        self.n[sem.name] = self.n.get(sem.name, 0) + k
        return self.n[sem.name]


def build(nc, t, out):
    ctx = ExitStack()
    with ctx:
        base = (nc.sbuf_base + 63) // 64 * 64
        top = [base]

        def at(name, shape, dtype, offset):
            return nc.alloc_sbuf_tensor_at(name, shape, dtype, offset=offset)

        def place(name, shape, dtype):
            a = top[0]
            size = int(np.prod(shape[1:])) * (2 if dtype == BF16 else 4)
            top[0] = a + (size + 31) // 32 * 32
            return at(name, shape, dtype, a)

        def region(kib):
            a = top[0]
            top[0] = a + kib * 1024
            return a

        K = 1024
        raw = [place(f"w_raw{q}", [P, UK, NC], F32) for q in range(UQ)]
        w_hi = [place(f"w_hi{s}", [P, KT, NC], F32R) for s in range(2)]
        w_lo = [place(f"w_lo{s}", [P, KT, NC], F32R) for s in range(2)]
        xt_hi = place("xt_hi", [P, KT, S], F32R)
        xt_lo = place("xt_lo", [P, KT, S], F32R)
        x = place("x", [P, TT, D], F32)
        H = region(32)
        ht_hi = at("ht_hi", [P, KT, S], F32R, H)
        ht_lo = at("ht_lo", [P, KT, S], F32R, H + 16 * K)
        q_a = at("q_a", [P, 4, S], F32, H)
        q_b = at("q_b", [P, 4, S], F32, H + 8 * K)
        k_b = at("k_b", [P, 4, S], F32, H + 16 * K)
        v_b = at("v_b", [P, TT, S], F32, H + 24 * K)
        pooled = at("pooled", [P, 4, S], F32, H)
        q_2 = at("q_2", [P, 4, S], F32, H + 8 * K)
        k_2 = at("k_2", [P, 4, S], F32, H + 16 * K)
        v_2 = at("v_2", [P, TT, S], F32, H + 24 * K)
        mix_gate = at("mix_gate", [P, D], F32, H)
        mix_gain = at("mix_gain", [P, D], F32, H + 4 * K)
        mlp_scale = at("mlp_scale", [P, D], F32, H + 8 * K)
        mlp_shift = at("mlp_shift", [P, D], F32, H + 12 * K)
        mlp_gain2 = at("mlp_gain2", [P, D], F32, H + 16 * K)
        A = region(16)
        mixed = at("mixed", [P, TT, D], F32, A)
        frow = at("frow", [CR, 6, S], F32, A)
        sel_raw = at("sel_raw", [CR, NH, P], F32, A + 12 * K)
        wm = [at(f"wm{i}", [P, UK, NC], F32, A + 4 * K * i) for i in range(2)]
        mod_lo = [[at(f"mod_lo{i}{j}", [P, NC], F32R, A + 8 * K + 4 * K * i + 2 * K * j) for j in range(2)]
                  for i in range(2)]
        mod_acc = [[at(f"mod_acc{i}{j}", [P, NC], F32, A + 8 * K + 4 * K * i + 2 * K * j) for j in range(2)]
                   for i in range(2)]
        ct_hi = at("ct_hi", [P, KT, CTX], F32R, A)
        ct_lo = at("ct_lo", [P, KT, CTX], F32R, A + 8 * K)
        v_odd = at("v_odd", [P, TT - 1, S], F32, A)
        q_pad2 = at("q_pad2", [P, 4, P], F32, A + 10 * K)
        attn_2 = [at(f"attn_2{i}", [P, NC], F32, A + 6 * K + 2 * K * i) for i in range(2)]
        sub = at("sub", [P, TT, D], F32, A)
        T = region(8)
        xr = [at(f"xr{i}", [P, D], F32, T + 4 * K * i) for i in range(2)]
        qn = [at(f"qn{i}", [P, NC], F32, T + 2 * K * i) for i in range(2)]
        qsq = [at(f"qsq{i}", [P, NC], F32, T + 4 * K + 2 * K * i) for i in range(2)]
        prob = [at(f"prob{i}", [P, NC], F32, T + 2 * K * i) for i in range(2)]
        prob_t = [at(f"prob_t{i}", [P, 4, P], F32, T + 4 * K + 2 * K * i) for i in range(2)]
        relu = [at(f"relu{i}", [P, NC], F32, T + 2 * K * i) for i in range(2)]
        hid = [at(f"hid{i}", [P, NC], F32, T + 4 * K + 2 * K * i) for i in range(2)]
        upad = at("upad", [P, 544], F32, T)
        wsum = [at(f"wsum{i}", [P, 544], F32, T + 2176 * (i + 1)) for i in range(2)]
        ident = place("ident", [P, P], F32)
        identb = place("identb", [P, P], BF16)
        J = top[0]
        junk = place("junk", [P, D], BF16)
        v_a = at("v_a", [P, TT, P], F32, J)
        pool_w = at("pool_w", [P, 4, P], F32, J)
        causal = place("causal", [P, P], BF16)
        window = place("window", [P, 3, 256], BF16)
        st = place("st", [P, 4, 32], F32)
        half_sq = place("half_sq", [P, TT], F32)
        hst = place("hst", [P, 4, NH], F32)
        nmax = place("nmax", [P, NH], F32)
        den = place("den", [P, 2 * NH], F32)
        rden = place("rden", [P, 2 * NH], F32)
        gains = place("gains", [P, 4], F32)
        cvec = place("cvec", [P, 2, KT], F32)
        csil = place("csil", [P, 2, KT], F32)
        ctmp = place("ctmp", [P, 2, KT], F32)
        flog = place("flog", [P, TT, NH], F32)
        b_f = place("b_f", [NH, 1], F32)
        sink = place("sink", [1, NH], F32)
        sink_rest = place("sink_rest", [1, NH], F32)
        sink_parts = place("sink_parts", [1, 3, NH], BF16)
        ones_row = place("ones_row", [1, P], BF16)
        ones_col = place("ones_col", [P, 1], F32)
        ones_r = place("ones_r", [P, 1], F32R)
        pscale = place("pscale", [P, 4], F32)
        edge = place("edge", [P, 4, 16], F32)
        E = top[0]
        gain1 = at("gain1", [P, D], F32, E)
        alibi = at("alibi", [P, NH, 256], BF16, E)
        k_a = at("k_a", [P, 2, S], F32, E + 4 * K)
        c_parts = at("c_parts", [CR, S], F32R, E + 8 * K)
        q_pad1 = at("q_pad1", [P, 4, P], F32, E + 10 * K)
        negsel = at("negsel", [CR, NH, P], F32R, E + 12 * K)
        gain2 = at("gain2", [P, D], F32, E)
        mod_rows_t = at("mod_rows_t", [33, MB, NC], F32, E)
        b_row = mod_rows_t[0:1]
        mod_row = [mod_rows_t[0:1], mod_rows_t[32:33]]
        mod_hi = [at(f"mod_hi{j}", [P, NC], F32R, E + 8 * K + 2 * K * j) for j in range(2)]
        mod_gain = at("mod_gain", [P, D], F32, E)
        cmod_scale = at("cmod_scale", [P, D], F32, E + 4 * K)
        cmod_shift = at("cmod_shift", [P, D], F32, E + 8 * K)
        mod_scale = at("mod_scale", [P, D], F32, E + 12 * K)
        mod_shift = at("mod_shift", [P, D], F32, E + 4 * K)
        rpb_run = at("rpb_run", [P, NH, RUN], F32, E)
        k_c = at("k_c", [P, 4, CTX], F32, E + 8512)
        v_c = at("v_c", [P, CT, S], F32, E + 8512 + 4 * K)
        fin_gate = at("fin_gate", [P, D], F32, E)
        fin_gain = at("fin_gain", [P, D], F32, E + 4 * K)
        assert E + 17 * K <= nc.sbuf_usable_end, (E, nc.sbuf_usable_end)

        mods = nc.dram_tensor("mods", (2, 12 * NC), F32, kind="Internal").ap()

        def ps(name):
            return ctx.enter_context(nc.psum_tensor(name, [P, NC], F32))

        gp = [ps(f"gemm{i}") for i in range(4)]
        aux = [ps(f"aux{i}") for i in range(4)]

        sems = {}

        def sem(name):
            sems[name] = ctx.enter_context(nc.semaphore(name))
            return sems[name]

        x_loaded = [sem(f"x_loaded{m}") for m in range(TT)]
        ident_loaded = sem("ident_loaded")
        gain1_loaded, gain2_loaded = sem("gain1_loaded"), sem("gain2_loaded")
        heads_loaded, vec_loaded = sem("heads_loaded"), sem("vec_loaded")
        alibi_loaded, negsel_loaded = sem("alibi_loaded"), sem("negsel_loaded")
        mod_loaded, cmod_loaded, shift_loaded = sem("mod_loaded"), sem("cmod_loaded"), sem("shift_loaded")
        cx_loaded = [sem(f"cx_loaded{m}") for m in range(CT)]
        rpb_loaded, pool_loaded = sem("rpb_loaded"), sem("pool_loaded")
        tail_loaded, fin_loaded = sem("tail_loaded"), sem("fin_loaded")
        v_shifted, out_stored = sem("v_shifted"), sem("out_stored")
        raw_loaded = [sem(f"raw_loaded{q}") for q in range(UQ)]
        hi_split, unit_split = sem("hi_split"), sem("unit_split")
        gemm_done, gemm_free = sem("gemm_done"), sem("gemm_free")
        ones_ready, negsel_ready = sem("ones_ready"), sem("negsel_ready")
        ssq_done, ms_done, ln_done, rs0_done, rs_done = (sem(n) for n in (
            "ssq_done", "ms_done", "ln_done", "rs0_done", "rs_done"))
        xr_step, xr_ready = sem("xr_step"), sem("xr_ready")
        xr_turned, xt_hi_done, xt_lo_done = sem("xr_turned"), sem("xt_hi_done"), sem("xt_lo_done")
        hsq_done, hms_done, hln_done, hrs0_done, hrs_done = (sem(n) for n in (
            "hsq_done", "hms_done", "hln_done", "hrs0_done", "hrs_done"))
        qn_turned, qk_stored = sem("qn_turned"), sem("qk_stored")
        v_copied, k_scaled, f_turned, f_step, f_act = (sem(n) for n in (
            "v_copied", "k_scaled", "f_turned", "f_step", "f_act"))
        c_hi_done, c_ready = sem("c_hi_done"), sem("c_ready")
        score_done, bias_added, max_done, exp_done = (sem(n) for n in (
            "score_done", "bias_added", "max_done", "exp_done"))
        turned, turn_read, turn_hi, pv_done, rden_done, heads_out = (sem(n) for n in (
            "turned", "turn_read", "turn_hi", "pv_done", "rden_done", "heads_out"))
        pads_clear, q_padded = sem("pads_clear"), sem("q_padded")
        relu_done, hid_ready, hid_hi, hid_lo = (sem(n) for n in ("relu_done", "hid_ready", "hid_hi", "hid_lo"))
        silu_step, silu_act, wm_used, mod_summed, mod_rowed, mod_stored = (sem(n) for n in (
            "silu_step", "silu_act", "wm_used", "mod_summed", "mod_rowed", "mod_stored"))
        mod_hi_done, mod_split = sem("mod_hi_done"), sem("mod_split")
        wm_loaded = [sem(f"wm_loaded{i}") for i in range(2)]
        b_loaded = sem("b_loaded")
        pool_step, pool_done, pool_mixed, pool_hi = (sem(n) for n in (
            "pool_step", "pool_done", "pool_mixed", "pool_hi"))
        pool_scaled, pool_lo = sem("pool_scaled"), sem("pool_lo")
        mod_made, tail_step, fin_step = sem("mod_made"), sem("tail_step"), sem("fin_step")

        GATE_CREDIT = 1

        @block_fn(nc, ctx, "sync")
        def _(sp):
            def small(dst, src, s):
                sp.dma_start(dst, src).then_inc(s, 16)

            def x_tile(m):
                sp.dma_start(x[:, m, :], t["x"][m * P:(m + 1) * P, :]).then_inc(x_loaded[m], 16)

            x_tile(0)
            small(ident[:], t["c_ident"], ident_loaded)
            x_tile(1)

            def unit(q, src, width, wait):
                if wait is not None:
                    sp.wait_ge(unit_split, wait)
                sp.dma_start(raw[q][:, :, 0:width], src).then_inc(raw_loaded[q], 16)

            def rows(w, r0, q):
                return w[r0 + q * UK * P:r0 + (q + 1) * UK * P, :].rearrange("(k p) n -> p k n", p=P)

            def slab(s, w, c0, width):
                for q in range(UQ):
                    wait = 4 * (s - 1) + q + 1 if s else None
                    unit(q, rows(w, 0, q)[:, :, c0:c0 + width], width, wait)
                    if s == 0 and q in (1, 3):
                        x_tile(2 + q // 2)

            for s, (c0, width) in enumerate(IN1_COLS):
                if s == 1:
                    small_loads = (
                        (gains[0:HD, 0:1], t["q_norm_a"].rearrange("(p a) -> p a", a=1), heads_loaded),
                        (gains[HD:P, 0:1], t["q_norm_a"].rearrange("(p a) -> p a", a=1), heads_loaded),
                        (gains[0:HD, 1:2], t["k_norm_a"].rearrange("(p a) -> p a", a=1), heads_loaded),
                        (gains[HD:P, 1:2], t["k_norm_a"].rearrange("(p a) -> p a", a=1), heads_loaded),
                        (gains[0:HD, 2:3], t["q_norm_b"].rearrange("(p a) -> p a", a=1), heads_loaded),
                        (gains[HD:P, 2:3], t["q_norm_b"].rearrange("(p a) -> p a", a=1), heads_loaded),
                        (gains[0:HD, 3:4], t["k_norm_b"].rearrange("(p a) -> p a", a=1), heads_loaded),
                        (gains[HD:P, 3:4], t["k_norm_b"].rearrange("(p a) -> p a", a=1), heads_loaded),
                        (b_f[:], t["b_forget"].rearrange("(p a) -> p a", a=1), vec_loaded),
                        (sink[:], t["sink_logits"].rearrange("(a n) -> a n", a=1), vec_loaded),
                        (cvec[:, 0, :], t["c"], vec_loaded),
                        (cvec[:, 1, :], t["c_ctx"], vec_loaded),
                        (identb[:], t["c_identb"], vec_loaded),
                        (causal[:], t["c_causal"], vec_loaded),
                        (window[:], t["c_window"], vec_loaded),
                        (edge[:], t["c_edge"], vec_loaded),
                        (pscale[:], t["pool_scale"], vec_loaded),
                        (sel_raw[:].rearrange("h g p -> h (g p)"), t["c_negsel"], negsel_loaded),
                    )
                    for q in range(UQ):
                        src = rows(t["w_in"], 0, q)
                        for args in small_loads[5 * q:5 * (q + 1)]:
                            small(*args)
                        sp.wait_ge(unit_split, q + 1)
                        sp.dma_start(raw[q][:, :, 0:256], src[:, :, c0:c0 + 256]).then_inc(raw_loaded[q], 16)
                        sp.dma_start(raw[q][:, :, 256:KV_W], src[:, :, 2304:2312]).then_inc(raw_loaded[q], 16)
                else:
                    slab(s, t["w_in"], c0, width)
            for j in range(N_OUT):
                slab(SLAB_OUT1 + j, t["w_out"], j * NC, NC)

            def mlp(s0, up, down):
                with sp.Fori(0, NCH) as i:
                    for a in range(2):
                        for q in range(UQ):
                            src = rows(up, 0, q)[:, :, bass.ds(i * D + a * NC, NC)]
                            unit(q, src, NC, i * 16 + (4 * (s0 + a - 1) + q + 1))
                    down_r = down.rearrange("(c u k p) n -> c u p k n", c=NCH, k=UK, p=P)
                    for a in range(2):
                        for q in range(UQ):
                            src = down_r[bass.ds(i, 1), q, :, :, a * NC:(a + 1) * NC]
                            src = src.rearrange("o p k n -> (o p) k n")
                            unit(q, src, NC, i * 16 + (4 * (s0 + a + 1) + q + 1))

            mlp(SLAB_MLP1, t["w_up"], t["w_down"])
            for j, c0 in enumerate((0, 512, 1024, 1536)):
                slab(SLAB_IN2 + j, t["w_in_2"], c0, NC)
            for j in range(N_OUT):
                slab(SLAB_OUT2 + j, t["w_out_2"], j * NC, NC)
            mlp(SLAB_MLP2, t["w_mlp_in_2"], t["w_mlp_out_2"])
            for m in range(TT):
                for j in range(2):
                    cols = slice(j * NC, (j + 1) * NC)
                    sp.wait_ge(fin_step, 2 * m + j + 1)
                    sp.dma_start(out[m * P:(m + 1) * P, cols], x[:, m, cols]).then_inc(out_stored, 16)
            sp.wait_ge(out_stored, 16 * 2 * TT)

        @block_fn(nc, ctx, "gpsimd")
        def _(pool):
            def low(s, q, width, wait):
                pool.wait_ge(hi_split, wait)
                ks = slice(UK * q, UK * (q + 1))
                pool.tensor_tensor(w_lo[s % 2][:, ks, 0:width], raw[q][:, :, 0:width],
                                   w_hi[s % 2][:, ks, 0:width].bitcast(F32), ALU.subtract).then_inc(unit_split, 1)

            def lows(first, slabs):
                with pool.Fori(0, slabs // 2) as i:
                    for a in range(2):
                        for q in range(UQ):
                            low(first + a, q, NC, i * 8 + (4 * (first + a) + q + 1))
                if slabs % 2:
                    for q in range(UQ):
                        low(first + slabs - 1, q, NC, 4 * (first + slabs - 1) + q + 1)

            def clear_pads(q_pad, count):
                pool.memset(q_pad[:], 0.0).then_inc(pads_clear, 1)
                pool.wait_ge(pads_clear, count)

            def pad_queries(q_pad, i, i0, q):
                if i >= 4:
                    pool.wait_ge(score_done, i0 + i - 3)
                o = HD * (i % 2)
                pool.tensor_copy(q_pad[o:o + HD, i % 4, :], q).then_inc(q_padded, 1)
                pool.wait_ge(q_padded, i0 + i + 1)

            clear_pads(q_pad1, 1)
            for s in range(N_IN1 + 1):
                for q in range(UQ):
                    low(s, q, KV_W if s == 1 else NC, 4 * s + q + 1)
            pool.wait_ge(qk_stored, 16)
            for i, (n, kind, h) in enumerate(U1):
                o = HD * (h % 2)
                pad_queries(q_pad1, i, 0, (q_b if kind else q_a)[o:o + HD, h // 2, n * P:(n + 1) * P])
            lows(SLAB_OUT1 + 1, SLAB_OUT2 - SLAB_OUT1)
            pool.wait_ge(gemm_done, TILE_OUT2 - TT)
            clear_pads(q_pad2, 2)
            pool.wait_ge(gemm_free, freed(TILE_IN2 + 7))
            for i, (n, h) in enumerate(U2):
                o = HD * (h % 2)
                pad_queries(q_pad2, i, len(U1), q_2[o:o + HD, h // 2, n * P:(n + 1) * P])
                if i - 4 in SPLIT_IN_ATTENTION:
                    q = SPLIT_IN_ATTENTION.index(i - 4)
                    low(SLAB_OUT2 + 1, q, NC, 4 * (SLAB_OUT2 + 1) + q + 1)
                    pool.wait_ge(unit_split, 4 * (SLAB_OUT2 + 1) + q + 1)
                if i - 4 in POOL_SPLIT_IN:
                    j = POOL_SPLIT_IN.index(i - 4)
                    pool.wait_ge(pool_hi, 1)
                    pool.tensor_tensor(xt_lo[:, j, :], pooled[:, j, :], xt_hi[:, j, :].bitcast(F32),
                                       ALU.subtract).then_inc(pool_lo, 1)
                    pool.wait_ge(pool_lo, j + 1)
            lows(SLAB_MLP2, SLABS - SLAB_MLP2)

        @block_fn(nc, ctx, "scalar")
        def _(act):
            tally = Tally()

            def did(ins, s):
                ins.then_inc(s, 1)
                act.wait_ge(s, tally.up(s))

            def load(dst, src, s):
                act.dma_start(dst, src).then_inc(s, 16)

            def spread(v, n=D):
                return v.partition_broadcast(P)

            act.preload_act_table_set("natural_log_exp_and_others")
            load(gain1[:], spread(t["attn_norm_g"]), gain1_loaded)
            def high(s, q, width=NC, loaded=None, free=None):
                act.wait_ge(raw_loaded[q], loaded)
                if free is not None:
                    act.wait_ge(gemm_done, free)
                act.activation(w_hi[s % 2][:, UK * q:UK * (q + 1), 0:width], raw[q][:, :, 0:width],
                               ACT.Copy).then_inc(hi_split, 1)

            def arrived(s):
                return 16 * (s + 1) + (16 if s >= 1 else 0)

            def high_of(s, q):
                high(s, q, KV_W if s == 1 else NC, arrived(s), slab_end(s - 2) if s >= 2 else None)

            def squares(ready, src, dst):
                if ready is not None:
                    act.wait_ge(*ready)
                did(act.activation(junk[:, 0:src.shape[-1]], src, ACT.Square, accum_out=dst), ssq_done)

            def first_root(k):
                act.wait_ge(ms_done, k + 1)
                did(act.activation(st[:, 2, k:k + 1], st[:, 1, k:k + 1], ACT.Ln, scale=-LN_SCALE), ln_done)
                did(act.activation(st[:, 3, k:k + 1], st[:, 2, k:k + 1], ACT.Exp, scale=-0.5), rs0_done)

            def stat(k, ready, src):
                squares(ready, src, st[:, 0, k:k + 1])
                first_root(k)

            def xt_high(n, cols, permute=False, dst=None):
                for half in range(2):
                    act.wait_ge(xr_turned, 2 * n + half + 1)
                    did(act.activation(token_cols(xt_hi if dst is None else dst, half, cols, permute),
                                       bank_cols(aux[(2 * n + half) % 4], permute), ACT.Copy), xt_hi_done)

            for m in range(TT):
                stat(STAT_N1 + m, (x_loaded[m], 16), x[:, m, :])
                if m in (1, 2):
                    high_of(0, 2 * m - 2)
                    high_of(0, 2 * m - 1)
                if m >= 1:
                    xt_high(NT_1 + m - 1, m - 1)
            xt_high(NT_1 + 3, 3)
            act.wait_ge(xr_ready, 4)
            load(alibi[:], t["c_alibi"], alibi_loaded)
            act.wait_ge(vec_loaded, 16 * 9)
            did(act.activation(ctmp[:], cvec[:], ACT.Exp, scale=-1.0), silu_act)
            act.wait_ge(negsel_loaded, 16)
            did(act.activation(negsel[:], sel_raw[:], ACT.Copy), negsel_ready)

            act.wait_ge(heads_loaded, 16 * 8)

            def head_gain(u):
                kind, m = u // 4, u % 4
                dst = (q_a, k_a, q_b, k_b)[kind]
                pairs = 2 if kind == 1 else 4
                act.wait_ge(qn_turned, u + 1)
                did(act.activation(dst[:, 0:pairs, m * P:(m + 1) * P],
                                   aux[u % 4][:, 0:pairs * P].rearrange("p (h s) -> p h s", h=pairs),
                                   ACT.Copy, scale=gains[:, kind:kind + 1]), qk_stored)

            for g in range(4 * N_IN1):
                s, m = g // 4, g % 4
                if m < 2:
                    high_of(s + 1, 2 * m)
                    high_of(s + 1, 2 * m + 1)
                if g < 16:
                    heads = 2 if s == 1 else NH
                    act.wait_ge(gemm_done, g + 1)
                    if g >= 2:
                        act.wait_ge(hms_done, g - 1)
                    did(act.activation(qsq[g % 2][:, 0:heads * HD], gp[g % 4][:, 0:heads * HD], ACT.Square), hsq_done)
                    act.wait_ge(hms_done, g + 1)
                    did(act.activation(hst[:, 2, 0:heads], hst[:, 1, 0:heads], ACT.Ln,
                                       scale=-LN_SCALE), hln_done)
                    did(act.activation(hst[:, 3, 0:heads], hst[:, 2, 0:heads], ACT.Exp, scale=-0.5), hrs0_done)
                if s == 1:
                    did(act.activation(v_a[:, m, :], gp[g % 4][:, P:2 * P], ACT.Copy), v_copied)
                    did(act.activation(flog[:, m, :], gp[g % 4][:, 256:KV_W], ACT.Copy), v_copied)
                if 2 <= g <= 17:
                    head_gain(g - 2)
                if g == 12:
                    act.wait_ge(f_step, 3)
                    did(act.activation(frow[0:NH, 3, :], frow[0:NH, 2, :], ACT.Exp, scale=-1.0), f_act)
                    act.wait_ge(f_step, 4)
                    did(act.activation(frow[0:NH, 3, :], frow[0:NH, 3, :], ACT.Ln), f_act)
                if g == 13:
                    act.wait_ge(f_step, 8)
                    did(act.activation(c_parts[:], frow[:, 0, :], ACT.Copy), c_hi_done)
                    did(act.activation(c_parts[0:NH, :], frow[0:NH, 5, :], ACT.Copy), c_hi_done)

            def exp_unit(i, cols, column):
                act.wait_ge(max_done, i + 1)
                if i >= 2:
                    act.wait_ge(turned, turn[("T", i - 2)] + 1)
                if i >= 16:
                    act.wait_ge(rden_done, i // 8 - 1)
                lo, hi = cols
                did(act.activation(prob[i % 2][:, lo:hi] if hi <= NC else None, gp[i % 4][:, lo:hi], ACT.Exp,
                                   bias=nmax[:, i % 8:i % 8 + 1], accum_out=den[:, column:column + 1]), exp_done)

            turn = TURN1
            for i, step in enumerate(STEPS1):
                if i < len(U1):
                    n, kind, h = U1[i]
                    exp_unit(i, score_cols(n, kind), i % 16)
                for what, k in step:
                    if what == "M":
                        for half in range(2):
                            w = turn[("M", k, half)]
                            act.wait_ge(turned, w + 1)
                            did(act.activation(xt_hi[:, 4 * half:4 * half + 4, k * P:(k + 1) * P],
                                               aux[w % 2][:].rearrange("p (k s) -> p k s", k=4), ACT.Copy), turn_hi)
            load(gain2[:], spread(t["mlp_norm_g"]), gain2_loaded)

            for j in range(N_OUT):
                for m in range(TT):
                    high_of(SLAB_OUT1 + j + 1, m)
                    if j:
                        stat(STAT_N2 + m, (gemm_free, TILE_OUT1 + 4 * j + m + 1), x[:, m, :])
                        if m:
                            xt_high(NT_2 + m - 1, m - 1)
            xt_high(NT_2 + 3, 3)

            def mlp(s0, t0, up0, mod, last_down):
                def split(c, i):
                    s, q = s0 + c // 4 + 1, c % 4
                    act.wait_ge(raw_loaded[q], i * 64 + arrived(s))
                    act.wait_ge(gemm_done, i * 16 + slab_end(s - 2))
                    act.activation(w_hi[s % 2][:, UK * q:UK * (q + 1), :], raw[q][:, :, :],
                                   ACT.Copy).then_inc(hi_split, 1)

                def squared_relu(c, i):
                    act.wait_ge(gemm_done, i * 16 + (t0 + c + 1))
                    if c >= 2:
                        act.wait_ge(hid_ready, i * 8 + (up0 + c - 1))
                        act.wait_ge(hid_hi, i * 8 + (up0 + c - 1))
                    act.activation(relu[c % 2][:], gp[(t0 + c) % 4][:], ACT.Relu).then_inc(relu_done, 1)
                    act.wait_ge(relu_done, i * 8 + (up0 + c + 1))
                    act.activation(ht_hi[:, c, :], relu[c % 2][:], ACT.Square).then_inc(hid_hi, 1)

                def up(i, mod):
                    for c in range(4):
                        split(c, i)
                    for c in range(8):
                        if c >= 4:
                            split(c, i)
                        squared_relu(c, i)
                        if mod:
                            mod_loads(c, i)
                            if c in MOD_SPLIT_IN:
                                mod_high(MOD_SPLIT_IN.index(c), i)
                    act.wait_ge(hid_ready, i * 8 + (up0 + 8))
                    act.wait_ge(hid_hi, i * 8 + (up0 + 8))

                def chunk(i, mod):
                    if mod:
                        act.wait_ge(wm_used, before(i, 2 * MB_UNITS) + GATE_CREDIT)
                        for u in range(2):
                            wm_load(u, i)
                    up(i, mod)
                    for c in range(8, 16):
                        split(c, i)
                        if mod:
                            mod_loads(c, i)
                            if c in MOD_SPLIT_IN:
                                mod_high(MOD_SPLIT_IN.index(c), i)
                    if mod:
                        act.wait_ge(mod_rowed, before(i, MB) + vectors(i) * MB)
                        for j in range(vectors(i)):
                            act.dma_start(mods[j:j + 1, bass.ds(i * MB * NC, MB * NC)],
                                          mod_row[j].rearrange("o a n -> o (a n)")).then_inc(mod_stored, 16)

                chunk(0, mod)
                with act.Fori(1, NCH - 1) as i:
                    chunk(i, mod)
                if mod:
                    act.wait_ge(mod_stored, 16 * NCH)
                    first_loads()
                up(NCH - 1, False)
                last_down(lambda c: split(c, NCH - 1))

            def mod_loads(c, i):
                if c == 2:
                    if not isinstance(i, int):
                        act.wait_ge(mod_stored, before(i, 16))
                    act.dma_start(b_row.rearrange("o a n -> o (a n)"),
                                  t["b_mod"].rearrange("(a n) -> a n", a=1)[:, bass.ds(i * MB * NC, MB * NC)]
                                  ).then_inc(b_loaded, 16)
                if c >= 1:
                    for u in range(mod_units(c - 2) + 2, min(mod_units(c - 1) + 2, MB_UNITS)):
                        act.wait_ge(wm_used, before(i, 2 * MB_UNITS) + (GATE_CREDIT + 2 * vectors(i) * (u - 1)))
                        wm_load(u, i)

            def mod_high(k, i):
                act.wait_ge(wm_used, before(i, 2 * MB_UNITS) + (GATE_CREDIT + KT * vectors(i) * (k + 1)))
                if k or not isinstance(i, int):
                    act.wait_ge(mod_summed, i * MB + k)
                for j in range(vectors(i)):
                    act.activation(mod_hi[j][:], mod_acc[j][k % 2][:], ACT.Copy).then_inc(mod_hi_done, 1)

            def wm_load(u, i):
                src = t["w_mod"].rearrange("(u k p) n -> u p k n", k=UK, p=P)[
                    u % 4, :, :, bass.ds(i * MB * NC + (u // 4) * NC, NC)]
                act.dma_start(wm[u % 2][:], src).then_inc(wm_loaded[u % 2], 16)

            def mod(j, k):
                return spread(mods[j, k * D:(k + 1) * D])

            def first_loads():
                load(mod_gain[:], spread(t["g_pre_mix"]), cmod_loaded)
                load(cmod_scale[:], mod(1, 1), cmod_loaded)
                load(cmod_shift[:], mod(1, 0), cmod_loaded)
                load(mod_scale[:], mod(0, 1), mod_loaded)

            def norms_of_block_2(split):
                act.wait_ge(hid_lo, 8 * NCH)
                for m in range(CT):
                    load(xr[m][:], t["ctx"][m * P:(m + 1) * P, :], cx_loaded[m])
                for m in range(CT + 1):
                    if m < 2:
                        split(8 + 2 * m)
                        split(9 + 2 * m)
                    if m < CT:
                        stat(STAT_CTX + m, (cx_loaded[m], 16), xr[m][:])
                    if 1 <= m <= CT:
                        xt_high(NT_CTX + m - 1, m - 1, False, ct_hi)
                    if m == CT:
                        act.wait_ge(xr_ready, NT_CTX + CT)
                        load(mod_shift[:], mod(0, 0), shift_loaded)
                for m in range(TT):
                    if m < 2:
                        split(12 + 2 * m)
                        split(13 + 2 * m)
                    stat(STAT_N3 + m, (gemm_free, freed(TILE_IN2 - TT + m)), x[:, m, :])
                    if m == TT - 1:
                        high_of(SLAB_IN2 + 1, 0)
                        high_of(SLAB_IN2 + 1, 1)
                    if m:
                        xt_high(NT_3 + m - 1, m - 1, True)
                high_of(SLAB_IN2 + 1, 2)
                high_of(SLAB_IN2 + 1, 3)
                xt_high(NT_3 + 3, 3, True)

            mlp(SLAB_MLP1, TILE_MLP1, 0, True, norms_of_block_2)

            act.wait_ge(xr_ready, NT_3 + TT)
            for b in range(2):
                for h in range(NH):
                    off = RPB_LEN - 1 - (RPAD + h * RPH * RPW + (KH - 1) * RPW - 1 + RUN - 1) + 8 * b
                    act.dma_start(rpb_run[64 * b:64 * b + 64, h, :],
                                  bass.AP(tensor=t["rpb"].tensor, offset=off, ap=[[RPW, GR], [1, 8], [1, RUN]])
                                  ).then_inc(rpb_loaded, 16)
            load(pool_w[:], t["pool_w"].rearrange("g c d -> c g d"), pool_loaded)
            for s in (SLAB_IN2 + 2, SLAB_IN2 + 3, SLAB_OUT2):
                for q in range(UQ):
                    high_of(s, q)
            act.wait_ge(gemm_free, freed(TILE_OUT2 - 1))
            load(v_odd[0:64, :, :], v_2[64:P, 0:TT - 1, :], v_shifted)
            load(v_odd[64:P, :, :], v_2[0:64, 1:TT, :], v_shifted)

            turn = TURN2
            t0, e0, d0 = len(TURN1), len(U1), 2 * TT
            for i, step in enumerate(STEPS2):
                if i < len(U2):
                    k = e0 + i
                    act.wait_ge(max_done, k + 1)
                    if i >= 2:
                        act.wait_ge(turned, t0 + turn[("T", i - 2)] + 1)
                    if i >= 16:
                        act.wait_ge(rden_done, d0 + i // 8 - 1)
                    did(act.activation(prob[i % 2][:], gp[i % 4][:], ACT.Exp, bias=nmax[:, i % 8:i % 8 + 1],
                                       accum_out=den[:, i % 16:i % 16 + 1]), exp_done)
                if i == POOL_SPLIT_IN[0]:
                    act.wait_ge(pool_scaled, 4)
                    did(act.activation(xt_hi[:, 0:4, :], pooled[:], ACT.Copy), pool_hi)
                if i in SPLIT_IN_ATTENTION:
                    high_of(SLAB_OUT2 + 1, SPLIT_IN_ATTENTION.index(i))
                for what, k in step:
                    if what == "M":
                        w = turn[("M", k, 0)]
                        act.wait_ge(turned, t0 + w + 1)
                        did(act.activation(grid_cols(xt_hi, k), grid_bank(aux[w % 2]), ACT.Copy), turn_hi)

            load(mix_gate[:], mod(0, 2), tail_loaded)
            load(mix_gain[:], spread(t["g_post_mix"]), tail_loaded)
            load(mlp_scale[:], mod(0, 4), tail_loaded)
            load(mlp_shift[:], mod(0, 3), tail_loaded)
            load(mlp_gain2[:], spread(t["g_pre_mlp"]), tail_loaded)
            for e, (j, m) in enumerate(OUT2_ORDER):
                g = TILE_OUT2 + e
                k = STAT_TAIL + 2 * m
                if e == 5:
                    xt_high(NT_4, 0)
                if e == 6:
                    for q in range(UQ):
                        high_of(SLAB_MLP2, q)
                squares((gemm_done, g + 1), gp[g % 4][:], (st[:, 0, k:k + 1], half_sq[:, m:m + 1])[j])
                if j:
                    first_root(k)
                    if m >= 2:
                        xt_high(NT_4 + m - 1, m - 1)
                    stat(k + 1, (tail_step, 2 * (m + 1)), x[:, m, :])
            xt_high(NT_4 + 3, 3)
            load(fin_gate[:], mod(0, 5), fin_loaded)
            load(fin_gain[:], spread(t["g_post_mlp"]), fin_loaded)

            def last_norm(split):
                last = TILE_MLP2 + 16 * NCH - 2 * TT
                for c in range(8, 12):
                    split(c)
                    m = c - 8
                    squares((gemm_free, freed(last + m)), sub[:, m, 0:NC], half_sq[:, m:m + 1])
                for m in range(TT):
                    k = STAT_FIN + m
                    squares((gemm_free, freed(last + TT + m)), sub[:, m, NC:D], st[:, 0, k:k + 1])
                    first_root(k)

            mlp(SLAB_MLP2, TILE_MLP2, 8 * NCH, False, last_norm)

        @block_fn(nc, ctx, "tensor")
        def _(pe):
            def passes(bank, lhs, rhs, last_k=None, mid=None, by_unit=False, ks=range(KT)):
                for k in ks:
                    if by_unit and k % UK == 0:
                        pe.wait_ge(unit_split, k // UK + 1)
                    if k == KT // 2 and mid is not None:
                        mid()
                    if k == KT - 1 and last_k is not None:
                        pe.wait_ge(*last_k)
                    (lh, ll), (rh, rl) = lhs(k), rhs(k)
                    pe.matmul(bank, lh, rh, start=(k == 0), stop=False)
                    pe.matmul(bank, lh, rl, start=False, stop=False)
                    mm = pe.matmul(bank, ll, rh, start=False, stop=(k == KT - 1))
                return mm

            def product(g, bank, lhs, rhs, n, wait_free=True, mid=None, by_unit=False):
                if wait_free:
                    pe.wait_ge(gemm_free, freed(g - 4))
                passes(bank[:, 0:n], lhs, rhs, mid=mid, by_unit=by_unit).then_inc(gemm_done, 1)

            def early_and_late(nt, col, banks, early, late, wait_bank, turns, permute=False):
                pe.wait_ge(xt_lo_done, 2 * (nt + 2))
                for j in range(4):
                    wait_bank(j)
                    mid = (lambda: turn_rows(nt + 2 + turns.index(j), permute)) if j in turns else None
                    passes(early(banks[j]), col(j), lambda k: (early(xt_hi[:, k, :]), early(xt_lo[:, k, :])),
                           mid=mid)
                if 4 in turns:
                    turn_rows(nt + 3, permute)
                pe.wait_ge(xt_lo_done, 2 * (nt + TT))
                for j in range(4):
                    passes(late(banks[j]), col(j), lambda k: (late(xt_hi[:, k, :]), late(xt_lo[:, k, :]))
                           ).then_inc(gemm_done, 1)

            def tokens(hi, lo, m):
                return lambda k: (hi[:, k, m * P:(m + 1) * P], lo[:, k, m * P:(m + 1) * P])

            def all_tokens(hi, lo, n=S):
                return lambda k: (hi[:, k, 0:n], lo[:, k, 0:n])

            def w_cols(s, n=NC, c0=0):
                return lambda k: (w_hi[s % 2][:, k, c0:c0 + n], w_lo[s % 2][:, k, c0:c0 + n])

            def turn_rows(n, permute=False, grid=False):
                pe.wait_ge(xr_ready, n + 1)
                for half in range(2):
                    a = 2 * n + half
                    if a >= 4:
                        pe.wait_ge(xt_lo_done, a - 3)
                    for j in range(4):
                        src = xr[n % 2][:, (4 * half + j) * P:(4 * half + j + 1) * P]
                        dst = aux[a % 4][:, j * P:(j + 1) * P]
                        idn = ident[:]
                        if permute:
                            dst = dst.rearrange("p (b r c) -> p r b c", r=2, c=8)
                        mm = pe.transpose(dst, src, idn)
                    mm.then_inc(xr_turned, 1)

            pe.wait_ge(ident_loaded, 16)
            turn_rows(NT_1)
            turn_rows(NT_1 + 1)

            def split_ready(s):
                pe.wait_ge(unit_split, 4 * (s + 1))

            def turn_heads(u):
                pe.wait_ge(gemm_free, u + 1)
                if u >= 4:
                    pe.wait_ge(qk_stored, u - 3)
                pairs = 2 if u // 4 == 1 else 4
                for j in range(pairs):
                    mm = pe.transpose(aux[u % 4][:, j * P:(j + 1) * P], qn[u % 2][:, j * P:(j + 1) * P], ident[:])
                mm.then_inc(qn_turned, 1)

            def between(g):
                if g < TT - 2:
                    turn_rows(NT_1 + g + 2)
                if 2 <= g <= 17:
                    if g == 2:
                        pe.wait_ge(xt_lo_done, 2 * TT)
                    if g == 13:
                        pe.wait_ge(f_step, 1)
                    turn_heads(g - 2)
                if g == 11:
                    pe.wait_ge(v_copied, 2 * TT)
                    pe.wait_ge(qk_stored, 8)
                    for k in range(TT):
                        mm = pe.transpose(aux[3][0:NH, k * P:(k + 1) * P], flog[:, k, :], ident[:])
                    mm.then_inc(f_turned, 1)

            for g in range(4 * N_IN1):
                s, m = g // 4, g % 4
                if m == 0 and g:
                    split_ready(s)
                if g < 4:
                    pe.wait_ge(xt_lo_done, 2 * (NT_1 + m + 1))
                product(g, gp[g % 4], tokens(xt_hi, xt_lo, m), w_cols(s, KV_W if s == 1 else NC),
                        KV_W if s == 1 else NC, wait_free=g >= 4, mid=lambda: between(g), by_unit=g == 0)

            def out_product_1(j, m):
                g = TILE_OUT1 + 4 * j + m
                if m == 0:
                    split_ready(SLAB_OUT1 + j)
                if j == 0:
                    pe.wait_ge(turn_read, TURN1[("M", m, 1)] + 1)
                if j and m == 2:
                    pe.wait_ge(heads_out, 2 * TT)
                product(g, gp[g % 4], tokens(xt_hi, xt_lo, m), w_cols(SLAB_OUT1 + j), NC,
                        mid=(lambda: turn_rows(NT_2 + m - 2)) if j and m >= 2 else None)

            pe.wait_ge(pads_clear, 1)
            pe.wait_ge(qk_stored, 16)
            pe.wait_ge(negsel_ready, 1)
            pe.wait_ge(ones_ready, 2)
            pe.wait_ge(vec_loaded, 16 * 9)
            pe.wait_ge(alibi_loaded, 16)
            pe.wait_ge(silu_step, 8)
            for i, step in enumerate(STEPS1):
                if i < len(U1):
                    n, kind, h = U1[i]
                    bank = gp[i % 4]
                    if i >= 4:
                        pe.wait_ge(exp_done, i - 3)
                    else:
                        pe.wait_ge(gemm_free, 4 * N_IN1 - 3 + i)
                    pe.wait_ge(q_padded, i + 1)
                    if kind == 0:
                        lo = 0 if n else P
                        swap = 0 if (h // 4) == (h % 2) else 1
                        for part in range(3):
                            pe.matmul(bank[:, 256:257], ones_row[:], sink_parts[:, part, h:h + 1],
                                      start=(part == 0), stop=(part == 2))
                        pe.matmul(bank[:, lo:256], q_pad1[:, i % 4, :],
                                  k_a[:, swap, (n - 1) * P + lo:(n + 1) * P], start=True, stop=False)
                        mm = pe.matmul(bank[:, lo:256], identb[:], alibi[:, h, lo:256], start=False, stop=True)
                    else:
                        w = (n + 1) * P
                        if (n, h) == (0, 0):
                            pe.wait_ge(c_ready, 1)
                        pe.matmul(bank[:, 0:w], q_pad1[:, i % 4, :], k_b[:, h // 2, 0:w],
                                  start=True, stop=False)
                        pe.matmul(bank[:, 0:w], negsel[:, h, :], c_parts[:, 0:w], start=False, stop=False)
                        mm = pe.matmul(bank[:, w - P:w], identb[:], causal[:], start=False, stop=True)
                    mm.then_inc(score_done, 1)
                for what, k in step:
                    if what == "M" and k == TT - 1:
                        out_product_1(0, 0)
                    if what == "M":
                        pe.wait_ge(heads_out, 2 * (k + 1))
                        for half in range(2):
                            w = TURN1[("M", k, half)]
                            pe.wait_ge(turn_read, w - 1)
                            for j in range(4):
                                mm = pe.transpose(aux[w % 2][:, j * P:(j + 1) * P],
                                                  mixed[:, k, (4 * half + j) * P:(4 * half + j + 1) * P], ident[:])
                            mm.then_inc(turned, 1)
                        continue
                    n, kind, h = U1[k]
                    blocks = score_blocks(n, kind)
                    if what == "T":
                        w = TURN1[("T", k)]
                        pe.wait_ge(exp_done, k + 1)
                        if w >= 2:
                            pe.wait_ge(turn_read, w - 1)
                        for b in blocks:
                            mm = pe.transpose(aux[w % 2][:, b * P:(b + 1) * P],
                                              prob[k % 2][:, b * P:(b + 1) * P], ident[:])
                        mm.then_inc(turned, 1)
                    else:
                        pe.wait_ge(turn_read, TURN1[("T", k)] + 1)
                        if k % 8 == 0 and k >= 16:
                            pe.wait_ge(heads_out, k // 8 - 1)
                        for b in blocks:
                            v = (v_a[:, n - 1 + b, (h // 4) * HD:(h // 4 + 1) * HD] if kind == 0
                                 else v_b[:, b, h * HD:(h + 1) * HD])
                            mm = pe.matmul(aux[2 + (k // 8) % 2][:, h * HD:(h + 1) * HD],
                                           prob_t[k % 2][:, b, :], v, start=(b == blocks[0]), stop=(b == blocks[-1]))
                        mm.then_inc(pv_done, 1)

            for j in range(N_OUT):
                for m in range(TT):
                    if j or m:
                        out_product_1(j, m)

            def mlp(s0, t0, up0, nt, mod, turns, mid):
                f0 = freed(t0 - 1)

                def bank_free(c, i):
                    if 4 <= c < 12:
                        pe.wait_ge(relu_done, i * 8 + (up0 + c - 3))
                    else:
                        pe.wait_ge(gemm_free, i * 8 + (f0 + (c - 3 if c < 4 else c - 11)))

                def chunk(i, mod, mid, turns=None):
                    def weights(c):
                        if c % 4 == 0:
                            pe.wait_ge(unit_split, i * 16 + 4 * (s0 + c // 4 + 1))

                    weights(0)
                    if turns is not None:
                        early_and_late(nt, lambda j: w_cols(s0, P, j * P), [gp[(t0 + j) % 4] for j in range(4)],
                                       lambda ap: ap[:, 0:EARLY], lambda ap: ap[:, EARLY:S],
                                       lambda j: bank_free(j, i), turns)
                    for c in range(0 if turns is None else 4, 8):
                        weights(c)
                        bank_free(c, i)
                        passes(gp[(t0 + c) % 4][:], w_cols(s0 + c // 4, P, (c % 4) * P), all_tokens(xt_hi, xt_lo),
                               mid=(lambda: sum_mod(SUM_IN.index(c), i)) if mod and c in SUM_IN else None
                               ).then_inc(gemm_done, 1)
                    for c in range(8, 16):
                        weights(c)
                        bank_free(c, i)
                        if c == 8:
                            pe.wait_ge(hid_lo, i * 8 + (up0 + 7))
                        passes(gp[(t0 + c) % 4][:], tokens(ht_hi, ht_lo, c % 4), w_cols(s0 + c // 4),
                               (hid_lo, i * 8 + (up0 + 8)) if c == 8 else None,
                               (lambda: mid(c)) if mid is not None else
                               (lambda: sum_mod(SUM_IN.index(c), i)) if mod and c in SUM_IN else None
                               ).then_inc(gemm_done, 1)

                chunk(0, mod, None, turns)
                with pe.Fori(1, NCH - 1) as i:
                    chunk(i, mod, None)
                chunk(NCH - 1, False, mid)

            def sum_mod(k, i):
                pe.wait_ge(mod_split, before(i, MB) + vectors(i) * (k + 1))
                if k:
                    pe.wait_ge(mod_rowed, before(i, MB) + vectors(i) * k)
                for j in range(vectors(i)):
                    pe.matmul(aux[j][0:1, :], ones_r[:], mod_hi[j][:], start=True, stop=False)
                    mm = pe.matmul(aux[j][0:1, :], ones_r[:], mod_lo[j][k % 2][:], start=False, stop=True)
                mm.then_inc(mod_summed, 1)

            def turns_of_block_2(c):
                if c in (10, 11):
                    if c == 10:
                        pe.wait_ge(mod_rowed, MB * NCH)
                    turn_rows(NT_CTX + c - 10)
                elif c >= 14:
                    turn_rows(NT_3 + c - 14, permute=True)

            mlp(SLAB_MLP1, TILE_MLP1, 0, NT_2, True, (0, 1), turns_of_block_2)

            g = TILE_IN2

            def wait_bank(j):
                pe.wait_ge(gemm_free, freed(TILE_IN2 + j - 4))

            split_ready(SLAB_IN2)
            early_and_late(NT_3, lambda j: w_cols(SLAB_IN2, P, j * P), [gp[(g + j) % 4] for j in range(4)],
                           lambda ap: ap[:, 0:S].rearrange("p (b s) -> p b s", s=64)[:, :, 0:32],
                           lambda ap: ap[:, 0:S].rearrange("p (b s) -> p b s", s=64)[:, :, 32:64],
                           wait_bank, (0, 2), permute=True)
            g += 4
            split_ready(SLAB_IN2 + 1)
            for j in range(4):
                product(g, gp[g % 4], w_cols(SLAB_IN2 + 1, P, j * P), all_tokens(xt_hi, xt_lo), S)
                g += 1
            split_ready(SLAB_IN2 + 2)
            for j in range(4):
                product(g, gp[g % 4], w_cols(SLAB_IN2 + 2, P, j * P), all_tokens(xt_hi, xt_lo), S)
                g += 1
            for j in range(4):
                product(g, gp[g % 4], w_cols(SLAB_IN2 + 2, P, j * P), all_tokens(ct_hi, ct_lo, CTX), CTX)
                g += 1
            pe.wait_ge(pool_done, 4)
            pe.wait_ge(pool_loaded, 16)
            for j in range(4):
                mm = pe.matmul(aux[j][:], pool_w[:, j, :], pooled[:, j, :], start=True, stop=True)
                mm.then_inc(pool_mixed, 1)
            split_ready(SLAB_IN2 + 3)
            for m in range(CT):
                product(g, gp[g % 4], tokens(ct_hi, ct_lo, m), w_cols(SLAB_IN2 + 3), NC)
                g += 1
            for m in range(TT):
                product(g, gp[g % 4], tokens(xt_hi, xt_lo, m), w_cols(SLAB_IN2 + 3), NC)
                g += 1

            pe.wait_ge(pads_clear, 2)
            t0, e0, v0, h0 = len(TURN1), len(U1), len(U1), 2 * TT

            def out_product_2(e, ks=range(KT)):
                j, m = OUT2_ORDER[e]
                mm = passes(gp[(TILE_OUT2 + e) % 4][:], tokens(xt_hi, xt_lo, m), w_cols(SLAB_OUT2 + j), ks=ks,
                            mid={4: lambda: turn_rows(NT_4), 6: lambda: turn_rows(NT_4 + 1)}.get(e))
                if ks[-1] == KT - 1:
                    mm.then_inc(gemm_done, 1)

            def out_rows_ahead(e):
                if e == 0:
                    pe.wait_ge(pool_lo, 4)
                    pe.wait_ge(exp_done, e0 + len(U2))
                split_ready(SLAB_OUT2 + OUT2_ORDER[e][0])
                out_product_2(e, range(KT // 2))

            for i, step in enumerate(STEPS2):
                if i == 2:
                    pe.wait_ge(pool_scaled, 4)
                if i < len(U2):
                    n, h = U2[i]
                    pair, bank = h // 2, gp[i % 4]
                    if i >= 4:
                        pe.wait_ge(exp_done, e0 + i - 3)
                    else:
                        pe.wait_ge(gemm_free, freed(TILE_OUT2 - 1 - (TILE_OUT2 - 1 - i) % 4))
                    pe.wait_ge(q_padded, e0 + i + 1)
                    q = q_pad2[:, i % 4, :]
                    pe.matmul(bank[:, 0:256], q, k_2[:, pair, KSTART[n]:KSTART[n] + 256], start=True, stop=False)
                    pe.matmul(bank[:, 0:256], identb[:], window[:, (n + 1) // 2 if n < 3 else 2, :],
                              start=False, stop=True)
                    pe.matmul(bank[:, 256:512], q, k_c[:, pair, :], start=True, stop=True).then_inc(score_done, 1)
                for what, k in step:
                    if what == "M":
                        if k == TT - 1:
                            out_rows_ahead(0)
                        pe.wait_ge(heads_out, h0 + k + 1)
                        w = TURN2[("M", k, 0)]
                        pe.wait_ge(turn_read, t0 + w - 1)
                        for j in range(4):
                            dst = aux[w % 2][:, j * P:(j + 1) * P].rearrange("p (r b c) -> p b r c", b=2, c=8)
                            mm = pe.transpose(dst, attn_2[k % 2][:, j * P:(j + 1) * P], ident[:])
                        mm.then_inc(turned, 1)
                        continue
                    n, h = U2[k]
                    if what == "T":
                        w = TURN2[("T", k)]
                        pe.wait_ge(exp_done, e0 + k + 1)
                        if w >= 2:
                            pe.wait_ge(turn_read, t0 + w - 1)
                        for b in range(4):
                            mm = pe.transpose(aux[w % 2][:, b * P:(b + 1) * P],
                                              prob[k % 2][:, b * P:(b + 1) * P], ident[:])
                        mm.then_inc(turned, 1)
                    else:
                        pe.wait_ge(turn_read, t0 + TURN2[("T", k)] + 1)
                        if k % 8 == 0 and k >= 16:
                            pe.wait_ge(heads_out, h0 + k // 8 - 1)
                        cols = slice(h * HD, (h + 1) * HD)
                        if (n, h) == (1, 0):
                            pe.wait_ge(v_shifted, 32)
                        for b in range(4):
                            if b >= 2:
                                v = v_c[:, b - 2, cols]
                            elif KSTART[n] % P == 0:
                                v = v_2[:, KSTART[n] // P + b, cols]
                            else:
                                v = v_odd[:, KSTART[n] // P + b, cols]
                            mm = pe.matmul(aux[2 + (k // 8) % 2][:, cols], prob_t[k % 2][:, b, :], v,
                                           start=(b == 0), stop=(b == 3))
                        mm.then_inc(pv_done, 1)

            out_rows_ahead(1)
            pe.wait_ge(turn_read, t0 + TURN2[("M", TT - 1, 0)] + 1)
            for e in range(len(OUT2_ORDER)):
                if e >= 4:
                    pe.wait_ge(gemm_free, freed(TILE_OUT2 + e - 4))
                out_product_2(e, range(KT // 2 if e < 2 else 0, KT))
            mlp(SLAB_MLP2, TILE_MLP2, 8 * NCH, NT_4, False, (1, 3), None)

        @block_fn(nc, ctx, "vector")
        def _(dve):
            tally = Tally()

            def did(ins, s):
                ins.then_inc(s, 1)
                dve.wait_ge(s, tally.up(s))

            dve.memset(ones_col[:], 1.0)
            did(dve.memset(ones_row[:], 1.0), ones_ready)
            did(dve.tensor_copy(ones_r[:], ones_col[:]), ones_ready)

            def refine_heads(neg_ms, u, tmp):
                did(dve.tensor_tensor(tmp, neg_ms, u, ALU.mult), hrs_done)
                did(dve.tensor_tensor(tmp, tmp, u, ALU.mult), hrs_done)
                did(dve.scalar_tensor_tensor(u, tmp, 3 / LN_SCALE, u, ALU.add, ALU.mult), hrs_done)

            def mean_square(k, squares):
                dve.wait_ge(ssq_done, squares)
                did(dve.tensor_scalar(st[:, 1, k:k + 1], st[:, 0, k:k + 1], -1.0 / D, -EPS, ALU.mult, ALU.add),
                    ms_done)

            def refine(k):
                dve.wait_ge(rs0_done, k + 1)
                u = st[:, 3, k:k + 1]
                did(dve.tensor_scalar(st[:, 2, k:k + 1], st[:, 1, k:k + 1], u, u, ALU.mult, ALU.mult), rs_done)
                did(dve.scalar_tensor_tensor(u, st[:, 2, k:k + 1], 3 / LN_SCALE, u, ALU.add, ALU.mult), rs_done)

            def stat(k, squares=None):
                mean_square(k, k + 1 if squares is None else squares)
                refine(k)

            def scaled(n, k, src, gain, shift=None):
                if n >= 2:
                    dve.wait_ge(xr_turned, 2 * (n - 1))
                ins = dve.scalar_tensor_tensor(xr[n % 2][:], src, st[:, 3, k:k + 1], gain, ALU.mult, ALU.mult)
                if shift is None:
                    did(ins, xr_ready)
                else:
                    did(ins, xr_step)
                    did(dve.tensor_tensor(xr[n % 2][:], xr[n % 2][:], shift, ALU.add), xr_ready)

            def xt_low(n, cols, permute=False, dst=None):
                hi, lo = (xt_hi, xt_lo) if dst is None else dst
                for half in range(2):
                    dve.wait_ge(xt_hi_done, 2 * n + half + 1)
                    did(dve.tensor_tensor(token_cols(lo, half, cols, permute),
                                          bank_cols(aux[(2 * n + half) % 4], permute),
                                          token_cols(hi, half, cols, permute).bitcast(F32), ALU.subtract), xt_lo_done)

            dve.wait_ge(gain1_loaded, 16)
            for m in range(TT):
                stat(STAT_N1 + m)
                scaled(NT_1 + m, STAT_N1 + m, x[:, m, :], gain1[:])
                if m:
                    xt_low(NT_1 + m - 1, m - 1)
            xt_low(NT_1 + 3, 3)
            dve.wait_ge(silu_act, 1)
            did(dve.tensor_scalar(ctmp[:], ctmp[:], 1.0, None, ALU.add), silu_step)
            did(dve.reciprocal(csil[:], ctmp[:]), silu_step)
            did(dve.tensor_tensor(csil[:], csil[:], cvec[:], ALU.mult), silu_step)
            dve.wait_ge(vec_loaded, 16 * 9)
            rest = sink
            for part in range(3):
                did(dve.tensor_copy(sink_parts[:, part, :], rest[:]), silu_step)
                if part < 2:
                    did(dve.tensor_tensor(sink_rest[:], rest[:], sink_parts[:, part, :], ALU.subtract), silu_step)
                rest = sink_rest
            dve.wait_ge(heads_loaded, 16 * 8)
            did(dve.tensor_scalar(gains[:, 0:1], gains[:, 0:1], QSCALE, None, ALU.mult), silu_step)
            did(dve.tensor_scalar(gains[:, 2:3], gains[:, 2:3], QSCALE, None, ALU.mult), silu_step)

            for g in range(4 * N_IN1):
                s, m = g // 4, g % 4
                bank = gp[g % 4]
                dve.wait_ge(gemm_done, g + 1)
                if g >= 16:
                    did(dve.tensor_copy(v_b[:, m, :], bank[:]), gemm_free)
                    continue
                heads = 2 if s == 1 else NH
                dve.wait_ge(hsq_done, g + 1)
                did(dve.tensor_reduce(hst[:, 0, 0:heads], qsq[g % 2][:, 0:heads * HD].rearrange(
                    "p (h d) -> p h d", d=HD), AXX, ALU.add), rs_done)
                did(dve.tensor_scalar(hst[:, 1, 0:heads], hst[:, 0, 0:heads], -1.0 / HD, -EPS, ALU.mult, ALU.add),
                    hms_done)
                dve.wait_ge(hrs0_done, g + 1)
                refine_heads(hst[:, 1, 0:heads], hst[:, 3, 0:heads], hst[:, 2, 0:heads])
                if g >= 2:
                    dve.wait_ge(qn_turned, g - 1)
                if s == 1:
                    dve.wait_ge(v_copied, 2 * (m + 1))
                    k_in = bank[:, 0:P].rearrange("p (h d) -> p h d", d=HD)
                    scale = hst[:, 3, 0:2].unsqueeze(2).broadcast_to([P, 2, HD])
                    out_a = qn[g % 2][:, 0:P].rearrange("p (h d) -> p h d", d=HD)
                    first = qn[g % 2][:, P + HD:2 * P]
                    out_b = bass.AP(tensor=first.tensor, offset=first.offset,
                                    ap=[list(first.ap[0]), [-HD, 2], [1, HD]])
                    did(dve.tensor_tensor(out_a, k_in, scale, ALU.mult), k_scaled)
                    did(dve.tensor_tensor(out_b, k_in, scale, ALU.mult), gemm_free)
                else:
                    did(dve.tensor_tensor(qn[g % 2][:].rearrange("p (h d) -> p h d", d=HD),
                                          bank[:].rearrange("p (h d) -> p h d", d=HD),
                                          hst[:, 3, :].unsqueeze(2).broadcast_to([P, NH, HD]), ALU.mult), gemm_free)
                if g == 11:
                    dve.wait_ge(f_turned, 1)
                    dve.wait_ge(vec_loaded, 16 * 9)
                    did(dve.tensor_scalar(frow[0:NH, 0, :], aux[3][0:NH, :], b_f[:], None, ALU.add), f_step)
                    did(dve.tensor_scalar(frow[0:NH, 1, :], frow[0:NH, 0, :], -1.0, None, ALU.mult), f_step)
                    did(dve.tensor_tensor(frow[0:NH, 2, :], frow[0:NH, 0, :], frow[0:NH, 1, :], ALU.max), f_step)
                if g == 12:
                    dve.wait_ge(f_act, 1)
                    did(dve.tensor_scalar(frow[0:NH, 3, :], frow[0:NH, 3, :], 1.0, None, ALU.add), f_step)
                    dve.wait_ge(f_act, 2)
                    did(dve.scalar_tensor_tensor(frow[0:NH, 4, :], frow[0:NH, 0, :], 0.0, frow[0:NH, 3, :],
                                                 ALU.min, ALU.subtract), f_step)
                    did(dve.memset(frow[0:NH, 1, :], 1.0), f_step)
                    did(dve.tensor_tensor_scan(frow[0:NH, 5, :], frow[0:NH, 1, :], frow[0:NH, 4, :], 0.0,
                                               ALU.mult, ALU.add), f_step)
                    did(dve.memset(frow[:, 0, :], 0.0), f_step)
            dve.wait_ge(c_hi_done, 2)
            did(dve.tensor_tensor(c_parts[32:CR, :], frow[0:NH, 5, :], c_parts[0:NH, :].bitcast(F32),
                                  ALU.subtract), c_ready)

            def copy_turn(k, w, first, n_blocks, t0):
                dve.wait_ge(turned, t0 + w + 1)
                did(dve.tensor_copy(prob_t[k % 2][:, first:first + n_blocks, :],
                                    aux[w % 2][:, first * P:(first + n_blocks) * P].rearrange(
                                        "p (b s) -> p b s", b=n_blocks)), turn_read)

            def heads_tile(b, v0, e0, dst):
                dve.wait_ge(exp_done, e0 + 8 * b + 8)
                cols = slice(8 * (b % 2), 8 * (b % 2) + 8)
                did(dve.reciprocal(rden[:, cols], den[:, cols]), rden_done)
                dve.wait_ge(pv_done, v0 + 8 * b + 8)
                did(dve.tensor_tensor(dst.rearrange("p (h d) -> p h d", d=HD),
                                      aux[2 + b % 2][:].rearrange("p (h d) -> p h d", d=HD),
                                      rden[:, cols].unsqueeze(2).broadcast_to([P, NH, HD]), ALU.mult), heads_out)

            for i, step in enumerate(STEPS1):
                if i < len(U1):
                    n, kind, h = U1[i]
                    lo, hi = score_cols(n, kind)
                    dve.wait_ge(score_done, i + 1)
                    if i >= 8:
                        dve.wait_ge(exp_done, i - 7)
                    did(dve.tensor_reduce(nmax[:, i % 8:i % 8 + 1], gp[i % 4][:, lo:hi], AXX, ALU.max, negate=True),
                        max_done)
                for what, k in step:
                    if what == "T":
                        n, kind, h = U1[k]
                        blocks = score_blocks(n, kind)
                        if k >= 2:
                            dve.wait_ge(pv_done, k - 1)
                        copy_turn(k, TURN1[("T", k)], blocks[0], len(blocks), 0)
                    elif what == "V" and k % 8 == 7:
                        n, kind, h = U1[k]
                        heads_tile(k // 8, 0, 0, mixed[:, n, kind * S:(kind + 1) * S])
                    elif what == "M":
                        for half in range(2):
                            w = TURN1[("M", k, half)]
                            dve.wait_ge(turn_hi, 2 * k + half + 1)
                            hi_cols = xt_hi[:, 4 * half:4 * half + 4, k * P:(k + 1) * P]
                            did(dve.tensor_tensor(xt_lo[:, 4 * half:4 * half + 4, k * P:(k + 1) * P],
                                                  aux[w % 2][:].rearrange("p (k s) -> p k s", k=4),
                                                  hi_cols.bitcast(F32), ALU.subtract), turn_read)

            for j in range(N_OUT):
                for m in range(TT):
                    g = TILE_OUT1 + 4 * j + m
                    dve.wait_ge(gemm_done, g + 1)
                    cols = x[:, m, j * NC:(j + 1) * NC]
                    did(dve.tensor_tensor(cols, cols, gp[g % 4][:], ALU.add), gemm_free)
                    if j:
                        if m == 0:
                            dve.wait_ge(gain2_loaded, 16)
                        stat(STAT_N2 + m)
                        scaled(NT_2 + m, STAT_N2 + m, x[:, m, :], gain2[:])
                        if m:
                            xt_low(NT_2 + m - 1, m - 1)
            xt_low(NT_2 + 3, 3)

            def mlp(t0, acc, up0, mod, after, fresh=False):
                f0 = freed(t0 - 1)

                def chunk(i, mod, after, fresh=False):
                    for c in range(16):
                        bank = gp[(t0 + c) % 4]
                        if c < 8:
                            dve.wait_ge(relu_done, i * 8 + (up0 + c + 1))
                            if c >= 2:
                                dve.wait_ge(hid_lo, i * 8 + (up0 + c - 1))
                            dve.tensor_tensor(hid[c % 2][:], relu[c % 2][:], relu[c % 2][:], ALU.mult
                                              ).then_inc(hid_ready, 1)
                            dve.wait_ge(hid_hi, i * 8 + (up0 + c + 1))
                            dve.wait_ge(hid_ready, i * 8 + (up0 + c + 1))
                            dve.tensor_tensor(ht_lo[:, c, :], hid[c % 2][:], ht_hi[:, c, :].bitcast(F32),
                                              ALU.subtract).then_inc(hid_lo, 1)
                        else:
                            dve.wait_ge(gemm_done, i * 16 + (t0 + c + 1))
                            if c == 8:
                                dve.wait_ge(hid_lo, i * 8 + (up0 + 8))
                            cols = acc[:, c % 4, (c // 4 - 2) * NC:(c // 4 - 1) * NC]
                            if fresh:
                                dve.tensor_copy(cols, bank[:]).then_inc(gemm_free, 1)
                            else:
                                dve.tensor_tensor(cols, cols, bank[:], ALU.add).then_inc(gemm_free, 1)
                            if after is not None:
                                dve.wait_ge(gemm_free, i * 8 + (f0 + c - 7))
                                after(c)
                        if mod:
                            if c in SUM_IN:
                                mod_rows(SUM_IN.index(c), i)
                            if c in MOD_SPLIT_IN:
                                split_mod(MOD_SPLIT_IN.index(c), i)
                            for e in range(2 * vectors(i) * mod_units(c - 1), 2 * vectors(i) * mod_units(c)):
                                modulate(e, i)

                chunk(0, mod, None, fresh)
                with dve.Fori(1, NCH - 1) as i:
                    chunk(i, mod, None)
                dve.wait_ge(gemm_free, f0 + 8 * (NCH - 1))
                tally.up(gemm_free, 8 * NCH)
                chunk(NCH - 1, False, after)

            def modulate(e, i):
                nv = vectors(i)
                u, row, j = e // (2 * nv), e % (2 * nv) // nv, e % nv
                k, kt = u // UQ, (u % UQ) * UK + row
                acc = mod_acc[j][k % 2][:]
                w = wm[u % 2][:, row, :]
                if e % (2 * nv) == 0:
                    dve.wait_ge(wm_loaded[u % 2], i * (8 * MB_UNITS) + 16 * (u // 2 + 1))
                if e >= nv:
                    dve.wait_ge(wm_used, before(i, 2 * MB_UNITS) + (GATE_CREDIT + e - nv + 1))
                if kt == 0:
                    ins = dve.tensor_scalar(acc, w, csil[:, j, kt:kt + 1], None, ALU.mult)
                else:
                    ins = dve.scalar_tensor_tensor(acc, w, csil[:, j, kt:kt + 1], acc, ALU.mult, ALU.add)
                ins.then_inc(wm_used, 1)

            def split_mod(k, i):
                dve.wait_ge(mod_hi_done, before(i, MB) + vectors(i) * (k + 1))
                for j in range(vectors(i)):
                    dve.tensor_tensor(mod_lo[j][k % 2][:], mod_acc[j][k % 2][:], mod_hi[j][:].bitcast(F32),
                                      ALU.subtract).then_inc(mod_split, 1)

            def mod_rows(k, i):
                if k == 0:
                    dve.wait_ge(b_loaded, i * 16 + 16)
                dve.wait_ge(mod_summed, i * MB + (k + 1))
                for j in range(vectors(i))[::-1]:
                    if j == 0 and vectors(i) > 1:
                        dve.wait_ge(mod_rowed, before(i, MB) + (2 * k + 1))
                    dve.tensor_tensor(mod_row[j][:, k, :], aux[j][0:1, :], b_row[:, k, :], ALU.add
                                      ).then_inc(mod_rowed, 1)

            def norms_of_block_2(c):
                m = c - 8
                if m == 0:
                    dve.wait_ge(cmod_loaded, 48)
                    did(dve.scalar_tensor_tensor(cmod_scale[:], cmod_scale[:], 1.0, mod_gain[:], ALU.add, ALU.mult),
                        mod_made)
                    dve.wait_ge(mod_loaded, 16)
                    did(dve.scalar_tensor_tensor(mod_scale[:], mod_scale[:], 1.0, mod_gain[:], ALU.add, ALU.mult),
                        mod_made)
                if m < CT:
                    stat(STAT_CTX + m)
                    scaled(NT_CTX + m, STAT_CTX + m, xr[m][:], cmod_scale[:], cmod_shift[:])
                if 1 <= m <= CT:
                    xt_low(NT_CTX + m - 1, m - 1, False, (ct_hi, ct_lo))
                m = c - 12
                if m >= 0:
                    if m == 0:
                        dve.wait_ge(shift_loaded, 16)
                    mean_square(STAT_N3 + m, STAT_N3 + m + 1)
                    if m == 2:
                        xt_low(NT_3 + m - 1, m - 1, True)
                    refine(STAT_N3 + m)
                    scaled(NT_3 + m, STAT_N3 + m, x[:, m, :], mod_scale[:], mod_shift[:])
                    if m in (1, 3):
                        xt_low(NT_3 + m - 1, m - 1, True)

            did(dve.tensor_copy(ctmp[:, 0, :], csil[:, 0, :]), wm_used)
            mlp(TILE_MLP1, x, 0, True, norms_of_block_2)
            xt_low(NT_3 + 3, 3, True)

            g = TILE_IN2
            did(dve.memset(upad[:], 0.0), pool_step)
            for j in range(4):
                win = 2 ** (j + 1)
                dve.wait_ge(gemm_done, g + 1)
                grid = upad[:, 8:8 + S].rearrange("p (r b c) -> p b r c", r=GR, c=8)
                did(dve.tensor_copy(grid, gp[g % 4][:].rearrange("p (b r c) -> p b r c", r=GR, c=8)), gemm_free)
                src, width = upad, 528
                for e in range(j + 1):
                    width -= 2 ** e
                    did(dve.tensor_tensor(wsum[e % 2][:, 0:width], src[:, 0:width],
                                          src[:, 2 ** e:2 ** e + width], ALU.add), pool_step)
                    src = wsum[e % 2]
                first = 8 - win // 2
                left, right = src[:, first:first + 8], src[:, first + S - 8:first + S]
                dve.wait_ge(vec_loaded, 16 * 9)
                did(dve.tensor_tensor(left, left, edge[:, j, 0:8], ALU.mult), pool_step)
                did(dve.tensor_tensor(right, right, edge[:, j, 8:16], ALU.mult), pool_step)
                did(dve.scalar_tensor_tensor(pooled[:, j, :], src[:, first:first + S], 1.0 / win,
                                             upad[:, 8:8 + S], ALU.mult, ALU.subtract), pool_done)
                g += 1
            assert tally.n[pool_step.name] == POOL_STEPS
            for j in range(4):
                dve.wait_ge(gemm_done, g + 1)
                did(dve.tensor_scalar(q_2[:, j, :], gp[g % 4][:], QSCALE, None, ALU.mult), gemm_free)
                g += 1
            for j in range(4):
                dve.wait_ge(gemm_done, g + 1)
                did(dve.tensor_copy(k_2[:, j, :], gp[g % 4][:]), gemm_free)
                g += 1
            for j in range(4):
                dve.wait_ge(gemm_done, g + 1)
                did(dve.tensor_copy(k_c[:, j, :], gp[g % 4][:, 0:CTX]), gemm_free)
                g += 1
            for j in range(4):
                dve.wait_ge(pool_mixed, j + 1)
                did(dve.tensor_scalar(pooled[:, j, :], aux[j][:], pscale[:, j:j + 1], None, ALU.mult), pool_scaled)
            for m in range(CT):
                dve.wait_ge(gemm_done, g + 1)
                did(dve.tensor_copy(v_c[:, m, :], gp[g % 4][:]), gemm_free)
                g += 1
            for m in range(TT):
                dve.wait_ge(gemm_done, g + 1)
                did(dve.tensor_copy(v_2[:, m, :], gp[g % 4][:]), gemm_free)
                g += 1

            dve.wait_ge(rpb_loaded, 16 * 2 * NH)
            t0, e0, v0 = len(TURN1), len(U1), len(U1)
            for i, step in enumerate(STEPS2):
                if i < len(U2):
                    n, h = U2[i]
                    bank = gp[i % 4]
                    dve.wait_ge(score_done, e0 + i + 1)
                    if i >= 8:
                        dve.wait_ge(exp_done, e0 + i - 7)
                    local = bank[:, 0:256].rearrange("p (b r c) -> p b r c", r=KH, c=8)
                    run = rpb_run[:, h, RUN - 1 - KSHIFT[n]:RUN - KSHIFT[n]]
                    run = bass.AP(tensor=run.tensor, offset=run.offset,
                                  ap=[list(run.ap[0]), [-8, 4], [-RPW, KH], [-1, 8]])
                    did(dve.tensor_tensor(local, local, run, ALU.add), bias_added)
                    did(dve.tensor_reduce(nmax[:, i % 8:i % 8 + 1], bank[:], AXX, ALU.max, negate=True), max_done)
                for what, k in step:
                    if what == "T":
                        if k >= 2:
                            dve.wait_ge(pv_done, v0 + k - 1)
                        copy_turn(k, TURN2[("T", k)], 0, 4, t0)
                    elif what == "V" and k % 8 == 7:
                        if k >= 16:
                            dve.wait_ge(turned, t0 + TURN2[("M", k // 8 - 2, 0)] + 1)
                        heads_tile(k // 8, v0, e0, attn_2[(k // 8) % 2][:])
                    elif what == "M":
                        w = TURN2[("M", k, 0)]
                        dve.wait_ge(turn_hi, 2 * TT + k + 1)
                        did(dve.tensor_tensor(grid_cols(xt_lo, k), grid_bank(aux[w % 2]),
                                              grid_cols(xt_hi, k).bitcast(F32), ALU.subtract), turn_read)

            dve.wait_ge(tail_loaded, 16 * 5)
            did(dve.tensor_tensor(mix_gate[:], mix_gate[:], mix_gain[:], ALU.mult), mod_made)
            did(dve.scalar_tensor_tensor(mlp_scale[:], mlp_scale[:], 1.0, mlp_gain2[:], ALU.add, ALU.mult), mod_made)

            for e, (j, m) in enumerate(OUT2_ORDER):
                g = TILE_OUT2 + e
                k = STAT_TAIL + 2 * m
                cols = slice(j * NC, (j + 1) * NC)
                if e == 5:
                    xt_low(NT_4, 0)
                dve.wait_ge(gemm_done, g + 1)
                dve.wait_ge(ssq_done, tail_squares(e))
                if j:
                    did(dve.tensor_tensor(st[:, 0, k:k + 1], st[:, 0, k:k + 1], half_sq[:, m:m + 1], ALU.add),
                        tail_step)
                    mean_square(k, tail_squares(e))
                did(dve.tensor_tensor(sub[:, m, cols], gp[g % 4][:], mix_gate[:, cols], ALU.mult), gemm_free)
                if j:
                    refine(k)
                    did(dve.scalar_tensor_tensor(x[:, m, :], sub[:, m, :], st[:, 3, k:k + 1], x[:, m, :],
                                                 ALU.mult, ALU.add), tail_step)
                    if m >= 2:
                        xt_low(NT_4 + m - 1, m - 1)
                    stat(k + 1, tail_squares(e) + 1)
                    scaled(NT_4 + m, k + 1, x[:, m, :], mlp_scale[:], mlp_shift[:])
            xt_low(NT_4 + 3, 3)

            def last_norm(c):
                m = c - 12
                if m < 0:
                    return
                if m == 0:
                    dve.wait_ge(fin_loaded, 32)
                    did(dve.tensor_tensor(fin_gate[:], fin_gate[:], fin_gain[:], ALU.mult), mod_made)
                k = STAT_FIN + m
                summed = tail_squares(len(OUT2_ORDER) - 1) + 1 + TT + m + 1
                dve.wait_ge(ssq_done, summed)
                did(dve.tensor_tensor(st[:, 0, k:k + 1], st[:, 0, k:k + 1], half_sq[:, m:m + 1], ALU.add), tail_step)
                mean_square(k, summed)
                did(dve.tensor_tensor(sub[:, m, :], sub[:, m, :], fin_gate[:], ALU.mult), tail_step)
                refine(k)
                for j in range(2):
                    cols = slice(j * NC, (j + 1) * NC)
                    did(dve.scalar_tensor_tensor(x[:, m, cols], sub[:, m, cols], st[:, 3, k:k + 1], x[:, m, cols],
                                                 ALU.mult, ALU.add), fin_step)

            mlp(TILE_MLP2, sub, 8 * NCH, False, last_norm, fresh=True)


MOD_SPLIT_IN = (5, 9, 12, 14)
SUM_IN = (7, 11, 14, 15)


MOD_DONE = (1, 2, 3, 4, 5, 6, 7, 8, 9, 11, 12, 14, 15, 16, 16, 16)


def mod_units(c):
    return MOD_DONE[c] if c >= 0 else 0


POOL_STEPS = 1 + (1 + 2 + 3 + 4) + 2 * 4


def tail_squares(e):
    return STAT_TAIL + e + 1 + sum(j for j, m in OUT2_ORDER[:e])


def score_cols(n, kind):
    return ((0 if n else P), 257) if kind == 0 else (0, (n + 1) * P)


def score_blocks(n, kind):
    return ([0, 1] if n else [1]) if kind == 0 else list(range(n + 1))


def token_cols(dst, half, m, permute):
    if not permute:
        return dst[:, 4 * half:4 * half + 4, m * P:(m + 1) * P]
    return dst[:, 4 * half:4 * half + 4, :].rearrange("p k (b s) -> p k b s", s=64)[:, :, :, 16 * m:16 * m + 16]


def bank_cols(bank, permute):
    if not permute:
        return bank[:].rearrange("p (k s) -> p k s", k=4)
    return bank[:].rearrange("p (k b s) -> p k b s", k=4, s=16)


def grid_cols(dst, n):
    return dst[:, 4:8, :].rearrange("p k (r s) -> p k r s", s=GW)[:, :, :, 16 * n:16 * n + 16]


def grid_bank(bank):
    return bank[:].rearrange("p (k r s) -> p k r s", k=4, s=16)


_BLOCKS = {}


def block_fn(nc, ctx, engine):
    if id(nc) not in _BLOCKS:
        _BLOCKS[id(nc)] = ctx.enter_context(nc.Block())
    block = _BLOCKS[id(nc)]
    return {"sync": block.sync, "gpsimd": block.gpsimd, "scalar": block.scalar, "tensor": block.tensor,
            "vector": block.vector}[engine]


def constants():
    bf = np.dtype("bfloat16")
    q = np.arange(P)[:, None]
    k = np.arange(256)[None, :]
    dist = q + P - k
    band = (dist >= 0) & (dist < 128)
    alibi = np.stack([np.where(band, -(2.0 ** -(h + 1)) * dist, NEG) for h in range(NH)], axis=1)
    causal = np.where(np.arange(P)[None, :] <= q, 0.0, NEG)
    window = np.zeros((P, 3, 256))
    for v, (n, kc0) in enumerate(((0, 0), (1, 8), (3, 32))):
        for p in range(P):
            qc = 16 * n + 8 * (p // 64) + p % 8
            kc = kc0 + 8 * (np.arange(256) // 64) + np.arange(256) % 8
            first = min(max(qc - KW // 2, 0), GW - KW)
            window[p, v] = np.where((kc >= first) & (kc < first + KW), 0.0, NEG)
    edge = np.ones((4, 16))
    for g in range(4):
        w = 2 ** (g + 1)
        lo, hi = w // 2, w - 1 - w // 2
        for c, tok in enumerate(list(range(8)) + list(range(S - 8, S))):
            edge[g, c] = w / (min(tok + hi + 1, S) - max(tok - lo, 0))
    negsel = np.zeros((CR, NH, P))
    for h in range(NH):
        negsel[h, h] = negsel[32 + h, h] = -1.0
    return {
        "c_ident": np.eye(P, dtype=np.float32),
        "c_identb": np.eye(P).astype(bf),
        "c_alibi": alibi.astype(bf),
        "c_causal": causal.astype(bf),
        "c_window": window.astype(bf),
        "c_edge": np.broadcast_to(edge.astype(np.float32), (P, 4, 16)).copy(),
        "c_negsel": negsel.reshape(CR, NH * P).astype(np.float32),
    }


def kernel(**inputs):
    import concourse.bacc as bacc
    from concourse.bass_utils import run_bass_kernel_spmd

    def f(name, shape=None):
        a = np.ascontiguousarray(inputs[name])
        return a if shape is None else a.reshape(shape)

    def by_partition(name):
        return np.ascontiguousarray(f(name).reshape(-1, P).T)

    rpb = np.zeros(RPB_LEN, np.float32)
    rpb[RPAD:-RPAD] = f("rpb_2").reshape(-1)[::-1]
    arrays = {
        "x": f("x", (S, D)), "attn_norm_g": f("attn_norm_g"), "w_in": f("w_in"), "b_forget": f("b_forget"),
        "q_norm_a": f("q_norm_a"), "k_norm_a": f("k_norm_a"), "sink_logits": f("sink_logits"),
        "q_norm_b": f("q_norm_b"), "k_norm_b": f("k_norm_b"), "w_out": f("w_out"), "mlp_norm_g": f("mlp_norm_g"),
        "w_up": f("w_up"), "w_down": f("w_down"), "c": by_partition("c_2"), "ctx": f("ctx_2", (CTX, D)),
        "c_ctx": by_partition("c_ctx_2"), "w_mod": f("w_mod_2", (D, 6 * D)), "b_mod": f("b_mod_2", (6 * D,)),
        "g_pre_mix": f("g_pre_mix_2", (D,)), "g_post_mix": f("g_post_mix_2", (D,)),
        "g_pre_mlp": f("g_pre_mlp_2", (D,)), "g_post_mlp": f("g_post_mlp_2", (D,)),
        "w_in_2": f("w_in_2", (D, 2048)), "pool_w": f("pool_w_2", (4, P, P)),
        "pool_scale": by_partition("pool_scale_2"),
        "rpb": rpb, "w_out_2": f("w_out_2", (D, D)), "w_mlp_in_2": f("w_mlp_in_2", (D, DFF)),
        "w_mlp_out_2": f("w_mlp_out_2", (DFF, D)),
    }
    arrays.update(constants())
    nc = bacc.Bacc("TRN2", target_bir_lowering=False, num_devices=1)
    t = {}
    for name, a in arrays.items():
        t[name] = nc.dram_tensor(f"in_{name}", a.shape, mybir.dt.from_np(a.dtype), kind="ExternalInput").ap()
    out = nc.dram_tensor("out", (S, D), F32, kind="ExternalOutput").ap()
    build(nc, t, out)
    r = run_bass_kernel_spmd(nc, [{f"in_{name}": a for name, a in arrays.items()}], core_ids=[0])
    return r.results[0]["out"].reshape(1, S, D)
```
